# Optimizing a Trainium2 kernel written in Bass

```python
import math, functools
import jax, jax.numpy as jnp
from jax import lax
import numpy as np

D_MODEL = 2048
BATCH = 1
SEQ = 512
DEPTH = 1
DEC_BATCH = 8
DEC_SEQ = 1
PAST_LEN = 4096
PAGE_SIZE = 128

A_HEADS = 8
A_KV_HEADS = 2
A_HEAD_DIM = 128
A_WIDTH = A_HEADS * A_HEAD_DIM
IDX_HEADS = 16
IDX_DIM = 64
TOPK_MAX = 256
Q_BLOCK = 128
B_HEADS = 8
B_KDIM = 128
B_VDIM = 128
B_WIDTH = B_HEADS * B_VDIM
CONV_W = 4
CONV_DIM = 2 * B_HEADS * B_KDIM + B_WIDTH
GDN_CHUNK = 64
NORM_EPS = 1e-6

_SPLIT_SIZES = (A_WIDTH, A_KV_HEADS * A_HEAD_DIM, A_KV_HEADS * A_HEAD_DIM, IDX_HEADS * IDX_DIM, IDX_DIM, IDX_HEADS, A_WIDTH,
                CONV_DIM, B_HEADS, B_HEADS, B_WIDTH, D_MODEL, D_MODEL)
N_IN = sum(_SPLIT_SIZES)

kernel_name = 'dsa_gdn_parallel_hybrid_step'

def rmsnorm(x, g):
    xf = x.astype(jnp.float32)
    y = xf * lax.rsqrt(jnp.mean(xf * xf, axis=-1, keepdims=True) + NORM_EPS)
    return (y * g.astype(jnp.float32)).astype(x.dtype)

def l2norm(x):
    xf = x.astype(jnp.float32)
    return xf * lax.rsqrt(jnp.sum(xf * xf, axis=-1, keepdims=True) + NORM_EPS)

def split_proj(u):
    cuts = np.cumsum(_SPLIT_SIZES)[:-1].tolist()
    return jnp.split(u, cuts, axis=-1)

def indexer_scores(q_idx, w_idx, k_idx):
    s = jnp.einsum('bthd,bld->bthl', q_idx.astype(jnp.float32), k_idx.astype(jnp.float32)) * IDX_DIM ** -0.5
    return jnp.einsum('bthl,bth->btl', jax.nn.relu(s), w_idx.astype(jnp.float32)) * IDX_HEADS ** -0.5

def sparse_attend(q, k_sel, v_sel, valid):
    B, T = q.shape[:2]
    qg = q.reshape(B, T, A_KV_HEADS, A_HEADS // A_KV_HEADS, A_HEAD_DIM).astype(jnp.float32)
    logits = jnp.einsum('btngd,btknd->btngk', qg, k_sel.astype(jnp.float32)) * A_HEAD_DIM ** -0.5
    logits = jnp.where(valid[:, :, None, None, :], logits, -jnp.inf)
    p = jax.nn.softmax(logits, axis=-1)
    o = jnp.einsum('btngk,btknd->btngd', p, v_sel.astype(jnp.float32))
    return o.reshape(B, T, A_WIDTH).astype(q.dtype)

def dsa_prompt(q, k, v, q_idx, w_idx, k_idx):
    B, S = q.shape[:2]
    n_sel = min(TOPK_MAX, S // 4)
    key_pos = jnp.arange(S)
    b_ix = jnp.arange(B)[:, None, None]

    def block(i):
        t0 = i * Q_BLOCK
        qb = lax.dynamic_slice_in_dim(q, t0, Q_BLOCK, axis=1)
        qib = lax.dynamic_slice_in_dim(q_idx, t0, Q_BLOCK, axis=1)
        wb = lax.dynamic_slice_in_dim(w_idx, t0, Q_BLOCK, axis=1)
        q_pos = t0 + jnp.arange(Q_BLOCK)
        causal = key_pos[None, :] <= q_pos[:, None]
        scores = jnp.where(causal[None], indexer_scores(qib, wb, k_idx), -jnp.inf)
        _, sel = lax.top_k(scores, n_sel)
        valid = sel <= q_pos[None, :, None]
        return sparse_attend(qb, k[b_ix, sel], v[b_ix, sel], valid)

    out = lax.map(block, jnp.arange(S // Q_BLOCK))
    return jnp.moveaxis(out, 0, 1).reshape(B, S, A_WIDTH)

def dsa_sample(q, k, v, q_idx, w_idx, k_idx, layer, cache_k, cache_v, cache_kidx, page_table):
    B, T = q.shape[:2]
    L = PAST_LEN + T
    n_sel = min(TOPK_MAX, L // 4)
    b_ix = jnp.arange(B)[:, None, None]
    kidx_past = cache_kidx[layer, page_table].reshape(B, PAST_LEN, IDX_DIM).astype(k_idx.dtype)
    kidx_all = jnp.concatenate([kidx_past, k_idx], axis=1)
    q_pos = PAST_LEN + jnp.arange(T)
    causal = jnp.arange(L)[None, :] <= q_pos[:, None]
    scores = jnp.where(causal[None], indexer_scores(q_idx, w_idx, kidx_all), -jnp.inf)
    _, sel = lax.top_k(scores, n_sel)
    valid = sel <= q_pos[None, :, None]
    past_ix = jnp.minimum(sel, PAST_LEN - 1)
    phys = page_table[b_ix, past_ix // PAGE_SIZE]
    off = past_ix % PAGE_SIZE
    new_ix = jnp.clip(sel - PAST_LEN, 0, T - 1)
    is_new = (sel >= PAST_LEN)[..., None, None]
    k_sel = jnp.where(is_new, k[b_ix, new_ix], cache_k[layer, phys, off].astype(k.dtype))
    v_sel = jnp.where(is_new, v[b_ix, new_ix], cache_v[layer, phys, off].astype(v.dtype))
    return sparse_attend(q, k_sel, v_sel, valid)

def causal_conv(x, buf, w):
    T = x.shape[1]
    xp = jnp.concatenate([buf.astype(x.dtype), x], axis=1)
    y = xp[:, 0:T] * w[0]
    for j in range(1, CONV_W):
        y = y + xp[:, j:j + T] * w[j]
    return jax.nn.silu(y), xp[:, T:]

def gated_delta_chunked(q, k, v, g, beta, state0):
    f32 = jnp.float32
    B, T, H, _ = q.shape
    C = min(GDN_CHUNK, T)
    n = -(-T // C)
    pad = n * C - T

    def to_chunks(a):
        a = a.astype(f32)
        a = jnp.pad(a, [(0, 0), (0, pad)] + [(0, 0)] * (a.ndim - 2))
        a = a.reshape((B, n, C) + a.shape[2:])
        return jnp.moveaxis(a, (1, 3), (0, 2))

    qc, kc, vc, gc, bc = (to_chunks(a) for a in (q * B_KDIM ** -0.5, k, v, g, beta))
    gc = jnp.cumsum(gc, axis=-1)
    incl = jnp.tril(jnp.ones((C, C), bool))
    strict = jnp.tril(jnp.ones((C, C), bool), -1)
    eye = jnp.eye(C, dtype=f32)

    def chunk_step(S, inp):
        qi, ki, vi, gi, bi = inp
        decay = jnp.exp(jnp.where(incl, gi[..., :, None] - gi[..., None, :], -jnp.inf))
        kb = ki * bi[..., None]
        a_low = jnp.where(strict, jnp.einsum('bhid,bhjd->bhij', kb, ki) * decay, 0.0)
        rhs = jnp.concatenate([vi * bi[..., None], kb * jnp.exp(gi)[..., None]], axis=-1)
        sol = lax.linalg.triangular_solve(eye + a_low, rhs, left_side=True, lower=True, unit_diagonal=True)
        u, w = sol[..., :B_VDIM], sol[..., B_VDIM:]
        v_new = u - jnp.einsum('bhck,bhkv->bhcv', w, S)
        attn = jnp.einsum('bhik,bhjk->bhij', qi, ki) * decay
        out = (jnp.einsum('bhck,bhkv->bhcv', qi * jnp.exp(gi)[..., None], S)
               + jnp.einsum('bhij,bhjv->bhiv', attn, v_new))
        g_last = gi[..., -1:]
        S = (S * jnp.exp(g_last)[..., None]
             + jnp.einsum('bhck,bhcv->bhkv', ki * jnp.exp(g_last - gi)[..., None], v_new))
        return S, out

    S_fin, outs = lax.scan(chunk_step, state0.astype(f32), (qc, kc, vc, gc, bc))
    out = jnp.moveaxis(outs, (0, 2), (1, 3)).reshape(B, n * C, H, B_VDIM)[:, :T]
    return out, S_fin

def mixer_layer(x, attend, conv_buf, ssm0, pre_g, post_g, w_in_l, idx_kg, conv_w_l, a_log_l, dt_bias_l,
                gdn_g, w_pa_l, w_pb_l, w_o_l):
    B, T, _ = x.shape
    f32 = jnp.float32
    h = rmsnorm(x, pre_g)
    (qa, ka, va, qi, ki, wi, za, qkv_b, a_b, b_b, zb, ga, gb) = split_proj(jnp.einsum('btd,dn->btn', h, w_in_l))
    qa = qa.reshape(B, T, A_HEADS, A_HEAD_DIM)
    ka = ka.reshape(B, T, A_KV_HEADS, A_HEAD_DIM)
    va = va.reshape(B, T, A_KV_HEADS, A_HEAD_DIM)
    qi = qi.reshape(B, T, IDX_HEADS, IDX_DIM)
    ki = rmsnorm(ki, idx_kg)
    o_a = attend(qa, ka, va, qi, wi, ki)
    y_a = jnp.einsum('btc,cd->btd', o_a * jax.nn.silu(za), w_pa_l)
    conv_out, new_buf = causal_conv(qkv_b, conv_buf, conv_w_l)
    hk = B_HEADS * B_KDIM
    qb, kb, vb = jnp.split(conv_out, [hk, 2 * hk], axis=-1)
    qb = l2norm(qb.reshape(B, T, B_HEADS, B_KDIM))
    kb = l2norm(kb.reshape(B, T, B_HEADS, B_KDIM))
    vb = vb.reshape(B, T, B_HEADS, B_VDIM)
    g = -jnp.exp(a_log_l.astype(f32)) * jax.nn.softplus(a_b.astype(f32) + dt_bias_l.astype(f32))
    beta = jax.nn.sigmoid(b_b.astype(f32))
    o_b, ssm_new = gated_delta_chunked(qb, kb, vb, g, beta, ssm0)
    o_b = rmsnorm(o_b, gdn_g).astype(x.dtype).reshape(B, T, B_WIDTH)
    y_b = jnp.einsum('btc,cd->btd', o_b * jax.nn.silu(zb), w_pb_l)
    merged = jax.nn.sigmoid(ga) * y_a + jax.nn.sigmoid(gb) * y_b
    out = jnp.einsum('btd,de->bte', merged, w_o_l)
    x = x + rmsnorm(out, post_g)
    return x, (ka, va, ki, new_buf, ssm_new.astype(ssm0.dtype))

def setup_inputs(seed: int = 0) -> dict:
    key = jax.random.key(seed)
    ks = jax.random.split(key, 24)
    f32 = jnp.float32
    n_pages = PAST_LEN // PAGE_SIZE
    n_used = DEC_BATCH * n_pages
    n_pool = n_used + max(1, n_used // 4)

    def nrm(k, shape, s=1.0):
        return jax.random.normal(k, shape, f32) * s

    x_prompt = nrm(ks[0], (BATCH, SEQ, D_MODEL))
    x_sample = nrm(ks[1], (DEC_BATCH, DEC_SEQ, D_MODEL))
    cache_k = nrm(ks[2], (DEPTH, n_pool, PAGE_SIZE, A_KV_HEADS, A_HEAD_DIM))
    cache_v = nrm(ks[3], (DEPTH, n_pool, PAGE_SIZE, A_KV_HEADS, A_HEAD_DIM))
    cache_kidx = nrm(ks[4], (DEPTH, n_pool, PAGE_SIZE, IDX_DIM))
    state_conv = nrm(ks[5], (DEPTH, DEC_BATCH, CONV_W - 1, CONV_DIM))
    state_ssm = nrm(ks[6], (DEPTH, DEC_BATCH, B_HEADS, B_KDIM, B_VDIM), 0.05)
    page_table = jax.random.permutation(ks[7], n_pool)[:n_used].reshape(DEC_BATCH, n_pages).astype(jnp.int32)
    pre_norm = 1.0 + nrm(ks[8], (DEPTH, D_MODEL), 0.02)
    post_norm = 1.0 + nrm(ks[9], (DEPTH, D_MODEL), 0.02)
    w_in = nrm(ks[10], (DEPTH, D_MODEL, N_IN), D_MODEL ** -0.5)
    idx_k_norm = 1.0 + nrm(ks[11], (DEPTH, IDX_DIM), 0.02)
    conv_w = nrm(ks[12], (DEPTH, CONV_W, CONV_DIM), CONV_W ** -0.5)
    a_log = jnp.log(jax.random.uniform(ks[13], (DEPTH, B_HEADS), f32, 1.0, 16.0))
    dt = jnp.exp(jax.random.uniform(ks[14], (DEPTH, B_HEADS), f32, math.log(1e-3), math.log(1e-1)))
    dt_bias = dt + jnp.log(-jnp.expm1(-dt))
    gdn_norm = 1.0 + nrm(ks[15], (DEPTH, B_VDIM), 0.02)
    w_pa = nrm(ks[16], (DEPTH, A_WIDTH, D_MODEL), A_WIDTH ** -0.5)
    w_pb = nrm(ks[17], (DEPTH, B_WIDTH, D_MODEL), B_WIDTH ** -0.5)
    w_o = nrm(ks[18], (DEPTH, D_MODEL, D_MODEL), D_MODEL ** -0.5)
    return {'x_prompt': x_prompt, 'x_sample': x_sample, 'cache_k': cache_k, 'cache_v': cache_v,
            'cache_kidx': cache_kidx, 'state_conv': state_conv, 'state_ssm': state_ssm, 'page_table': page_table,
            'pre_norm': pre_norm, 'post_norm': post_norm, 'w_in': w_in, 'idx_k_norm': idx_k_norm, 'conv_w': conv_w,
            'a_log': a_log, 'dt_bias': dt_bias, 'gdn_norm': gdn_norm, 'w_pa': w_pa, 'w_pb': w_pb, 'w_o': w_o}

def reference(x_prompt, x_sample, cache_k, cache_v, cache_kidx, state_conv, state_ssm, page_table,
              pre_norm, post_norm, w_in, idx_k_norm, conv_w, a_log, dt_bias, gdn_norm, w_pa, w_pb, w_o):
    xp, xs = x_prompt, x_sample
    conv0_p = jnp.zeros((BATCH, CONV_W - 1, CONV_DIM), x_prompt.dtype)
    ssm0_p = jnp.zeros((BATCH, B_HEADS, B_KDIM, B_VDIM), x_prompt.dtype)
    new_p = []
    new_s = []
    for l in range(DEPTH):
        lp = (pre_norm[l], post_norm[l], w_in[l], idx_k_norm[l], conv_w[l], a_log[l], dt_bias[l],
              gdn_norm[l], w_pa[l], w_pb[l], w_o[l])
        xp, st_p = mixer_layer(xp, dsa_prompt, conv0_p, ssm0_p, *lp)
        samp_attend = functools.partial(dsa_sample, layer=l, cache_k=cache_k, cache_v=cache_v,
                                        cache_kidx=cache_kidx, page_table=page_table)
        xs, st_s = mixer_layer(xs, samp_attend, state_conv[l], state_ssm[l], *lp)
        new_p.append(st_p)
        new_s.append(st_s)
    k_p, v_p, kidx_p, conv_p, ssm_p = [jnp.stack(z) for z in zip(*new_p)]
    k_s, v_s, kidx_s, conv_s, ssm_s = [jnp.stack(z) for z in zip(*new_s)]
    return (xp, xs, k_p, v_p, kidx_p, conv_p, ssm_p, k_s, v_s, kidx_s, conv_s, ssm_s)


_drawn_inputs = setup_inputs


def setup_inputs(seed=0):
    import zlib

    import numpy as np

    out = dict(_drawn_inputs(seed))
    spreads = {}
    factors = {}
    for name, (base, spread) in spreads.items():
        noise = np.random.default_rng([zlib.crc32(name.encode()), seed]).standard_normal(out[name].shape)
        drawn = base * np.exp(spread * noise) if base else spread * noise
        out[name] = __import__('jax').numpy.asarray(drawn.astype(out[name].dtype))
    for name, factor in factors.items():
        out[name] = (out[name] * factor).astype(out[name].dtype)
    return out
```

```python
from contextlib import ExitStack

import concourse.bass as bass
from concourse import mybir

ALU = mybir.AluOpType
ACT = mybir.ActivationFunctionType
F32 = mybir.dt.float32
BF16 = mybir.dt.bfloat16
I32 = mybir.dt.int32
U32 = mybir.dt.uint32
AX = mybir.AxisListType.X

P = 128
D = 2048
KT = D // P
NP = 512
NS = 8
T = NP + NS
HALF = T // 2
TT = NP // P
TOK = [P] * TT + [NS]
HD = 128
AH, AKV = 8, 2
GRP = AH // AKV
IH, ID = 16, 64
BH = 8
CONV = 4
CD = 3 * BH * HD
PAGE, NPG, NPOOL = 128, 32, 320
PAST = PAGE * NPG
SEL_P = 128
SEL_S = 256
EPS = 1e-6
NEG = -1.0e30
TAKEN = -3.0e38
A_SCALE = HD ** -0.5
I_SCALE = ID ** -0.5 * IH ** -0.5

C_Q = 0
C_KI = 2560
C_ZA = 2640
C_AB = 6736
C_ZB = 6752
C_GA = 7776
C_GB = 9824

U_K, U_V, U_QI = 8, 10, 12
U_BQ, U_BK, U_BV = 8, 16, 24

G_B, G_C, G_D, G_E, G_F = 0, 20, 52, 60, 124
L_C, L_D, L_E, L_F = 20, 52, 60, 108
RING = 4


def tok(t):
    return slice(t * P, t * P + TOK[t])


def build(nc, x_prompt, x_sample, cache_k, cache_v, cache_kidx, state_conv, state_ssm, page_table, pre_norm,
          post_norm, w_in, idx_k_norm, conv_w, a_log, dt_bias, gdn_norm, w_pa, w_pb, w_o,
          y_p, y_s, k_p, v_p, kidx_p, conv_p, ssm_p, k_s, v_s, kidx_s, conv_s, ssm_s):
    with ExitStack() as ctx:
        def sb(name, shape, dt=F32):
            return ctx.enter_context(nc.sbuf_tensor(name, shape, dt))

        def sem(name):
            return ctx.enter_context(nc.semaphore(name))

        hT = sb("hT", [P, KT, T])
        ring = sb("ring", [P, RING, KT, P])
        UA = sb("UA", [P, 20, T])
        UB = sb("UB", [P, 32, T])
        idx = sb("idx", [P, TT, NP])
        UAf = UA[:, :, :].rearrange("p a b -> p (a b)")
        UBf = UB[:, :, :].rearrange("p a b -> p (a b)")
        idf = idx[:, :, :].rearrange("p a b -> p (a b)")
        hTf = hT[:, :, :].rearrange("p a b -> p (a b)")

        ident = sb("ident", [P, P])
        ones = sb("ones", [P, P])
        tri_le = sb("tri_le", [P, P])
        tri_lt = sb("tri_lt", [P, P])
        swap = sb("swap", [P, P])
        parT = sb("parT", [P, 113])
        stT = sb("stT", [P, 24, 24])
        small = sb("small", [P, 160])
        ab = sb("ab", [P, 5, 96])
        kin = sb("kin", [P, 5, 2, ID])
        kIT = sb("kIT", [P, T])
        qblk = sb("qblk", [P, NS, 32])
        wbc = sb("wbc", [P, NS, IH])
        Y = sb("Y", [P, NS, NPG + 1])
        bit_i = sb("bit_i", [P, 32], I32)
        bit_f = sb("bit_f", [P, 32])
        thr_i = sb("thr_i", [P, NS], I32)
        cand_i = sb("cand_i", [P, NS], I32)
        m_i = sb("m_i", [P, NS], I32)
        srt = sb("srt", [P, 12, NS])
        iota_b = sb("iota_b", [P, SEL_S], BF16)
        coef = sb("coef", [3, 1])
        pg_i = sb("pg_i", [P, P], I32)
        off_i = sb("off_i", [P, P], I32)
        sel_i = sb("sel_i", [P, 16], I32)
        gv = sb("gv", [P, 12, 5 * BH])
        qm = sb("qm", [P, 1088])
        vn = sb("vn", [P, TT, 256])
        gsm = sb("gsm", [P, 8, 64])
        cols = sb("cols", [P, 64])
        top8 = sb("top8", [P, TT, 8])

        rs_x = small[:, 0:5]
        ssq = small[:, 5:10]
        ki_s = small[:, 10:15]
        ki_r = small[:, 15:20]
        pm64 = small[:, 20:21]
        alog = small[:, 24:32]
        dtb = small[:, 32:40]
        eps_c = small[:, 40:41]
        idxg = small[:, 64:128]
        mx = small[:, 128:130]
        nm = small[:, 130:132]
        sm = small[:, 132:134]
        rc = small[:, 134:136]
        g_pre = parT[:, 0:16]
        gdn_g = parT[:, 112:113]

        def conv_col(j, tile):
            return parT[:, 16 + 24 * j + tile:17 + 24 * j + tile]

        x_nat = UAf[:, 0:5 * D].rearrange("p (t d) -> p t d", t=5)
        st_nat = UBf[0:24, 0:CD]
        wa = UBf[:, 3072:3072 + KT * 96].rearrange("p (k n) -> p k n", k=KT)
        kraw = [UBf[:, 4608 + 2048 * i:6656 + 2048 * i].rearrange("p (c d) -> p c d", c=16) for i in range(2)]
        kTp = [UBf[:, 8704 + 2048 * i:10752 + 2048 * i].rearrange("p (c d) -> p c d", c=16) for i in range(2)]
        rel = UBf[:, 12800:14848].rearrange("p (r n) -> p r n", r=4)
        wsum = UBf[:, 14848:15360]
        junk = UBf[:, 12800:14848]
        knat_t = UBf[:, 15360:15872]

        pt_i = UBf[:, 15872:16128].bitcast(I32)
        xw = UBf[0:NS, 16128:16256].rearrange("p (b h) -> p b h", b=NS)
        par = UBf[:, 16256:16384]

        QS = UAf[:, U_QI * T:U_QI * T + 8 * T]
        NY = NS * (NPG + 1)
        ge, t1, pos, wsum_gt = (QS[:, NY * x:NY * x + NY] for x in range(4))
        rk = QS[:, 4 * NY:4 * NY + 400]
        rk2 = QS[:, 4 * NY + 400:4 * NY + 400 + NS * 17]
        qs0 = 4 * NY + 400 + NS * 17
        vals = QS[:, qs0:qs0 + 384].bitcast(BF16).rearrange("p (c s v) -> p c s v", s=2, v=3)
        onehot = QS[:, qs0 + 384:qs0 + 896].bitcast(BF16).rearrange("p (r n) -> p r n", r=4)
        row3 = QS[0:3, qs0 + 896:qs0 + 1408].rearrange("p (r n) -> p r n", r=2)
        QS = UAf[:, U_QI * T:U_QI * T + 8 * T]
        Lb = QS[:, 0:1024].rearrange("p (r n) -> p r n", r=2)
        PTs = QS[:, 1024:2048].rearrange("p (r n) -> p r n", r=2)
        KTs = QS[:, 2048:2562].rearrange("p (n c) -> p n c", n=2)
        kv_sel = QS[:, 2562:2562 + 1536].rearrange("p (s h c) -> p s h c", s=3, h=2)
        Ls = idf[0:64, 0:257]
        PTs_s = idf[:, 512:640].rearrange("p (h c) -> p h c", h=2)
        tmpS = idf[:, 640:704]

        kd = idf[:, 0:512].rearrange("p (c n) -> p c n", c=4)
        vb = idf[:, 512:1024].rearrange("p (c n) -> p c n", c=4)
        Ds = idf[:, 1024:1536].rearrange("p (c n) -> p c n", c=4)
        atT = idf[:, 1536:2048].rearrange("p (c n) -> p c n", c=4)
        R2 = UAf[:, U_K * T:U_K * T + 4 * T]
        Mb = [R2[:, 512 * i:512 * i + 512].rearrange("p (c n) -> p c n", c=4) for i in range(4)]
        Yt = qm[:, 0:512].rearrange("p (c n) -> p c n", c=4)
        outn = qm[:, 512:1024].rearrange("p (c n) -> p c n", c=4)
        vnf = vn[:, :, :].rearrange("p a b -> p (a b)")
        Di = vnf[:, 0:512].rearrange("p (c n) -> p c n", c=4)
        Sst = vnf[:, 512:640]
        rr = vnf[:, 640:768]
        vnew = vnf[:, 768:896]
        nsq = idf[:, 0:T]
        nrm = idf[:, T:2 * T]
        cvt = idf[:, 2 * T:3 * T]
        Sld = [idf[:, 512 * i:512 * i + 512].rearrange("p (r n) -> p r n", r=4) for i in range(4)]
        vexp = [R2[0:64, 512 * i:512 * i + 512].rearrange("p (r n) -> p r n", r=4) for i in range(2)]
        kns = gv[0:64, 8:12, :].rearrange("p a b -> p (a b)")[:, 0:P]
        kqs = gv[:, 1:5, :].rearrange("p a b -> p (a b)")[:, 0:P].rearrange("p (e t) -> p e t", t=2)
        ga_sb = idf[:, 0:T]
        gb_sb = idf[:, T:2 * T]
        m1 = idf[:, 2 * T:3 * T]
        m2b = qm[:, 0:T]
        oT = [idf[:, 0:T], idf[:, T:2 * T]]
        Yo = UAf[:, 0:5 * D].rearrange("p (t d) -> p t d", t=5)
        xf = UBf[:, 0:4 * D].rearrange("p (t d) -> p t d", t=4)
        xfs = hTf[:, 0:D]
        postb = hTf[:, D:2 * D]
        osq = hTf[:, 2 * D:3 * D]

        pj = [ctx.enter_context(nc.psum_tensor(f"pj{i}", [P, 2, 512], F32)) for i in range(2)]
        mb = [ctx.enter_context(nc.psum_tensor(f"mb{i}", [P, 512], F32)) for i in range(4)]

        consts = sem("consts")
        par_in, st_in, wa_in = sem("par_in"), sem("st_in"), sem("wa_in")
        x_in = [sem(f"x_in{t}") for t in range(5)]
        row_in, pt_in = sem("row_in"), sem("pt_in")
        w_in_s = [sem(f"w_slot{i}") for i in range(RING)]
        parT_ps, parT_sb, sq_done, x_ms, x_sqrt, x_scaled = (sem(n) for n in (
            "parT_ps", "parT_sb", "sq_done", "x_ms", "x_sqrt", "x_scaled"))
        xT_ps, xT_sb, ab_ps, ab_sb, ki_ms, ki_sqrt, ki_done, kiT_ps, kiT_sb = (sem(n) for n in (
            "xT_ps", "xT_sb", "ab_ps", "ab_sb", "ki_ms", "ki_sqrt", "ki_done", "kiT_ps", "kiT_sb"))
        proj_done, proj_evac, y_evac = sem("proj_done"), sem("proj_evac"), sem("y_evac")
        kv_ps, kv_sb, kv_out = sem("kv_ps"), sem("kv_sb"), sem("kv_out")
        q_swap, q_blk, w_x, w_bc = sem("q_swap"), sem("q_blk"), sem("w_x"), sem("w_bc")
        idx_ps, idx_relu, idx_acc, idx_mask = sem("idx_ps"), sem("idx_relu"), sem("idx_acc"), sem("idx_mask")
        off_done, kraw_in = sem("off_done"), [sem("kraw_in0"), sem("kraw_in1")]
        kp_ps, kp_sb, ks_ps, ks_sum = sem("kp_ps"), sem("kp_sb"), sem("ks_ps"), sem("ks_sum")
        cnt_part, cnt_all, srch, topk = sem("cnt_part"), sem("cnt_all"), sem("srch"), sem("topk")
        rank_in, rank_ps, hot, hot_ps, row_sb, row_ps, sel_done = (sem(n) for n in (
            "rank_in", "rank_ps", "hot", "hot_ps", "row_sb", "row_ps", "sel_done"))
        kv_in = [sem(f"kv_in{i}") for i in range(3)]
        masks = sem("masks")
        lg_ps, lg_max, p_exp, p_rc, p_rdy, pt_ps, pt_sb, pv_ps, pv_sb = (sem(n) for n in (
            "lg_ps", "lg_max", "p_exp", "p_rc", "p_rdy", "pt_ps", "pt_sb", "pv_ps", "pv_sb"))
        sk_ps, sk_sb, sl_ps, s_max, s_exp, s_p, sp_ps, sp_sb, so_ps, so_sb = (sem(n) for n in (
            "sk_ps", "sk_sb", "sl_ps", "s_max", "s_exp", "s_p", "sp_ps", "sp_sb", "so_ps", "so_sb"))
        cv_ps, cv_sb, cv_out, cv_acc, cv_silu, cv_samp = (sem(n) for n in (
            "cv_ps", "cv_sb", "cv_out", "cv_acc", "cv_silu", "cv_samp"))
        nq_sq, nq_ps, nq_rt, nq_done = sem("nq_sq"), sem("nq_ps"), sem("nq_rt"), sem("nq_done")
        dec_a, dec_v, dec_ps, dec_e, dec_done = sem("dec_a"), sem("dec_v"), sem("dec_ps"), sem("dec_e"), sem("dec_done")
        g_pre_ps, g_row, g_exp, g_msk, g_n, g_at, g_tr, g_nt, g_y = (sem(n) for n in (
            "g_pre_ps", "g_row", "g_exp", "g_msk", "g_n", "g_at", "g_tr", "g_nt", "g_y"))
        g_sq, g_m, g_mt, g_yps = sem("g_sq"), sem("g_m"), sem("g_mt"), sem("g_yps")
        c_ks, c_r, c_vps, c_vn, c_st, c_s, c_o, g_oT, g_out, ssm_out = (sem(n) for n in (
            "c_ks", "c_r", "c_vps", "c_vn", "c_st", "c_s", "c_o", "g_oT", "g_out", "ssm_out"))
        S_in = [sem(f"S_in{i}") for i in range(4)]
        s_kq, s_bc, s_bcs, s_ks, s_vn, s_tps, s_tsb, s_vx, s_op, s_new = (sem(n) for n in (
            "s_kq", "s_bc", "s_bcs", "s_ks", "s_vn", "s_tps", "s_tsb", "s_vx", "s_op", "s_new"))
        S_out = [sem(f"S_out{i}") for i in range(4)]
        slot_free, round_on = sem("slot_free"), sem("round_on")
        mrg, g_nt_in = sem("mrg"), sem("g_nt_in")
        z_silu, gated = sem("z_silu"), sem("gated")
        oT_ps, oT_sb, x_back, o_ms, o_rt, y_fin, y_out = (sem(n) for n in (
            "oT_ps", "oT_sb", "x_back", "o_ms", "o_rt", "y_fin", "y_out"))
        dve_c, act_c, pool_c = sem("dve_c"), sem("act_c"), sem("pool_c")

        def linker(eng, s):
            n = [0]

            def link(ins):
                n[0] += 1
                ins.then_inc(s, 1)
                eng.wait_ge(s, n[0])
            return link

        w_in_v = w_in[0].rearrange("(k p) n -> p k n", p=P)
        pa_v = w_pa[0].rearrange("(k p) n -> p k n", p=P)
        pb_v = w_pb[0].rearrange("(k p) n -> p k n", p=P)
        o_v = w_o[0].rearrange("(k p) n -> p k n", p=P)
        kidx_rows = cache_kidx[0].rearrange("g (q s) d -> (g q) (s d)", s=2)
        ck_rows = cache_k[0].rearrange("g t n d -> (g t) (n d)")
        cv_rows = cache_v[0].rearrange("g t n d -> (g t) (n d)")
        N_CONST = 15

        block = ctx.enter_context(nc.Block())

        @block.sync
        def _(sp):
            sp.dma_start(par[0:16, :], pre_norm[0].rearrange("(k p) -> k p", p=P)).then_inc(par_in, 16)
            sp.dma_start(par[16:112, :], conv_w[0].rearrange("j (c p) -> (j c) p", p=P)).then_inc(par_in, 16)
            sp.dma_start(par[112:113, :], gdn_norm[0:1, :]).then_inc(par_in, 16)
            for t in range(TT):
                sp.dma_start(x_nat[:, t, :], x_prompt[0, tok(t), :]).then_inc(x_in[t], 16)
            sp.dma_start(x_nat[0:NS, TT, :], x_sample.rearrange("b s d -> (b s) d")).then_inc(x_in[TT], 16)
            sp.dma_start(wa[:, :, 0:80], w_in_v[:, :, C_KI:C_KI + 80]).then_inc(wa_in, 16)
            sp.dma_start(wa[:, :, 80:96], w_in_v[:, :, C_AB:C_AB + 16], ).then_inc(wa_in, 16)
            sp.dma_start(st_nat, state_conv[0].rearrange("b j c -> (b j) c")).then_inc(st_in, 16)
            sp.dma_start(conv_s[0, :, 0:2, :], state_conv[0, :, 1:3, :]).then_inc(cv_out, 16)

            def load(slot, src, dst=None):
                sp.dma_start(ring[:, slot, :, :] if dst is None else dst, src).then_inc(w_in_s[slot], 16)

            for s in range(RING):
                load(s, w_in_v[:, :, C_Q + P * s:C_Q + P * s + P])
            with sp.Fori(1, 5) as i:
                for u in range(4):
                    sp.wait_ge(proj_done, 4 * i + (u - 3))
                    sp.sem_inc(slot_free, 1)
                    load(u, w_in_v[:, :, bass.ds(C_Q + P * u + 4 * P * i, P)])
            with sp.Fori(0, 8) as i:
                for u in range(4):
                    sp.wait_ge(proj_done, 4 * i + (L_C + u - 3))
                    sp.sem_inc(slot_free, 1)
                    load(u, w_in_v[:, :, bass.ds(C_ZA + P * u + 4 * P * i, P)])
            with sp.Fori(0, 2) as i:
                for u in range(4):
                    sp.wait_ge(proj_done, 4 * i + (L_D + u - 3))
                    sp.sem_inc(slot_free, 1)
                    load(u, w_in_v[:, :, bass.ds(C_ZB + P * u + 4 * P * i, P)])

            def merge_loads(i, first):
                for l in range(12):
                    j, q = divmod(l, 3)
                    slot = l % 4
                    if first and j == 0:
                        sp.wait_ge(proj_done, L_E - 3 + q)
                    else:
                        sp.wait_ge(proj_done, 16 * i + (G_E + 4 * j + (-4, -3, -2)[q]))
                        sp.sem_inc(slot_free, 1)
                    col = 4 * P * i + P * j
                    if q < 2:
                        load(slot, w_in_v[:, :, bass.ds(col + (C_GA, C_GB)[q], P)])
                    else:
                        load(slot, pa_v[:, :, bass.ds(col, P)], ring[:, slot, 0:8, :])
                        load(slot, pb_v[:, :, bass.ds(col, P)], ring[:, slot, 8:16, :])
            merge_loads(0, True)
            with sp.Fori(1, 4) as i:
                merge_loads(i, False)
            for u in range(4):
                sp.wait_ge(proj_done, (120, 121, 122, 124)[u])
                load(u, o_v[:, :, P * u:P * u + P])
            with sp.Fori(1, 4) as i:
                for u in range(4):
                    sp.wait_ge(proj_done, 4 * i + (G_F + u - 3))
                    sp.sem_inc(slot_free, 1)
                    load(u, o_v[:, :, bass.ds(P * u + 4 * P * i, P)])
            sp.wait_ge(y_evac, 32)
            sp.wait_ge(proj_done, G_F)
            for t in range(TT):
                sp.dma_start(xf[:, t, :], x_prompt[0, tok(t), :]).then_inc(x_back, 16)
            sp.dma_start(xfs[0:NS, :], x_sample.rearrange("b s d -> (b s) d")).then_inc(x_back, 16)
            sp.dma_start(postb, post_norm[0:1, :].broadcast_to([P, D])).then_inc(x_back, 16)
            for t in range(5):
                sp.wait_ge(y_fin, t + 1)
                sp.dma_start(y_p[0, tok(t), :] if t < TT else y_s.rearrange("b s d -> (b s) d"),
                             Yo[0:TOK[t], t, :]).then_inc(y_out, 16)
            sp.wait_ge(y_out, 16 * 5)

        @block.gpsimd
        def _(pool):
            link = linker(pool, pool_c)
            g = nc.gpsimd
            link(g.memset(ones[:, :], 1.0))
            g.affine_select(out=ident[:, :], in_=ones[:, :], compare_op=ALU.is_equal, fill=0.0, base=0,
                            pattern=[[-1, P]], channel_multiplier=1).then_inc(consts, 1)
            g.affine_select(out=tri_le[:, :], in_=ones[:, :], compare_op=ALU.is_ge, fill=0.0, base=0,
                            pattern=[[1, P]], channel_multiplier=-1).then_inc(consts, 1)
            g.affine_select(out=tri_lt[:, :], in_=ones[:, :], compare_op=ALU.is_gt, fill=0.0, base=0,
                            pattern=[[1, P]], channel_multiplier=-1).then_inc(consts, 1)
            link(g.affine_select(out=swap[:, :], in_=ones[:, :], compare_op=ALU.is_equal, fill=0.0, base=64,
                                 pattern=[[-1, P]], channel_multiplier=1))
            g.affine_select(out=swap[:, :], in_=swap[:, :], compare_op=ALU.not_equal, fill=1.0, base=-64,
                            pattern=[[-1, P]], channel_multiplier=1).then_inc(consts, 1)
            link(g.iota(pm64, [[0, 1]], base=0, channel_multiplier=1, allow_small_or_imprecise_dtypes=True))
            g.iota(small[64:128, 20:21], [[0, 1]], base=0, channel_multiplier=1,
                   allow_small_or_imprecise_dtypes=True).then_inc(consts, 1)
            pool.wait_ge(consts, 5)
            g.iota(iota_b[:, :], [[1, SEL_S]], base=0, channel_multiplier=0,
                   allow_small_or_imprecise_dtypes=True).then_inc(consts, 1)
            g.memset(eps_c, EPS).then_inc(consts, 1)
            link(g.memset(coef[:, :], 1.0))
            link(g.affine_select(out=coef[:, :], in_=coef[:, :], compare_op=ALU.not_equal, fill=2048.0, base=-1,
                                 pattern=[[0, 1]], channel_multiplier=1))
            g.affine_select(out=coef[:, :], in_=coef[:, :], compare_op=ALU.not_equal, fill=128.0, base=-2,
                            pattern=[[0, 1]], channel_multiplier=1).then_inc(consts, 1)
            for s in range(31):
                g.memset(bit_i[:, s:s + 1], 1 << (30 - s))
                g.memset(bit_f[:, s:s + 1], float(1 << (30 - s)))
            g.memset(bit_i[:, 31:32], 0)
            g.memset(bit_f[:, 31:32], 0.0).then_inc(consts, 1)
            g.memset(qblk[:, :, :], 0.0).then_inc(consts, 1)
            g.memset(qm[:, :], 0.0).then_inc(consts, 1)
            g.memset(ab[:, :, :], 0.0).then_inc(consts, 1)
            g.memset(small[:, 0:20], 1.0).then_inc(consts, 1)
            g.memset(Y[:, :, NPG:NPG + 1], TAKEN).then_inc(consts, 1)
            blk = cols[0:64, 0:8]
            link(g.affine_select(out=blk, in_=ones[0:64, 0:8], compare_op=ALU.is_ge, fill=0.0, base=0,
                                 pattern=[[-8, 8]], channel_multiplier=1))
            g.affine_select(out=blk, in_=blk, compare_op=ALU.is_ge, fill=0.0, base=7,
                            pattern=[[8, 8]], channel_multiplier=-1).then_inc(consts, 1)

            pool.wait_ge(off_done, 1)
            for b in range(NS):
                if b >= 2:
                    pool.wait_ge(kp_ps, 4 * (b - 1))
                for c in range(16):
                    g.indirect_dma_start(out=kraw[b % 2][:, c, :], out_offset=None, in_=kidx_rows,
                                         in_offset=bass.IndirectOffsetOnAxis(ap=off_i[:, 16 * b + c:16 * b + c + 1].bitcast(U32), axis=0),
                                         ).then_inc(kraw_in[b % 2], 16)
            for t in range(1, TT):
                pool.wait_ge(idx_acc, 16 * t)
                g.affine_select(out=idx[:, t, t * P:t * P + P], in_=idx[:, t, t * P:t * P + P], compare_op=ALU.is_ge,
                                fill=NEG, base=0, pattern=[[-1, P]], channel_multiplier=1).then_inc(idx_mask, 1)
            link(g.memset(idx[:, 0, 0:P], 0.0))
            g.affine_select(out=idx[:, 0, 0:P], in_=idx[:, 0, 0:P], compare_op=ALU.is_ge,
                            fill=NEG, base=0, pattern=[[-1, P]], channel_multiplier=1).then_inc(idx_mask, 1)

            pool.wait_ge(sel_done, 1)
            def gather(m):
                if m >= 3:
                    prev = m - 3
                    if prev < NS:
                        pool.wait_ge(sk_ps, prev + 1)
                    else:
                        pool.wait_ge(so_ps, prev - NS + 1)
                b = m % NS
                for half in range(2):
                    g.indirect_dma_start(out=kv_sel[:, m % 3, half, :], out_offset=None,
                                         in_=ck_rows if m < NS else cv_rows,
                                         in_offset=bass.IndirectOffsetOnAxis(
                                             ap=sel_i[:, 2 * b + half:2 * b + half + 1].bitcast(U32), axis=0),
                                         ).then_inc(kv_in[m % 3], 16)
            for m in range(3):
                gather(m)
            for n in range(AH * TT):
                L = P * (n % TT + 1)
                pool.wait_ge(p_rc, n + 1)
                g.tensor_scalar(Lb[:, n % 2, 0:L], Lb[:, n % 2, 0:L], rc[:, n % 2:n % 2 + 1], None,
                                ALU.mult).then_inc(p_rdy, 1)
            for m in range(3, 2 * NS):
                gather(m)

            for h in range(BH):
                pool.wait_ge(g_exp, h + 1)
                if h:
                    pool.wait_ge(g_oT, h)
                g.affine_select(out=Ds, in_=Di, compare_op=ALU.is_gt, fill=0.0, base=0,
                                pattern=[[0, TT], [-1, P]], channel_multiplier=1).then_inc(g_msk, 1)
                pool.wait_ge(g_msk, 2 * h + 1)
                g.affine_select(out=Di, in_=Di, compare_op=ALU.is_ge, fill=0.0, base=0,
                                pattern=[[0, TT], [-1, P]], channel_multiplier=1).then_inc(g_msk, 1)
            pool.wait_ge(s_tsb, 2)
            for q in range(16):
                if q >= 2:
                    pool.wait_ge(s_op, q - 1)
                g.tensor_tensor(vexp[q % 2], gsm[0:64, 0:2, :].rearrange("p a b -> p (a b)").unsqueeze(1).broadcast_to([64, 4, P]),
                                ident[0:64, 4 * q:4 * q + 4].unsqueeze(2).broadcast_to([64, 4, P]), ALU.mult).then_inc(s_vx, 1)

        @block.tensor
        def _(pe):
            te = nc.tensor
            pe.wait_ge(consts, N_CONST)
            pe.wait_ge(par_in, 48)
            te.transpose(mb[0][:, 0:113], par[0:113, :], ident[0:113, 0:113]).then_inc(parT_ps, 1)
            pe.wait_ge(st_in, 16)
            for c in range(24):
                m = te.transpose(mb[2 + c // 12][:, 24 * (c % 12):24 * (c % 12) + 24], st_nat[:, c * P:c * P + P],
                                 ident[0:24, 0:24])
            m.then_inc(parT_ps, 1)
            pe.wait_ge(parT_sb, 3)
            for t in range(5):
                n = TOK[t]
                pe.wait_ge(x_scaled, t + 1)
                for q in range(4):
                    e = 4 * t + q
                    if e >= 4:
                        pe.wait_ge(xT_sb, e - 3)
                    for u in range(4):
                        k = 4 * q + u
                        m = te.transpose(mb[q][:, u * P:u * P + n], x_nat[0:n, t, k * P:k * P + P], ident[0:n, 0:n])
                    m.then_inc(xT_ps, 1)
            pe.wait_ge(xT_sb, 20)
            pe.wait_ge(wa_in, 32)
            for t in range(5):
                n = TOK[t]
                for k in range(KT):
                    m = te.matmul(mb[0][0:n, 96 * t:96 * t + 96], hT[:, k, tok(t)], wa[:, k, :],
                                  start=(k == 0), stop=(k == KT - 1))
            m.then_inc(ab_ps, 1)
            pe.wait_ge(ki_done, 5)
            for t in range(5):
                n = TOK[t]
                m = te.transpose(mb[1 + t // 4][:, (t % 4) * P:(t % 4) * P + n], kin[0:n, t, :, :].rearrange("p a b -> p (a b)"),
                                 ident[0:n, 0:n])
            m.then_inc(kiT_ps, 1)

            def project(pair, slot, rhs, k0=0, kn=KT, extra=None):
                for k in range(kn):
                    for half in range(2):
                        m = te.matmul(pj[pair][:, half, 0:HALF], ring[:, slot, k0 + k, :],
                                      rhs[:, k, half * HALF:half * HALF + HALF], start=(k == 0), stop=(k == kn - 1))
                m.then_inc(proj_done, 1)

            def tiles_b(i, first):
                for u in range(4):
                    pe.wait_ge(w_in_s[u], 16 * i + 16)
                    if not (first and u < 2):
                        pe.wait_ge(proj_evac, 4 * i + (u - 1))
                    project(u % 2, u, hT)
            tiles_b(0, True)
            with pe.Fori(1, 5) as i:
                tiles_b(i, False)

            pe.wait_ge(proj_evac, 20)
            pe.wait_ge(kiT_sb, 2)
            for t in range(5):
                n = TOK[t]
                if t >= 2:
                    pe.wait_ge(kv_sb, t - 1)
                for c in range(4):
                    m = te.transpose(mb[t % 2][0:n, c * P:c * P + P], UA[:, U_K + c, tok(t)], ident[:, :])
                m.then_inc(kv_ps, 1)
            te.matmul(mb[2][:, 0:64], swap[:, :], UA[:, U_QI:U_QI + 8, NP:T], start=True, stop=True).then_inc(q_swap, 1)
            pe.wait_ge(w_x, 1)
            te.matmul(mb[3][:, 0:P], ones[0:NS, :], xw[:, :, :], start=True, stop=True).then_inc(q_swap, 1)
            pe.wait_ge(q_blk, 1)
            pe.wait_ge(w_bc, 1)
            pe.wait_ge(kv_sb, 5)
            for n in range(48):
                t, hh = n // 16 + 1, n % 16
                if n >= 4:
                    pe.wait_ge(idx_relu, n - 3)
                lo = 64 * (hh % 2)
                te.matmul(mb[n % 4][:, 0:P * (t + 1)], UA[lo:lo + 64, U_QI + hh // 2, tok(t)],
                          kIT[lo:lo + 64, 0:P * (t + 1)], start=True, stop=True).then_inc(idx_ps, 1)
            pe.wait_ge(idx_relu, 48)

            def kidx_T(b):
                pe.wait_ge(kraw_in[b % 2], 256 * (b // 2 + 1))
                for q in range(4):
                    if b:
                        pe.wait_ge(kp_sb, 4 * (b - 1) + q + 1)
                    for u in range(4):
                        m = te.transpose(mb[q][:, u * P:u * P + P], kraw[b % 2][:, 4 * q + u, :], ident[:, :])
                    m.then_inc(kp_ps, 1)

            def kidx_score(b):
                pe.wait_ge(kp_sb, 4 * (b + 1))
                if b >= 2:
                    pe.wait_ge(ks_sum, b - 1)
                for c in range(16):
                    m = te.matmul(pj[0][:, b % 2, 32 * c:32 * c + 32], kTp[b % 2][:, c, :], qblk[:, b, :],
                                  start=True, stop=True)
                m.then_inc(ks_ps, 1)
            kidx_T(0)
            for b in range(NS):
                if b + 1 < NS:
                    kidx_T(b + 1)
                kidx_score(b)
            for b in range(NS):
                m = te.matmul(pj[1][:, 0, 16 * b:16 * b + 16], kIT[0:64, NP + b:NP + b + 1].broadcast_to([64, P]),
                              qblk[0:64, b, 0:16], start=True, stop=True)
            m.then_inc(ks_ps, 1)
            pe.wait_ge(ks_sum, NS + 1)

            def count(v):
                pe.wait_ge(cnt_part, v)
                te.matmul(mb[0][:, 0:NS], ones[:, :], srt[:, 0, :], start=True, stop=True).then_inc(cnt_all, 1)
            count(1)
            with pe.Fori(0, 8) as i:
                for u in range(4):
                    pe.wait_ge(w_in_s[u], 16 * i + 16 * (L_C // 4 + 1))
                    pe.wait_ge(proj_evac, 4 * i + (G_C + u - 1))
                    project(u % 2, u, hT)
                    count(4 * i + (u + 2))

            srt_pair = t1[:, 0:NS * 17]
            pe.wait_ge(rank_in, 1)
            te.matmul(mb[0][:, 0:NS], ones[:, :], srt[:, 0, :], start=True, stop=True).then_inc(rank_ps, 1)
            pe.wait_ge(rank_in, 2)
            te.matmul(mb[2][:, 0:NS * 17], tri_lt[:, :], srt_pair, start=True, stop=True).then_inc(rank_ps, 1)
            te.matmul(mb[3][:, 0:NS * 17], ones[:, :], srt_pair, start=True, stop=True).then_inc(rank_ps, 1)
            pe.wait_ge(rank_in, 3)
            te.matmul(mb[2][:, 0:NS * 17], tri_lt[:, :], srt_pair, start=True, stop=True).then_inc(rank_ps, 1)
            te.matmul(mb[3][:, 0:NS * 17], ones[:, :], srt_pair, start=True, stop=True).then_inc(rank_ps, 1)
            pe.wait_ge(rank_in, 4)
            te.matmul(mb[0][:, 8:8 + NS], ones[:, :], srt[:, 0, :], start=True, stop=True).then_inc(rank_ps, 1)
            for b in range(NS):
                if b >= 2:
                    pe.wait_ge(row_sb, b - 1)
                for c in range(NPG):
                    e = NPG * b + c
                    pe.wait_ge(hot, e + 1)
                    m = te.matmul(mb[1][0:3, 256 * (b % 2):256 * (b % 2) + 256] if b % 2 == 0 else mb[2][0:3, 0:256],
                                  vals[:, e // 2, e % 2, :], onehot[:, e % 4, :],
                                  start=(c == 0), stop=(c == NPG - 1))
                    m.then_inc(hot_ps, 1)
                pe.wait_ge(row_sb, b + 1)
                for half in range(2):
                    m = te.matmul(mb[3][:, 2 * b + half:2 * b + half + 1], row3[0:3, b % 2, half * P:half * P + P],
                                  coef[:, :], start=True, stop=True)
                m.then_inc(row_ps, 1)
            pe.wait_ge(sel_done, 1)
            pe.wait_ge(masks, 1)
            pe.wait_ge(proj_evac, G_D)

            def logits(n):
                h, t = divmod(n, TT)
                if n >= 2:
                    pe.wait_ge(lg_max, n - 1)
                te.matmul(mb[n % 2][:, 0:P * (t + 1)], UA[:, h, tok(t)], UA[:, U_K + h // GRP, 0:P * (t + 1)],
                          start=True, stop=True).then_inc(lg_ps, 1)

            def probs_T(n):
                pe.wait_ge(p_rdy, n + 1)
                if n >= 2:
                    pe.wait_ge(pt_sb, n - 1)
                for l in range(n % TT + 1):
                    m = te.transpose(mb[2 + n % 2][:, l * P:l * P + P], Lb[:, n % 2, l * P:l * P + P], ident[:, :])
                m.then_inc(pt_ps, 1)

            def probs_v(n):
                h, t = divmod(n, TT)
                pe.wait_ge(pt_sb, n + 1)
                if n >= 2:
                    pe.wait_ge(pv_sb, n - 1)
                c0 = (h // GRP) * HD
                for l in range(t + 1):
                    m = te.matmul(pj[0][:, n % 2, 0:P], vn[:, l, c0:c0 + HD], PTs[:, n % 2, l * P:l * P + P],
                                  start=(l == 0), stop=(l == t))
                m.then_inc(pv_ps, 1)
            NI = AH * TT
            for n in range(NI + 2):
                if n < NI:
                    logits(n)
                if 1 <= n <= NI:
                    probs_T(n - 1)
                if n >= 2:
                    probs_v(n - 2)
            pe.wait_ge(pv_sb, NI)

            for b in range(NS):
                pe.wait_ge(kv_in[b % 3], 32 * (b // 3 + 1))
                if b >= 2:
                    pe.wait_ge(sk_sb, b - 1)
                for n in range(AKV):
                    for half in range(2):
                        m = te.transpose(mb[b % 2][:, n * 256 + half * P:n * 256 + half * P + P],
                                         kv_sel[:, b % 3, half, n * HD:n * HD + HD], ident[:, :])
                m.then_inc(sk_ps, 1)
                pe.wait_ge(sk_sb, b + 1)
                for n in range(AKV):
                    m = te.matmul(pj[1][0:64, 0, 0:257], qm[:, (2 * b + n) * 64:(2 * b + n) * 64 + 64], KTs[:, n, :],
                                  start=(b == 0 and n == 0), stop=(b == NS - 1 and n == AKV - 1))
                m.then_inc(sl_ps, 1)
            pe.wait_ge(s_p, 1)
            te.transpose(mb[2][:, 0:64], Ls[:, 0:P], ident[0:64, 0:64])
            te.transpose(mb[2][:, 64:128], Ls[:, P:2 * P], ident[0:64, 0:64])
            te.matmul(mb[2][:, 128:192], Ls[:, 256:257].broadcast_to([64, P]), ident[0:64, 0:64],
                      start=True, stop=True).then_inc(sp_ps, 1)
            pe.wait_ge(sp_sb, 1)
            for b in range(NS):
                m_ = NS + b
                pe.wait_ge(kv_in[m_ % 3], 32 * (m_ // 3 + 1))
                for n in range(AKV):
                    for half in range(2):
                        c = b * AH + n * GRP
                        m = te.matmul(mb[3][:, c:c + GRP], kv_sel[:, m_ % 3, half, n * HD:n * HD + HD],
                                      PTs_s[:, half, c:c + GRP], start=(half == 0), stop=(half == 1))
                m.then_inc(so_ps, 1)
            pe.wait_ge(so_sb, 1)

            with pe.Fori(0, 2) as i:
                for u in range(4):
                    pe.wait_ge(w_in_s[u], 16 * i + 16 * (L_D // 4 + 1))
                    pe.wait_ge(proj_evac, 4 * i + (G_D + u - 1))
                    project(u % 2, u, hT)
            pe.wait_ge(proj_evac, G_E)

            for q in range(6):
                if q >= 2:
                    pe.wait_ge(cv_sb, q - 1)
                for u in range(4):
                    m = te.transpose(mb[q % 2][0:11, u * P:u * P + P], UB[:, U_BQ + 4 * q + u, NP - 3:T], ident[:, :])
                m.then_inc(cv_ps, 1)

            def head_sums(n):
                pe.wait_ge(nq_sq, n + 1)
                if n >= 1:
                    pe.wait_ge(nq_rt, n)
                for half in range(2):
                    m = te.matmul(pj[0][:, half, 0:HALF], ones[:, :], nsq[:, half * HALF:half * HALF + HALF],
                                  start=True, stop=True)
                m.then_inc(nq_ps, 1)
            for n in range(16):
                head_sums(n)
            pe.wait_ge(nq_done, 16)

            pe.wait_ge(dec_v, 1)
            te.matmul(mb[2][:, 0:32], tri_le[:, :], gv[:, 0, 0:32], start=True, stop=True)
            te.matmul(mb[2][:, 32:64], ones[:, :], gv[:, 0, 0:32], start=True, stop=True).then_inc(dec_ps, 1)
            pe.wait_ge(dec_done, 1)

            for h in range(BH):
                for c in range(TT):
                    m = te.matmul(mb[2][:, c * P:c * P + P], gv[:, 0, c * BH + h:c * BH + h + 1].broadcast_to([P, P]),
                                  tri_le[:, :], start=True, stop=True)
                m.then_inc(g_row, 1)
                for c in range(TT):
                    te.transpose(mb[0][:, c * P:c * P + P], UB[:, U_BK + h, tok(c)], ident[:, :])
                    te.transpose(mb[1][:, c * P:c * P + P], UB[:, U_BV + h, tok(c)], ident[:, :])
                    te.matmul(mb[3][:, c * P:c * P + P], UB[:, U_BK + h, tok(c)], UB[:, U_BK + h, tok(c)],
                              start=True, stop=True)
                    m = te.matmul(pj[0][:, 0, c * P:c * P + P], UB[:, U_BQ + h, tok(c)], UB[:, U_BK + h, tok(c)],
                                  start=True, stop=True)
                m.then_inc(g_pre_ps, 1)
                pe.wait_ge(g_n, h + 1)
                for c in range(TT):
                    m = te.transpose(mb[2][:, c * P:c * P + P], Mb[0][:, c, :], ident[:, :])
                m.then_inc(g_tr, 1)
                pe.wait_ge(g_at, h + 1)
                for c in range(TT):
                    m = te.transpose(pj[0][:, 1, c * P:c * P + P], outn[:, c, :], ident[:, :])
                m.then_inc(g_tr, 1)
                pe.wait_ge(g_nt, 2 * h + 1)
                pe.wait_ge(g_y, 7 * h + 1)
                for s in range(1, 7):
                    M, MT = Mb[2 * ((s - 1) % 2)], Mb[2 * ((s - 1) % 2) + 1]
                    M2 = Mb[2 * (s % 2)]
                    if s > 1:
                        pe.wait_ge(g_mt, 5 * h + s - 1)
                    for c in range(TT):
                        m = te.matmul(pj[1][:, 0, c * P:c * P + P], MT[:, c, :], M[:, c, :], start=True, stop=True)
                    m.then_inc(g_sq, 1)
                    if s < 6:
                        for c in range(TT):
                            m = te.matmul(pj[1][:, 1, c * P:c * P + P], M[:, c, :], MT[:, c, :], start=True, stop=True)
                        m.then_inc(g_sq, 1)
                    pe.wait_ge(g_m, 6 * h + s)
                    pe.wait_ge(g_y, 7 * h + s)
                    for c in range(TT):
                        m = te.matmul(mb[3][:, c * P:c * P + P], M2[:, c, :], Yt[:, c, :], start=True, stop=True)
                    m.then_inc(g_yps, 1)
                pe.wait_ge(g_nt, 2 * h + 2)
                pe.wait_ge(g_y, 7 * h + 7)
                for c in range(TT):
                    e = TT * h + c
                    if c:
                        pe.wait_ge(c_s, e)
                        te.matmul(mb[0][:, c * P:c * P + P], UB[:, U_BK + h, tok(c)], Sst, start=True, stop=True).then_inc(c_ks, 1)
                    pe.wait_ge(c_r, e + 1)
                    te.matmul(mb[1][:, c * P:c * P + P], Yt[:, c, :], rr, start=True, stop=True).then_inc(c_vps, 1)
                    pe.wait_ge(c_vn, e + 1)
                    if e:
                        pe.wait_ge(c_o, e)
                    te.matmul(mb[2][:, c * P:c * P + P], kd[:, c, :], vnew, start=True, stop=True)
                    m = te.matmul(mb[3][:, c * P:c * P + P], atT[:, c, :], vnew, start=True, stop=True)
                    if c:
                        m = te.matmul(pj[0][:, 0, c * P:c * P + P], UB[:, U_BQ + h, tok(c)], Sst, start=True, stop=True)
                    m.then_inc(c_st, 1)
                pe.wait_ge(c_o, TT * h + TT)
                for c in range(TT):
                    m = te.transpose(mb[2][:, c * P:c * P + P], outn[:, c, :], ident[:, :])
                m.then_inc(g_oT, 1)
                pe.wait_ge(g_out, h + 1)

            pe.wait_ge(s_bc, 1)
            te.matmul(mb[0][:, 0:64], ones[0:NS, :], gsm[0:NS, 2, :], start=True, stop=True)
            te.matmul(mb[0][:, 64:128], ones[0:NS, :], gsm[0:NS, 3, :], start=True, stop=True)
            te.matmul(mb[0][:, 128:192], ones[:, :], gsm[:, 4, :], start=True, stop=True).then_inc(s_bcs, 1)
            for q in range(16):
                pe.wait_ge(S_in[q % 4], 16 * (q // 4 + 1))
                for r in range(4):
                    e = 4 * q + r
                    m = te.matmul(mb[1][:, 2 * e:2 * e + 2], Sld[q % 4][:, r, :], kqs[:, e, :], start=True, stop=True)
                m.then_inc(s_ks, 1)
            pe.wait_ge(s_vn, 1)
            te.transpose(mb[2][0:64, 0:P], gsm[:, 5, :], ident[:, :])
            te.transpose(mb[2][0:64, P:2 * P], gsm[:, 6, :], ident[:, :]).then_inc(s_tps, 1)
            pe.wait_ge(s_tsb, 2)
            for q in range(16):
                pe.wait_ge(s_vx, q + 1)
                if q >= 2:
                    pe.wait_ge(s_new, q - 1)
                te.matmul(mb[2 + q % 2][:, :], kns, vexp[q % 2].rearrange("p r n -> p (r n)"),
                          start=True, stop=True).then_inc(s_op, 1)
            pe.wait_ge(s_new, 16)
            for n in range(16, 24):
                head_sums(n)
            pe.wait_ge(gated, 16)

            def merge(i, first):
                for j in range(4):
                    def arrived(l):
                        n = 0
                        for x in range(l % 4, l + 1, 4):
                            n += 32 if x % 3 == 2 else 16
                        pe.wait_ge(w_in_s[l % 4], 64 * i + (240 + n))
                    l = 3 * j
                    arrived(l)
                    if first and j == 0:
                        pass
                    else:
                        pe.wait_ge(y_evac, 8 * i + (2 * j - 1))
                    project(0, l % 4, hT)
                    arrived(l + 1)
                    if not (first and j == 0):
                        pe.wait_ge(y_evac, 8 * i + 2 * j)
                    project(1, (l + 1) % 4, hT)
                    arrived(l + 2)
                    pe.wait_ge(proj_evac, 8 * i + (G_E + 2 * j + 1))
                    project(0, (l + 2) % 4, UA[:, 0:8, :], 0, 8)
                    pe.wait_ge(proj_evac, 8 * i + (G_E + 2 * j + 2))
                    project(1, (l + 2) % 4, UB[:, U_BQ:U_BQ + 8, :], 8, 8)
            merge(0, True)
            with pe.Fori(1, 4) as i:
                merge(i, False)

            mT = UB[:, 16:32, :]
            pe.wait_ge(y_evac, 32)

            def out_T(i, j, first):
                pe.wait_ge(proj_evac, 4 * i + (93 + j))
                if not (first and j < 2):
                    pe.wait_ge(oT_sb, 4 * i + (j - 1))
                for t in range(TT):
                    te.transpose(mb[j % 2][:, t * P:t * P + P], oT[j % 2][:, tok(t)], ident[:, :])
                te.transpose(mb[2 + j % 2][0:NS, 0:P], oT[j % 2][:, NP:T], ident[:, :]).then_inc(oT_ps, 1)

            def out_tiles(i, first):
                for u in range(4):
                    pe.wait_ge(w_in_s[u], 16 * i + (496 + 16))
                    if not (first and u < 2):
                        pe.wait_ge(proj_evac, 4 * i + (92 + u - 1))
                    project(u % 2, u, mT)
                    if not (first and u == 0):
                        if u:
                            out_T(i, u - 1, first)
                        else:
                            out_T(i - 1, 3, False)
            out_tiles(0, True)
            with pe.Fori(1, 4) as i:
                out_tiles(i, False)
            out_T(3, 3, False)


        @block.scalar
        def _(act):
            sc = nc.scalar
            link = linker(act, act_c)
            act.dma_start(idxg, idx_k_norm[0:1, :].broadcast_to([P, ID])).then_inc(row_in, 16)
            act.dma_start(alog, a_log[0:1, :].broadcast_to([P, BH])).then_inc(row_in, 16)
            act.dma_start(dtb, dt_bias[0:1, :].broadcast_to([P, BH])).then_inc(row_in, 16)
            act.dma_start(pt_i[:, :], page_table.rearrange("(a b) n -> a (b n)", a=1).broadcast_to([P, NS * NPG])).then_inc(pt_in, 16)
            act.wait_ge(consts, N_CONST)
            for t in range(5):
                n = TOK[t]
                act.wait_ge(x_in[t], 16)
                if t:
                    act.wait_ge(sq_done, t)
                sc.activation(junk[0:n, :], x_nat[0:n, t, :], ACT.Square, accum_out=ssq[0:n, t:t + 1]).then_inc(sq_done, 1)
            act.wait_ge(x_ms, 1)
            sc.activation(rs_x, rs_x, ACT.Sqrt).then_inc(x_sqrt, 1)
            act.wait_ge(ki_ms, 1)
            sc.activation(ki_r, ki_s, ACT.Sqrt).then_inc(ki_sqrt, 1)
            act.wait_ge(kiT_ps, 1)
            sc.activation(kIT[:, 0:NP], mb[1][:, :], ACT.Copy).then_inc(kiT_sb, 1)
            sc.activation(kIT[:, NP:T], mb[2][:, 0:NS], ACT.Copy).then_inc(kiT_sb, 1)

            def evac(dst, pair, done, func=ACT.Copy):
                act.wait_ge(proj_done, done)
                sc.activation(dst.rearrange("p (h n) -> p h n", h=2), pj[pair][:, :, 0:HALF], func).then_inc(proj_evac, 1)
            with act.Fori(0, 5) as i:
                for u in range(4):
                    evac(UA[:, bass.ds(4 * i + u, 1), :].rearrange("p a b -> p (a b)"), u % 2, 4 * i + (u + 1))
            for t in range(5):
                n = TOK[t]
                act.wait_ge(kv_ps, t + 1)
                if t:
                    act.wait_ge(kv_out, 32 * t)
                sc.activation(knat_t[0:n, :], mb[t % 2][0:n, :], ACT.Copy).then_inc(kv_sb, 1)
                act.wait_ge(kv_sb, t + 1)
                if t < TT:
                    link(sc.activation(vn[:, t, :], knat_t[:, 256:512], ACT.Copy))
                    act.dma_start(k_p[0, 0, tok(t)].rearrange("s n d -> s (n d)"), knat_t[:, 0:256]).then_inc(kv_out, 16)
                    act.dma_start(v_p[0, 0, tok(t)].rearrange("s n d -> s (n d)"), knat_t[:, 256:512]).then_inc(kv_out, 16)
                else:
                    act.dma_start(k_s[0].rearrange("b s n d -> (b s) (n d)"), knat_t[0:NS, 0:256]).then_inc(kv_out, 16)
                    act.dma_start(v_s[0].rearrange("b s n d -> (b s) (n d)"), knat_t[0:NS, 256:512]).then_inc(kv_out, 16)
            act.wait_ge(ki_done, 5)
            for t in range(TT):
                act.dma_start(kidx_p[0, 0, tok(t), :], kin[:, t, 0, :]).then_inc(kv_out, 16)
            act.dma_start(kidx_s[0].rearrange("b s d -> (b s) d"), kin[0:NS, TT, 0, :]).then_inc(kv_out, 16)
            for n in range(48):
                L = P * (n // 16 + 2)
                act.wait_ge(idx_ps, n + 1)
                if n >= 4:
                    act.wait_ge(idx_acc, n - 3)
                sc.activation(rel[:, n % 4, 0:L], mb[n % 4][:, 0:L], ACT.Relu).then_inc(idx_relu, 1)
            for b in range(NS):
                if b >= 2:
                    act.wait_ge(ks_ps, b - 1)
                for q in range(4):
                    act.wait_ge(kp_ps, 4 * b + q + 1)
                    sc.activation(kTp[b % 2][:, 4 * q:4 * q + 4, :].rearrange("p a b -> p (a b)"), mb[q][:, :],
                                  ACT.Copy).then_inc(kp_sb, 1)
            act.wait_ge(kv_out, 32 * 5 + 16 * 5)
            with act.Fori(0, 8) as i:
                for u in range(4):
                    evac(UB[:, bass.ds(4 * i + u, 1), :].rearrange("p a b -> p (a b)"), u % 2, 4 * i + (G_C + u + 1))
            for b in range(NS):
                act.wait_ge(hot_ps, NPG * (b + 1))
                if b >= 2:
                    act.wait_ge(row_ps, b - 1)
                sc.activation(row3[:, b % 2, :], mb[1][0:3, 0:256] if b % 2 == 0 else mb[2][0:3, 0:256],
                              ACT.Copy).then_inc(row_sb, 1)
            NI = AH * TT
            for n in range(NI + 1):
                if n < NI:
                    L = P * (n % TT + 1)
                    act.wait_ge(lg_max, n + 1)
                    sc.activation(Lb[:, n % 2, 0:L], Lb[:, n % 2, 0:L], ACT.Exp, bias=nm[:, n % 2:n % 2 + 1], scale=A_SCALE,
                                  accum_out=sm[:, n % 2:n % 2 + 1]).then_inc(p_exp, 1)
                if n >= 1:
                    m = n - 1
                    L = P * (m % TT + 1)
                    act.wait_ge(pt_ps, m + 1)
                    if m >= 2:
                        act.wait_ge(pv_ps, m - 1)
                    sc.activation(PTs[:, m % 2, 0:L], mb[2 + m % 2][:, 0:L], ACT.Copy).then_inc(pt_sb, 1)
            for b in range(NS):
                act.wait_ge(sk_ps, b + 1)
                if b:
                    act.wait_ge(sl_ps, b)
                link(sc.activation(KTs[:, :, 0:256], mb[b % 2][:, :].rearrange("p (n c) -> p n c", n=2), ACT.Copy))
                sc.activation(KTs[:, :, 256:257], UA[:, U_K:U_K + 2, NP + b:NP + b + 1], ACT.Copy).then_inc(sk_sb, 1)
            act.wait_ge(s_max, 1)
            sc.activation(Ls, Ls, ACT.Exp, bias=cols[0:64, 16:17], scale=A_SCALE, accum_out=cols[0:64, 17:18]).then_inc(s_exp, 1)
            act.wait_ge(sp_ps, 1)
            link(sc.activation(tmpS, mb[2][:, 128:192], ACT.Copy))
            sc.activation(PTs_s.rearrange("p h c -> p (h c)"), mb[2][:, 0:128], ACT.Copy).then_inc(sp_sb, 1)
            act.wait_ge(so_sb, 1)
            with act.Fori(0, 2) as i:
                for u in range(4):
                    evac(UA[:, bass.ds(4 * i + (U_QI + u), 1), :].rearrange("p a b -> p (a b)"), u % 2, 4 * i + (G_D + u + 1))

            for q in range(6):
                act.wait_ge(cv_ps, q + 1)
                if q:
                    act.wait_ge(cv_out, 16 + 32 * q)
                sc.activation(R2[0:11, 0:512], mb[q % 2][0:11, :], ACT.Copy).then_inc(cv_sb, 1)
                act.wait_ge(cv_sb, q + 1)
                act.dma_start(conv_p[0, 0, :, 512 * q:512 * q + 512], R2[0:3, 0:512]).then_inc(cv_out, 16)
                act.dma_start(conv_s[0, :, 2, 512 * q:512 * q + 512], R2[3:11, 0:512]).then_inc(cv_out, 16)
            act.wait_ge(cv_out, 16 + 32 * 6)
            act.wait_ge(kv_out, 32 * 5 + 16 * 5)
            for c in range(24):
                act.wait_ge(cv_acc, c + 1)
                sc.activation(UB[:, U_BQ + c, :], cvt, ACT.Silu).then_inc(cv_silu, 1)

            def norm_steps(n):
                src = UB[:, U_BQ + n, :] if n < 16 else UB[:, U_BQ + n - 16, :]
                if n:
                    act.wait_ge(nq_ps, n)
                sc.activation(nsq, src, ACT.Square).then_inc(nq_sq, 1)
                act.wait_ge(nq_ps, n + 1)
                if n:
                    act.wait_ge(nq_done, n)
                sc.activation(nrm.rearrange("p (h n) -> p h n", h=2), pj[0][:, :, 0:HALF], ACT.Sqrt, bias=eps_c,
                              scale=1.0 if n < 16 else 1.0 / HD).then_inc(nq_rt, 1)
            for n in range(16):
                norm_steps(n)
            act.wait_ge(dec_a, 1)
            link(sc.activation(gv[:, 1, :], gv[:, 1, :], ACT.Exp, scale=-1.0))
            link(sc.activation(gv[:, 1, :], gv[:, 1, :], ACT.Ln, bias=1.0))
            link(sc.activation(alog, alog, ACT.Exp))
            sc.activation(gv[:, 2, :].rearrange("p (t h) -> p t h", t=5), ab[:, :, 88:96], ACT.Sigmoid).then_inc(dec_e, 1)
            act.wait_ge(dec_a, 2)
            link(sc.activation(gv[:, 4, 0:32], gv[:, 3, 0:32], ACT.Exp))
            link(sc.activation(gv[:, 5, 0:32], gv[:, 5, 0:32], ACT.Exp))
            sc.activation(gv[:, 6, 0:32], gv[:, 6, 0:32], ACT.Exp).then_inc(dec_e, 1)
            for h in range(BH):
                act.wait_ge(g_nt_in, h + 1)
                sc.activation(Di, Di, ACT.Exp, scale=-1.0).then_inc(g_exp, 1)
                act.wait_ge(g_y, 7 * h + 1)
                sc.activation(Mb[1], mb[2][:, :].rearrange("p (c n) -> p c n", c=4), ACT.Copy).then_inc(g_nt, 1)
                act.wait_ge(g_tr, 2 * h + 2)
                sc.activation(atT, pj[0][:, 1, :].rearrange("p (c n) -> p c n", c=4), ACT.Copy).then_inc(g_nt, 1)
                for s in range(1, 6):
                    act.wait_ge(g_sq, 11 * h + 2 * s)
                    act.wait_ge(g_m, 6 * h + s)
                    sc.activation(Mb[2 * (s % 2) + 1], pj[1][:, 1, :].rearrange("p (c n) -> p c n", c=4),
                                  ACT.Copy).then_inc(g_mt, 1)
                for c in range(TT):
                    act.wait_ge(c_vps, TT * h + c + 1)
                    sc.activation(vnew, mb[1][:, c * P:c * P + P], ACT.Copy).then_inc(c_vn, 1)
                act.wait_ge(g_oT, h + 1)
                sc.activation(UB[:, U_BQ + h, 0:NP], mb[2][:, :], ACT.Copy).then_inc(g_out, 1)
                act.wait_ge(c_s, TT * h + TT)
                act.dma_start(ssm_p[0, 0, h], Sst).then_inc(ssm_out, 16)
            act.wait_ge(ssm_out, 16 * BH)
            def load_S(q, n):
                h, b0 = q // 2, 4 * (q % 2)
                act.dma_start(Sld[n % 4], state_ssm[0, b0:b0 + 4, h].rearrange("b k v -> k b v")).then_inc(S_in[n % 4], 16)
            for q in range(16):
                if q >= 4:
                    act.wait_ge(s_ks, q - 3)
                load_S(q, q)
            act.wait_ge(s_bcs, 1)
            sc.activation(gsm[:, 7, :], mb[0][:, 0:64], ACT.Exp).then_inc(s_kq, 1)
            act.wait_ge(s_tps, 1)
            sc.activation(kns, mb[2][0:64, 0:P], ACT.Copy).then_inc(s_tsb, 1)
            sc.activation(gsm[0:64, 0:2, :].rearrange("p a b -> p (a b)"), mb[2][0:64, P:2 * P], ACT.Copy).then_inc(s_tsb, 1)
            for q in range(16 + 2):
                if q < 16:
                    if q >= 4:
                        act.wait_ge(S_out[q % 4], 16 * (q // 4))
                    else:
                        act.wait_ge(s_ks, 16)
                    load_S(q, q)
                if q >= 2:
                    m = q - 2
                    h, b0 = m // 2, 4 * (m % 2)
                    act.wait_ge(s_new, m + 1)
                    act.dma_start(ssm_s[0, b0:b0 + 4, h].rearrange("b k v -> k b v"), Sld[m % 4]).then_inc(S_out[m % 4], 16)
            for r in range(4):
                act.wait_ge(S_out[r], 16 * 4)
            for n in range(16, 24):
                norm_steps(n)
            for c in range(16):
                z = UB[:, c, :] if c < 8 else UA[:, U_QI + c - 8, :]
                sc.activation(z, z, ACT.Silu).then_inc(z_silu, 1)
            act.wait_ge(gated, 16)

            def gates(i):
                for j in range(4):
                    evac(ga_sb, 0, 16 * i + (G_E + 4 * j + 1), ACT.Sigmoid)
                    evac(gb_sb, 1, 16 * i + (G_E + 4 * j + 2), ACT.Sigmoid)
            with act.Fori(0, 4) as i:
                gates(i)

            def outs(i, first):
                for u in range(4):
                    if not (first and u < 2):
                        act.wait_ge(oT_ps, 4 * i + (u - 1))
                    evac(oT[u % 2], u % 2, 4 * i + (G_F + u + 1))
            outs(0, True)
            with act.Fori(1, 4) as i:
                outs(i, False)
            act.wait_ge(oT_sb, 16)
            act.wait_ge(x_back, 96)
            for t in range(5):
                n = TOK[t]
                if t:
                    act.wait_ge(sq_done, 5 + t)
                sc.activation(osq[0:n, :], Yo[0:n, t, :], ACT.Square, accum_out=ssq[0:n, t:t + 1]).then_inc(sq_done, 1)
            act.wait_ge(o_ms, 1)
            sc.activation(rs_x, rs_x, ACT.Sqrt).then_inc(o_rt, 1)

        @block.vector
        def _(dve):
            ve = nc.vector
            link = linker(dve, dve_c)
            dve.wait_ge(consts, N_CONST)
            dve.wait_ge(pt_in, 16)
            ptv = pt_i[:, :].rearrange("p (c s) -> p c s", s=2)
            ve.tensor_copy(pg_i[0:64, :], ptv[0:64, :, 0])
            link(ve.tensor_copy(pg_i[64:128, :], ptv[64:128, :, 1]))
            ve.tensor_scalar(off_i[:, :], pg_i[:, :], 64.0, pm64, ALU.mult, ALU.add).then_inc(off_done, 1)
            dve.wait_ge(parT_ps, 1)
            ve.tensor_copy(parT[:, :], mb[0][:, 0:113]).then_inc(parT_sb, 1)
            dve.wait_ge(parT_ps, 2)
            for c in range(2):
                ve.tensor_copy(stT[:, 12 * c:12 * c + 12, :].rearrange("p a b -> p (a b)"), mb[2 + c][:, 0:288]).then_inc(parT_sb, 1)
            dve.wait_ge(sq_done, 5)
            ve.tensor_scalar(rs_x, ssq, 1.0 / D, EPS, ALU.mult, ALU.add).then_inc(x_ms, 1)
            dve.wait_ge(x_sqrt, 1)
            link(ve.reciprocal(rs_x, rs_x))
            for t in range(5):
                n = TOK[t]
                ve.tensor_scalar(x_nat[0:n, t, :], x_nat[0:n, t, :], rs_x[0:n, t:t + 1], None, ALU.mult).then_inc(x_scaled, 1)
            dve.wait_ge(parT_sb, 3)
            for t in range(5):
                n = TOK[t]
                for q in range(4):
                    dve.wait_ge(xT_ps, 4 * t + q + 1)
                    ve.tensor_tensor(hT[:, 4 * q:4 * q + 4, tok(t)], mb[q][:, :].rearrange("p (a b) -> p a b", a=4)[:, :, 0:n],
                                     g_pre[:, 4 * q:4 * q + 4].unsqueeze(2).broadcast_to([P, 4, n]), ALU.mult).then_inc(xT_sb, 1)
            dve.wait_ge(ab_ps, 1)
            ve.tensor_copy(ab[:, 0:4, :].rearrange("p a b -> p (a b)"), mb[0][:, 0:384])
            link(ve.tensor_copy(ab[0:NS, 4, :], mb[0][0:NS, 384:480]))
            jk = junk[:, 0:5 * ID].rearrange("p (t d) -> p t d", t=5)
            link(ve.tensor_tensor(jk, ab[:, :, 0:ID], ab[:, :, 0:ID], ALU.mult))
            link(ve.tensor_reduce(ki_s, jk, AX, ALU.add))
            ve.tensor_scalar(ki_s, ki_s, 1.0 / ID, EPS, ALU.mult, ALU.add).then_inc(ki_ms, 1)
            dve.wait_ge(ki_sqrt, 1)
            dve.wait_ge(row_in, 48)
            link(ve.reciprocal(ki_r, ki_r))
            for t in range(5):
                ve.tensor_scalar(kin[:, t, 1, :], ab[:, t, 0:ID], ki_r[:, t:t + 1], None, ALU.mult)
            link(ve.tensor_scalar(ab[:, :, 64:80], ab[:, :, 64:80], I_SCALE, None, ALU.mult))
            for t in range(5):
                ve.tensor_tensor(kin[:, t, 0, :], kin[:, t, 1, :], idxg, ALU.mult)
            link(ve.memset(cols[:, 60:62], 0.0))
            for t in range(5):
                ve.tensor_copy(kin[:, t, 1, :], kin[:, t, 0, :]).then_inc(ki_done, 1)
            for b in range(NS):
                m = ve.tensor_scalar(xw[:, b, :].rearrange("p (e m) -> p e m", e=2), ab[0:NS, 4, 64:80].rearrange("p (m e) -> p e m", e=2),
                                     ident[0:NS, b:b + 1], None, ALU.mult)
            m.then_inc(w_x, 1)

            dve.wait_ge(q_swap, 1)
            qs = UA[:, U_QI:U_QI + 8, NP:T].rearrange("p m b -> p b m")
            qw = mb[2][:, 0:64].rearrange("p (m b) -> p b m", b=NS)
            ve.tensor_copy(qblk[0:64, :, 0:8], qs[0:64])
            ve.tensor_copy(qblk[0:64, :, 8:16], qw[0:64])
            ve.tensor_copy(qblk[64:128, :, 16:24], qw[64:128])
            ve.tensor_copy(qblk[64:128, :, 24:32], qs[64:128]).then_inc(q_blk, 1)
            dve.wait_ge(q_swap, 2)
            ve.tensor_copy(wbc[:, :, :].rearrange("p b h -> p (b h)"), mb[3][:, 0:P]).then_inc(w_bc, 1)
            qmd = qm[:, :].rearrange("p (c x) -> p c x", x=68)
            for b in range(NS):
                for n in range(AKV):
                    ve.tensor_copy(qmd[:, 2 * b + n, 0:GRP], UA[:, n * GRP:n * GRP + GRP, NP + b])

            for n in range(48):
                t, hh = n // 16 + 1, n % 16
                L = P * (t + 1)
                dve.wait_ge(idx_relu, n + 1)
                w = ab[:, t, 64 + hh:65 + hh]
                if hh == 0:
                    ve.tensor_scalar(idx[:, t, 0:L], rel[:, n % 4, 0:L], w, None, ALU.mult).then_inc(idx_acc, 1)
                else:
                    dve.wait_ge(idx_acc, n)
                    ve.scalar_tensor_tensor(out=idx[:, t, 0:L], in0=rel[:, n % 4, 0:L], scalar=w, in1=idx[:, t, 0:L],
                                            op0=ALU.mult, op1=ALU.add).then_inc(idx_acc, 1)
            for b in range(NS + 1):
                dve.wait_ge(ks_ps, b + 1)
                if b < NS:
                    link(ve.scalar_tensor_tensor(out=wsum.rearrange("p (c h) -> p c h", h=IH),
                                                 in0=pj[0][:, b % 2, :].rearrange("p (c h) -> p c h", h=IH), scalar=0.0,
                                                 in1=wbc[:, b, :].unsqueeze(1).broadcast_to([P, NPG, IH]),
                                                 op0=ALU.max, op1=ALU.mult))
                    ve.tensor_reduce(Y[:, b, 0:NPG], wsum.rearrange("p (c h) -> p c h", h=IH), AX, ALU.add).then_inc(ks_sum, 1)
                    dve.wait_ge(ks_sum, b + 1)
                else:
                    link(ve.scalar_tensor_tensor(out=wsum[:, 0:P].rearrange("p (b h) -> p b h", h=IH),
                                                 in0=pj[1][:, 0, 0:P].rearrange("p (b h) -> p b h", h=IH), scalar=0.0,
                                                 in1=wbc[:, :, :], op0=ALU.max, op1=ALU.mult))
                    ve.tensor_reduce(Y[0:1, :, NPG], wsum[0:1, 0:P].rearrange("p (b h) -> p b h", h=IH), AX, ALU.add).then_inc(ks_sum, 1)
                    dve.wait_ge(ks_sum, NS + 1)

            hi_i = ge[:, 0:P].bitcast(I32)
            lo_i = ge[:, P:2 * P].bitcast(I32)
            ve.tensor_scalar(hi_i, pg_i[:, :], 4, None, ALU.logical_shift_right)
            link(ve.tensor_scalar(lo_i, pg_i[:, :], 15, None, ALU.bitwise_and))
            for par_ in range(2):
                ve.tensor_copy(vals[:, :, par_, 1], hi_i)
                ve.tensor_copy(vals[:, :, par_, 2], lo_i)
                ve.tensor_scalar(t1[:, par_:par_ + 1], pm64, 2.0, float(par_), ALU.mult, ALU.add)
            link(ve.memset(t1[:, 2:2 + P], 0.0))
            for par_ in range(2):
                link(ve.tensor_scalar(vals[:, :, par_, 0], t1[:, 2:2 + P], t1[:, par_:par_ + 1], None, ALU.add))

            Yf = Y[:, :, :]
            ge3 = ge[:, :].rearrange("p (b c) -> p b c", b=NS)
            part, sgn, thr, dif, thm, fac, need, cgt = (srt[:, r, :] for r in range(8))
            link(ve.memset(thr_i[:, :], 0))
            link(ve.tensor_scalar(ge3, Yf, 0.0, None, ALU.is_ge))
            ve.tensor_reduce(part, ge3, AX, ALU.add).then_inc(cnt_part, 1)
            dve.wait_ge(cnt_all, 1)
            link(ve.tensor_scalar(sgn, mb[0][:, 0:NS], SEL_S - 0.5, None, ALU.is_gt))
            link(ve.tensor_scalar(sgn, sgn, 2.0, -1.0, ALU.mult, ALU.add))
            for t in range(1, TT):
                dve.wait_ge(idx_mask, t)
            with dve.Fori(0, 8) as i:
                for u in range(4):
                    s = 6 * (4 * i + u)
                    ve.tensor_tensor(cand_i[:, :], thr_i[:, :], bit_i[:, bass.ds(4 * i + u, 1)].broadcast_to([P, NS]),
                                     ALU.bitwise_or).then_inc(srch, 1)
                    dve.wait_ge(srch, s + 1)
                    ve.tensor_tensor(thr, cand_i[:, :].bitcast(F32), sgn, ALU.mult).then_inc(srch, 1)
                    dve.wait_ge(srch, s + 2)
                    ve.tensor_tensor(ge3, Yf, thr.unsqueeze(2).broadcast_to([P, NS, NPG + 1]), ALU.is_ge).then_inc(srch, 1)
                    dve.wait_ge(srch, s + 3)
                    ve.tensor_reduce(part, ge3, AX, ALU.add).then_inc(cnt_part, 1)
                    if u % 2 == 0:
                        for t in range(1, TT):
                            e = 6 * (2 * i + u // 2) + 2 * (t - 1)
                            L = P * (t + 1)
                            ve.max(top8[:, t, :], idx[:, t, 0:L]).then_inc(topk, 1)
                            dve.wait_ge(topk, e + 1)
                            dve.sem_inc(round_on, 1)
                            ve.match_replace(out=idx[:, t, 0:L], in_to_replace=top8[:, t, :], in_values=idx[:, t, 0:L],
                                             imm_value=TAKEN).then_inc(topk, 1)
                            dve.wait_ge(topk, e + 2)
                            dve.sem_inc(round_on, 1)
                    dve.wait_ge(cnt_all, 4 * i + (u + 2))
                    ve.scalar_tensor_tensor(out=dif, in0=mb[0][:, 0:NS], scalar=SEL_S - 0.5, in1=sgn,
                                            op0=ALU.subtract, op1=ALU.mult).then_inc(srch, 1)
                    dve.wait_ge(srch, s + 4)
                    ve.tensor_scalar(m_i[:, :], dif, 0.0, bit_f[:, bass.ds(4 * i + u, 1)], ALU.is_gt, ALU.mult).then_inc(srch, 1)
                    dve.wait_ge(srch, s + 5)
                    ve.tensor_tensor(thr_i[:, :], thr_i[:, :], m_i[:, :], ALU.bitwise_or).then_inc(srch, 1)
                    dve.wait_ge(srch, s + 6)
            link(ve.tensor_scalar(fac, sgn, 0.0, None, ALU.is_lt))
            link(ve.tensor_scalar(dif, fac, 0.7 * 2.0 ** -23, None, ALU.mult))
            link(ve.tensor_tensor(thm, thr_i[:, :].bitcast(F32), dif, ALU.mult))
            link(ve.tensor_tensor(thm, thm, thr_i[:, :].bitcast(F32), ALU.add))
            link(ve.tensor_scalar(fac, fac, 1.2e-38, None, ALU.mult))
            link(ve.tensor_tensor(thm, thm, fac, ALU.max))
            link(ve.tensor_tensor(thr, thm, sgn, ALU.mult))
            thb = thr.unsqueeze(2).broadcast_to([P, NS, NPG + 1])
            gt3 = wsum_gt[:, :].rearrange("p (b c) -> p b c", b=NS)
            link(ve.tensor_tensor(gt3, Yf, thb, ALU.is_gt))
            ve.tensor_reduce(part, gt3, AX, ALU.add).then_inc(rank_in, 1)
            link(ve.tensor_tensor(ge3, Yf, thb, ALU.is_equal))
            pair = t1[:, 0:NS * 17].rearrange("p (b c) -> p b c", b=NS)

            def pair_sums(src):
                s4 = src[:, :, 0:NPG].rearrange("p b (c s) -> p b c s", s=2)
                link(ve.tensor_copy(pair[:, :, 16:17], src[:, :, NPG:NPG + 1]))
                ve.tensor_tensor(pair[:, :, 0:16], s4[:, :, :, 0], s4[:, :, :, 1], ALU.add).then_inc(rank_in, 1)
            incl = rk[:, 0:NS * 17]
            rank = rk[:, 136:136 + 264].rearrange("p (b c) -> p b c", b=NS)
            rs17 = rk2[:, 0:NS * 17]
            link(ve.memset(rs17, 1.0))
            link(ve.memset(rs17.rearrange("p (b c) -> p b c", b=NS)[:, :, 0:1], 0.0))

            def rank_of(src):
                link(ve.tensor_tensor_scan(incl, rs17, mb[3][:, 0:NS * 17], 0.0, ALU.mult, ALU.add))
                link(ve.tensor_tensor(incl, incl, mb[3][:, 0:NS * 17], ALU.subtract))
                link(ve.tensor_tensor(incl, incl, mb[2][:, 0:NS * 17], ALU.add))
                i3 = incl.rearrange("p (b c) -> p b c", b=NS)
                r4 = rank[:, :, 0:NPG].rearrange("p b (c s) -> p b c s", s=2)
                s4 = src[:, :, 0:NPG].rearrange("p b (c s) -> p b c s", s=2)
                link(ve.tensor_copy(r4[:, :, :, 0], i3[:, :, 0:16]))
                link(ve.tensor_tensor(r4[:, :, :, 1], i3[:, :, 0:16], s4[:, :, :, 0], ALU.add))
                link(ve.tensor_copy(rank[:, :, NPG:NPG + 1], i3[:, :, 16:17]))
            pair_sums(ge3)
            dve.wait_ge(rank_ps, 1)
            link(ve.tensor_scalar(need, mb[0][:, 0:NS], -1.0, float(SEL_S), ALU.mult, ALU.add))
            dve.wait_ge(rank_ps, 3)
            rank_of(ge3)
            link(ve.tensor_tensor(rank, rank, need.unsqueeze(2).broadcast_to([P, NS, NPG + 1]), ALU.is_lt))
            link(ve.tensor_tensor(ge3, ge3, rank, ALU.mult))
            link(ve.tensor_tensor(gt3, gt3, ge3, ALU.add))
            pair_sums(gt3)
            dve.wait_ge(rank_ps, 5)
            rank_of(gt3)
            link(ve.tensor_scalar(rank, rank, 1.0, None, ALU.add))
            link(ve.tensor_tensor(rank, rank, gt3, ALU.mult))
            link(ve.tensor_scalar(pos[:, :].rearrange("p (b c) -> p b c", b=NS), rank, -1.0, None, ALU.add))
            ve.tensor_copy(part, gt3[:, :, NPG]).then_inc(rank_in, 1)
            dve.wait_ge(rank_ps, 6)
            link(ve.tensor_copy(cgt, mb[0][:, 8:8 + NS]))
            for e in range(NS * NPG):
                b, c = divmod(e, NPG)
                if e >= 4:
                    dve.wait_ge(hot_ps, e - 3)
                ve.tensor_scalar(onehot[:, e % 4, :], iota_b[:, :], pos[:, b * (NPG + 1) + c:b * (NPG + 1) + c + 1], None,
                                 ALU.is_equal).then_inc(hot, 1)
            dve.wait_ge(row_ps, NS)
            ve.tensor_copy(sel_i[:, :], mb[3][:, 0:16]).then_inc(sel_done, 1)
            dve.wait_ge(idx_mask, TT)
            for t in range(1, TT):
                L = P * (t + 1)
                m = ve.tensor_scalar(idx[:, t, 0:L], idx[:, t, 0:L], TAKEN, NEG, ALU.not_equal, ALU.mult)
            m.then_inc(masks, 1)
            dve.wait_ge(masks, 1)

            NI = AH * TT
            for n in range(NI + 2):
                if n < NI:
                    t = n % TT
                    L = P * (t + 1)
                    dve.wait_ge(lg_ps, n + 1)
                    if n >= 2:
                        dve.wait_ge(pt_ps, n - 1)
                    link(ve.tensor_tensor_reduce(Lb[:, n % 2, 0:L], mb[n % 2][:, 0:L], idx[:, t, 0:L], 1.0, NEG, ALU.add,
                                                 ALU.max, mx[:, n % 2:n % 2 + 1]))
                    ve.tensor_scalar(nm[:, n % 2:n % 2 + 1], mx[:, n % 2:n % 2 + 1], -A_SCALE, None, ALU.mult).then_inc(lg_max, 1)
                if 1 <= n <= NI:
                    m = n - 1
                    dve.wait_ge(p_exp, m + 1)
                    ve.reciprocal(rc[:, m % 2:m % 2 + 1], sm[:, m % 2:m % 2 + 1]).then_inc(p_rc, 1)
                if n >= 2:
                    m = n - 2
                    dve.wait_ge(pv_ps, m + 1)
                    ve.tensor_copy(UA[:, m // TT, tok(m % TT)], pj[0][:, m % 2, 0:P]).then_inc(pv_sb, 1)
            dve.wait_ge(sl_ps, NS)
            link(ve.tensor_copy(Ls, pj[1][0:64, 0, 0:257]))
            fl, f2 = cols[0:64, 18:19], cols[0:64, 19:20]
            link(ve.tensor_tensor(cols[0:64, 8:16], cols[0:64, 0:8], cgt[0:64, :], ALU.mult))
            link(ve.tensor_reduce(fl, cols[0:64, 8:16], AX, ALU.add))
            link(ve.tensor_scalar(f2, fl, 1.0, -NEG, ALU.subtract, ALU.mult))
            link(ve.tensor_scalar(fl, fl, NEG, None, ALU.mult))
            link(ve.tensor_tensor(Ls[:, 255:256], Ls[:, 255:256], fl, ALU.add))
            link(ve.tensor_tensor(Ls[:, 256:257], Ls[:, 256:257], f2, ALU.add))
            link(ve.tensor_reduce(cols[0:64, 20:21], Ls, AX, ALU.max))
            ve.tensor_scalar(cols[0:64, 16:17], cols[0:64, 20:21], -A_SCALE, None, ALU.mult).then_inc(s_max, 1)
            dve.wait_ge(s_exp, 1)
            link(ve.reciprocal(cols[0:64, 17:18], cols[0:64, 17:18]))
            ve.tensor_scalar(Ls, Ls, cols[0:64, 17:18], None, ALU.mult).then_inc(s_p, 1)
            dve.wait_ge(sp_sb, 1)
            tS = tmpS.rearrange("p (b h) -> p b h", b=NS)
            for n in range(AKV):
                ve.tensor_tensor(tS[:, :, n * GRP:n * GRP + GRP], tS[:, :, n * GRP:n * GRP + GRP],
                                 UA[:, U_V + n, NP:T].unsqueeze(2).broadcast_to([P, NS, GRP]), ALU.mult)
            link(ve.memset(cols[:, 60:62], 0.0))
            dve.wait_ge(so_ps, NS)
            ve.tensor_tensor(UA[:, 0:8, NP:T].rearrange("p h b -> p b h"), mb[3][:, 0:64].rearrange("p (b h) -> p b h", b=NS),
                             tS, ALU.add).then_inc(so_sb, 1)

            dve.wait_ge(cv_ps, 6)
            for c in range(24):
                raw = UB[:, U_BQ + c, :]
                if c:
                    dve.wait_ge(cv_silu, c)
                link(ve.tensor_scalar(cvt, raw, conv_col(3, c), None, ALU.mult))
                for j in range(3):
                    d = 3 - j
                    ve.scalar_tensor_tensor(out=cvt[:, d:NP], in0=raw[:, 0:NP - d], scalar=conv_col(j, c), in1=cvt[:, d:NP],
                                            op0=ALU.mult, op1=ALU.add).then_inc(cv_samp, 1)
                    m = ve.scalar_tensor_tensor(out=cvt[:, NP:T], in0=stT[:, c, j::3], scalar=conv_col(j, c), in1=cvt[:, NP:T],
                                                op0=ALU.mult, op1=ALU.add)
                    if j < 2:
                        link(m)
                        dve.wait_ge(cv_samp, 3 * c + j + 1)
                m.then_inc(cv_acc, 1)

            def norm_mul(n):
                dve.wait_ge(nq_rt, n + 1)
                link(ve.reciprocal(nrm, nrm))
                dst = UB[:, U_BQ + n, :] if n < 16 else UB[:, U_BQ + n - 16, :]
                sc_ = A_SCALE if n < 8 else (1.0 if n < 16 else gdn_g)
                ve.scalar_tensor_tensor(out=dst, in0=dst, scalar=sc_, in1=nrm, op0=ALU.mult, op1=ALU.mult).then_inc(nq_done, 1)
            for n in range(16):
                norm_mul(n)

            g3 = gv[:, 3, :].rearrange("p (t h) -> p t h", t=5)
            link(ve.tensor_tensor(g3, ab[:, :, 80:88], dtb.unsqueeze(1).broadcast_to([P, 5, BH]), ALU.add))
            link(ve.tensor_scalar(gv[:, 0, :], gv[:, 3, :], -1.0, None, ALU.mult))
            ve.tensor_tensor(gv[:, 1, :], gv[:, 3, :], gv[:, 0, :], ALU.max).then_inc(dec_a, 1)
            dve.wait_ge(dec_e, 1)
            link(ve.tensor_scalar(gv[:, 3, :], gv[:, 3, :], 0.0, None, ALU.max))
            link(ve.tensor_tensor(gv[:, 3, :], gv[:, 3, :], gv[:, 1, :], ALU.add))
            ve.scalar_tensor_tensor(out=gv[:, 0, :].rearrange("p (t h) -> p t h", t=5), in0=g3, scalar=-1.0,
                                    in1=alog.unsqueeze(1).broadcast_to([P, 5, BH]), op0=ALU.mult, op1=ALU.mult).then_inc(dec_v, 1)
            dve.wait_ge(dec_ps, 1)
            cum, beta, ecum, etot, kdec, nbe, nbeta = gv[:, 3, :], gv[:, 2, :], gv[:, 4, :], gv[:, 5, :], gv[:, 6, :], gv[:, 7, :], gv[:, 1, :]
            link(ve.tensor_copy(cum[:, 0:32], mb[2][:, 0:32]))
            link(ve.tensor_copy(etot[:, 0:32], mb[2][:, 32:64]))
            ve.tensor_tensor(kdec[:, 0:32], etot[:, 0:32], cum[:, 0:32], ALU.subtract).then_inc(dec_a, 1)
            dve.wait_ge(dec_e, 2)
            link(ve.tensor_scalar(nbeta, beta, -1.0, None, ALU.mult))
            ve.tensor_tensor(nbe[:, 0:32], nbeta[:, 0:32], ecum[:, 0:32], ALU.mult).then_inc(dec_done, 1)
            dve.wait_ge(dec_done, 1)

            def hc(v, h):
                return v[:, h:32:BH].unsqueeze(2).broadcast_to([P, TT, P])
            c4 = "p (c n) -> p c n"
            for h in range(BH):
                dve.wait_ge(g_row, h + 1)
                link(ve.tensor_tensor(Di, mb[2][:, :].rearrange(c4, c=4), hc(cum, h), ALU.subtract))
                ve.tensor_scalar(Di, Di, 0.0, None, ALU.max).then_inc(g_nt_in, 1)
                dve.wait_ge(g_pre_ps, h + 1)
                ve.tensor_tensor(kd, mb[0][:, :].rearrange(c4, c=4), hc(kdec, h), ALU.mult)
                ve.tensor_tensor(vb, mb[1][:, :].rearrange(c4, c=4), hc(beta, h), ALU.mult)
                dve.wait_ge(g_msk, 2 * h + 1)
                for c in range(TT):
                    e = c * BH + h
                    m = ve.scalar_tensor_tensor(out=Mb[0][:, c, :], in0=mb[3][:, c * P:c * P + P], scalar=nbeta[:, e:e + 1],
                                                in1=Ds[:, c, :], op0=ALU.mult, op1=ALU.mult)
                m.then_inc(g_n, 1)
                dve.wait_ge(g_msk, 2 * h + 2)
                ve.tensor_tensor(outn, pj[0][:, 0, :].rearrange(c4, c=4), Di, ALU.mult).then_inc(g_at, 1)
                dve.wait_ge(g_tr, 2 * h + 1)
                ve.tensor_tensor(Yt, mb[2][:, :].rearrange(c4, c=4), ident[:, :].unsqueeze(1).broadcast_to([P, TT, P]),
                                 ALU.add).then_inc(g_y, 1)
                for s in range(1, 7):
                    dve.wait_ge(g_sq, 11 * h + 2 * s - 1)
                    ve.tensor_copy(Mb[2 * (s % 2)], pj[1][:, 0, :].rearrange(c4, c=4)).then_inc(g_m, 1)
                    dve.wait_ge(g_yps, 6 * h + s)
                    dve.wait_ge(g_y, 7 * h + s)
                    ve.tensor_tensor(Yt, Yt, mb[3][:, :].rearrange(c4, c=4), ALU.add).then_inc(g_y, 1)
                for c in range(TT):
                    e = c * BH + h
                    n = TT * h + c
                    if c == 0:
                        ve.tensor_copy(rr, vb[:, 0, :]).then_inc(c_r, 1)
                    else:
                        dve.wait_ge(c_ks, 3 * h + c)
                        ve.scalar_tensor_tensor(out=rr, in0=mb[0][:, c * P:c * P + P], scalar=nbe[:, e:e + 1], in1=vb[:, c, :],
                                                op0=ALU.mult, op1=ALU.add).then_inc(c_r, 1)
                    dve.wait_ge(c_st, n + 1)
                    if c == 0:
                        if h:
                            dve.wait_ge(ssm_out, 16 * h)
                        ve.tensor_copy(Sst, mb[2][:, 0:P]).then_inc(c_s, 1)
                        ve.tensor_copy(outn[:, 0, :], mb[3][:, 0:P]).then_inc(c_o, 1)
                    else:
                        ve.scalar_tensor_tensor(out=Sst, in0=Sst, scalar=etot[:, e:e + 1], in1=mb[2][:, c * P:c * P + P],
                                                op0=ALU.mult, op1=ALU.add).then_inc(c_s, 1)
                        link(ve.tensor_copy(outn[:, c, :], mb[3][:, c * P:c * P + P]))
                        ve.scalar_tensor_tensor(out=outn[:, c, :], in0=pj[0][:, 0, c * P:c * P + P], scalar=ecum[:, e:e + 1],
                                                in1=outn[:, c, :], op0=ALU.mult, op1=ALU.add).then_inc(c_o, 1)
                    dve.wait_ge(c_s, n + 1)

            dve.wait_ge(g_out, BH)
            id8 = ident[0:NS, 0:NS].unsqueeze(1).broadcast_to([NS, BH, NS])
            for src, slot in ((0, 2), (2, 3)):
                ve.tensor_tensor(gsm[0:NS, slot, :].rearrange("p (h b) -> p h b", h=BH),
                                 gv[0:NS, src, 32:40].unsqueeze(2).broadcast_to([NS, BH, NS]), id8, ALU.mult)
            kS = UB[:, U_BK:U_BK + 8, NP:T]
            qS = UB[:, U_BQ:U_BQ + 8, NP:T]
            vS = UB[:, U_BV:U_BV + 8, NP:T]
            h8 = "p (h b) -> p h b"
            ve.tensor_tensor(gsm[:, 4, :].rearrange(h8, h=BH), kS, qS, ALU.mult)
            link(ve.tensor_copy(gsm[:, 5, :].rearrange(h8, h=BH), kS))
            ve.tensor_copy(kqs[:, :, 0].rearrange(h8, h=BH), kS)
            ve.tensor_copy(kqs[:, :, 1].rearrange(h8, h=BH), qS).then_inc(s_bc, 1)
            dve.wait_ge(s_kq, 1)
            eg, bt, qk, vv = gsm[:, 7, :], gsm[:, 2, :], gsm[:, 3, :], gsm[:, 6, :]
            ve.tensor_copy(bt, mb[0][:, 64:128])
            link(ve.tensor_copy(qk, mb[0][:, 128:192]))
            dve.wait_ge(s_ks, 16)
            kq_ps = mb[1][:, 0:P].rearrange("p (e t) -> p e t", t=2)
            link(ve.tensor_tensor(vv, kq_ps[:, :, 0], eg, ALU.mult))
            link(ve.tensor_tensor(vv.rearrange(h8, h=BH), vS, vv.rearrange(h8, h=BH), ALU.subtract))
            link(ve.tensor_tensor(vv, vv, bt, ALU.mult))
            link(ve.tensor_tensor(qk, qk, vv, ALU.mult))
            link(ve.tensor_tensor(bt, kq_ps[:, :, 1], eg, ALU.mult))
            ve.tensor_tensor(qS, bt.rearrange(h8, h=BH), qk.rearrange(h8, h=BH), ALU.add).then_inc(s_vn, 1)
            for q in range(16):
                dve.wait_ge(s_op, q + 1)
                dve.wait_ge(S_in[q % 4], 16 * (q // 4 + 5))
                for r in range(4):
                    e = 4 * q + r
                    m = ve.scalar_tensor_tensor(out=Sld[q % 4][:, r, :], in0=Sld[q % 4][:, r, :], scalar=eg[:, e:e + 1],
                                                in1=mb[2 + q % 2][:, r * P:r * P + P], op0=ALU.mult, op1=ALU.add)
                m.then_inc(s_new, 1)
            for n in range(16, 24):
                norm_mul(n)
            dve.wait_ge(nq_done, 24)
            for c in range(16):
                dve.wait_ge(z_silu, c + 1)
                dst = UA[:, c, :] if c < 8 else UB[:, U_BQ + c - 8, :]
                z = UB[:, c, :] if c < 8 else UA[:, U_QI + c - 8, :]
                ve.tensor_tensor(dst, dst, z, ALU.mult).then_inc(gated, 1)

            h2 = "p (h n) -> p h n"

            def merge(i):
                for j in range(4):
                    n = 4 * i + j
                    dve.wait_ge(proj_done, 16 * i + (G_E + 4 * j + 3))
                    ve.tensor_tensor(m1.rearrange(h2, h=2), pj[0][:, :, 0:HALF], ga_sb.rearrange(h2, h=2), ALU.mult).then_inc(y_evac, 1)
                    dve.wait_ge(proj_done, 16 * i + (G_E + 4 * j + 4))
                    ve.tensor_tensor(m2b.rearrange(h2, h=2), pj[1][:, :, 0:HALF], gb_sb.rearrange(h2, h=2), ALU.mult).then_inc(mrg, 1)
                    dve.wait_ge(mrg, n + 1)
                    ve.tensor_tensor(UB[:, bass.ds(4 * i + (16 + j), 1), :].rearrange("p a b -> p (a b)"), m1, m2b, ALU.add).then_inc(y_evac, 1)
                    dve.wait_ge(y_evac, 8 * i + (2 * j + 2))
            with dve.Fori(0, 4) as i:
                merge(i)

            def back(i):
                for u in range(4):
                    dve.wait_ge(oT_ps, 4 * i + (u + 1))
                    col = P * u + 4 * P * i
                    ve.tensor_copy(Yo[:, 0:4, bass.ds(col, P)], mb[u % 2][:, :].rearrange("p (t n) -> p t n", t=4))
                    ve.tensor_copy(Yo[0:NS, 4, bass.ds(col, P)], mb[2 + u % 2][0:NS, 0:P]).then_inc(oT_sb, 1)
            with dve.Fori(0, 4) as i:
                back(i)
            dve.wait_ge(sq_done, 10)
            ve.tensor_scalar(rs_x, ssq, 1.0 / D, EPS, ALU.mult, ALU.add).then_inc(o_ms, 1)
            dve.wait_ge(o_rt, 1)
            dve.wait_ge(x_back, 96)
            link(ve.reciprocal(rs_x, rs_x))
            for t in range(5):
                n = TOK[t]
                link(ve.scalar_tensor_tensor(out=Yo[0:n, t, :], in0=Yo[0:n, t, :], scalar=rs_x[0:n, t:t + 1], in1=postb[0:n, :],
                                             op0=ALU.mult, op1=ALU.mult))
                ve.tensor_tensor(Yo[0:n, t, :], Yo[0:n, t, :], xf[0:n, t, :] if t < TT else xfs[0:NS, :], ALU.add).then_inc(y_fin, 1)


_INS = ["x_prompt", "x_sample", "cache_k", "cache_v", "cache_kidx", "state_conv", "state_ssm", "page_table", "pre_norm",
        "post_norm", "w_in", "idx_k_norm", "conv_w", "a_log", "dt_bias", "gdn_norm", "w_pa", "w_pb", "w_o"]
_OUTS = [(1, NP, D), (NS, 1, D), (1, 1, NP, AKV, HD), (1, 1, NP, AKV, HD), (1, 1, NP, ID), (1, 1, CONV - 1, CD),
         (1, 1, BH, HD, HD), (1, NS, 1, AKV, HD), (1, NS, 1, AKV, HD), (1, NS, 1, ID), (1, NS, CONV - 1, CD),
         (1, NS, BH, HD, HD)]


def kernel(**inputs):
    import numpy as _np
    import concourse.bacc as _bacc
    from concourse import mybir as _mybir
    from concourse.bass_utils import run_bass_kernel_spmd as _run

    nc = _bacc.Bacc("TRN2", target_bir_lowering=False, num_devices=1)
    arrays, args = {}, []
    for name in _INS:
        a = _np.ascontiguousarray(inputs[name])
        arrays[f"in_{name}_dram"] = a
        args.append(nc.dram_tensor(f"in_{name}_dram", a.shape, _mybir.dt.from_np(a.dtype), kind="ExternalInput").ap())
    for i, shape in enumerate(_OUTS):
        args.append(nc.dram_tensor(f"out_{i}_dram", shape, _mybir.dt.float32, kind="ExternalOutput").ap())
    build(nc, *args)
    r = _run(nc, [arrays], core_ids=[0])
    return tuple(r.results[0][f"out_{i}_dram"] for i in range(len(_OUTS)))
```

```python
from contextlib import ExitStack

import concourse.bass as bass
from concourse import mybir

ALU = mybir.AluOpType
ACT = mybir.ActivationFunctionType
F32 = mybir.dt.float32
BF16 = mybir.dt.bfloat16
F16 = mybir.dt.float16
I32 = mybir.dt.int32
U32 = mybir.dt.uint32
AX = mybir.AxisListType.X

P = 128
D = 2048
KT = D // P
NP = 512
NS = 8
T = NP + NS
HALF = T // 2
TT = NP // P
TOK = [P] * TT + [NS]
HD = 128
AH, AKV = 8, 2
GRP = AH // AKV
IH, ID = 16, 64
BH = 8
CONV = 4
CD = 3 * BH * HD
PAGE, NPG, NPOOL = 128, 32, 320
PAST = PAGE * NPG
SEL_P = 128
SEL_S = 256
EPS = 1e-6
NEG = -1.0e30
TAKEN = -3.0e38
A_SCALE = HD ** -0.5
I_SCALE = ID ** -0.5 * IH ** -0.5

C_Q = 0
C_KI = 2560
C_ZA = 2640
C_AB = 6736
C_ZB = 6752
C_GA = 7776
C_GB = 9824

U_K, U_V, U_QI = 8, 10, 12
U_BQ, U_BK, U_BV = 8, 16, 24

G_B, G_H, G_C, G_A, G_D, G_G, G_E, G_F = 0, 20, 28, 60, 68, 76, 92, 124
L_F = 108
W_SC = 256.0
X_SC = 16.0
UNSC = 1.0 / (W_SC * X_SC)


def tok(t):
    return slice(t * P, t * P + TOK[t])


def build(nc, x_prompt, x_sample, cache_k, cache_v, cache_kidx, state_conv, state_ssm, page_table, pre_norm,
          post_norm, w_in, idx_k_norm, conv_w, a_log, dt_bias, gdn_norm, w_pa, w_pb, w_o,
          y_p, y_s, k_p, v_p, kidx_p, conv_p, ssm_p, k_s, v_s, kidx_s, conv_s, ssm_s):
    with ExitStack() as ctx:
        def sb(name, shape, dt=F32):
            return ctx.enter_context(nc.sbuf_tensor(name, shape, dt))

        def sem(name):
            return ctx.enter_context(nc.semaphore(name))

        hT = sb("hT", [P, KT, 2, T], F16)
        raw = sb("raw", [P, 2, KT, P])
        wsp = sb("wsp", [P, 2, 2, KT, P], F16)
        UA = sb("UA", [P, 20, T])
        UB = sb("UB", [P, 32, T])
        idx = sb("idx", [P, TT, NP])
        UAf = UA[:, :, :].rearrange("p a b -> p (a b)")
        UBf = UB[:, :, :].rearrange("p a b -> p (a b)")
        idf = idx[:, :, :].rearrange("p a b -> p (a b)")
        hTf = hT[:, :, :, :].rearrange("p a s b -> p (a s b)").bitcast(F32)
        UA16 = UAf[:, 0:8 * T].bitcast(F16).rearrange("p (k s n) -> p k s n", k=8, s=2)
        UBq16 = UBf[:, U_BQ * T:(U_BQ + 8) * T].bitcast(F16).rearrange("p (k s n) -> p k s n", k=8, s=2)
        mT16 = UBf[:, 16 * T:32 * T].bitcast(F16).rearrange("p (k s n) -> p k s n", k=16, s=2)

        ident = sb("ident", [P, P])
        ones = sb("ones", [P, P])
        tri_le = sb("tri_le", [P, P])
        tri_lt = sb("tri_lt", [P, P])
        swap = sb("swap", [P, P])
        parT = sb("parT", [P, 113])
        stT = sb("stT", [P, 24, 24])
        small = sb("small", [P, 160])
        ab = sb("ab", [P, 5, 96])
        kin = sb("kin", [P, 5, 2, ID])
        kIT = sb("kIT", [P, T])
        qblk = sb("qblk", [P, NS, 32])
        wbc = sb("wbc", [P, NS, IH])
        Y = sb("Y", [P, NS, NPG + 1])
        bit_i = sb("bit_i", [P, 32], I32)
        bit_f = sb("bit_f", [P, 32])
        thr_i = sb("thr_i", [P, NS], I32)
        cand_i = sb("cand_i", [P, NS], I32)
        m_i = sb("m_i", [P, NS], I32)
        srt = sb("srt", [P, 12, NS])
        iota_b = sb("iota_b", [P, SEL_S], BF16)
        coef = sb("coef", [3, 1])
        pg_i = sb("pg_i", [P, P], I32)
        off_i = sb("off_i", [P, P], I32)
        sel_i = sb("sel_i", [P, 16], I32)
        gv = sb("gv", [P, 12, 5 * BH])
        qm = sb("qm", [P, 1088])
        vn = sb("vn", [P, TT, 256])
        gsm = sb("gsm", [P, 8, 64])
        cols = sb("cols", [P, 64])
        top8 = sb("top8", [P, TT, 8])

        rs_x = small[:, 0:5]
        ssq = small[:, 5:10]
        ki_s = small[:, 10:15]
        ki_r = small[:, 15:20]
        pm64 = small[:, 20:21]
        alog = small[:, 24:32]
        dtb = small[:, 32:40]
        eps_c = small[:, 40:41]
        idxg = small[:, 64:128]
        mx = small[:, 128:130]
        nm = small[:, 130:132]
        sm = small[:, 132:134]
        rc = small[:, 134:136]
        g_pre = parT[:, 0:16]
        gdn_g = parT[:, 112:113]

        def conv_col(j, tile):
            return parT[:, 16 + 24 * j + tile:17 + 24 * j + tile]

        x_nat = UAf[:, 0:5 * D].rearrange("p (t d) -> p t d", t=5)
        st_nat = UBf[0:24, 0:CD]
        wa = UBf[:, 3072:3072 + KT * 96].rearrange("p (k n) -> p k n", k=KT)
        wa16 = UBf[:, 15872 - 1536:15872].bitcast(F16).rearrange("p (s k n) -> p s k n", s=2, k=KT)
        kraw = [UBf[:, 4608 + 2048 * i:6656 + 2048 * i].rearrange("p (c d) -> p c d", c=16) for i in range(2)]
        kTp = [UBf[:, 8704 + 2048 * i:10752 + 2048 * i].rearrange("p (c d) -> p c d", c=16) for i in range(2)]
        rel = UBf[:, 12800:14848].rearrange("p (r n) -> p r n", r=4)
        wsum = UBf[:, 3072:3584]
        xtmp = UBf[:, 12800:13824].rearrange("p (r a n) -> p r a n", r=2, a=4)
        junk = UBf[:, 12800:14848]
        knat_t = UBf[:, 3584:4096]

        pt_i = UBf[:, 15872:16128].bitcast(I32)
        xw = UBf[0:NS, 16128:16256].rearrange("p (b h) -> p b h", b=NS)
        par = UBf[:, 16256:16384]

        QS = UAf[:, U_QI * T:U_QI * T + 8 * T]
        NY = NS * (NPG + 1)
        ge, t1, pos, wsum_gt = (QS[:, NY * x:NY * x + NY] for x in range(4))
        rk = QS[:, 4 * NY:4 * NY + 400]
        rk2 = QS[:, 4 * NY + 400:4 * NY + 400 + NS * 17]
        qs0 = 4 * NY + 400 + NS * 17
        vals = QS[:, qs0:qs0 + 384].bitcast(BF16).rearrange("p (c s v) -> p c s v", s=2, v=3)
        onehot = QS[:, qs0 + 384:qs0 + 896].bitcast(BF16).rearrange("p (r n) -> p r n", r=4)
        row3 = QS[0:3, qs0 + 896:qs0 + 1408].rearrange("p (r n) -> p r n", r=2)
        QS = UAf[:, U_QI * T:U_QI * T + 8 * T]
        Lb = QS[:, 0:1024].rearrange("p (r n) -> p r n", r=2)
        PTs = QS[:, 1024:2048].rearrange("p (r n) -> p r n", r=2)
        KTs = QS[:, 2048:2562].rearrange("p (n c) -> p n c", n=2)
        kv_sel = QS[:, 2562:2562 + 1536].rearrange("p (s h c) -> p s h c", s=3, h=2)
        Ls = idf[0:64, 0:257]
        PTs_s = idf[:, 512:640].rearrange("p (h c) -> p h c", h=2)
        tmpS = idf[:, 640:704]

        kd = idf[:, 0:512].rearrange("p (c n) -> p c n", c=4)
        vb = idf[:, 512:1024].rearrange("p (c n) -> p c n", c=4)
        Ds = idf[:, 1024:1536].rearrange("p (c n) -> p c n", c=4)
        atT = idf[:, 1536:2048].rearrange("p (c n) -> p c n", c=4)
        R2 = UAf[:, U_K * T:U_K * T + 4 * T]
        Mb = [R2[:, 512 * i:512 * i + 512].rearrange("p (c n) -> p c n", c=4) for i in range(4)]
        Yt = qm[:, 0:512].rearrange("p (c n) -> p c n", c=4)
        outn = qm[:, 512:1024].rearrange("p (c n) -> p c n", c=4)
        vnf = vn[:, :, :].rearrange("p a b -> p (a b)")
        Di = vnf[:, 0:512].rearrange("p (c n) -> p c n", c=4)
        Sst = vnf[:, 512:640]
        rr = vnf[:, 640:768]
        vnew = vnf[:, 768:896]
        nrm = [idf[:, 0:T], idf[:, T:2 * T], idf[:, 2 * T:3 * T], qm[:, 0:T]]
        cvt = [idf[:, 2 * T:3 * T], idf[:, T:2 * T]]
        gate = [kIT[:, :], stT[:, :, :].rearrange("p a b -> p (a b)")[:, 0:T]]
        gate_e = [UBf[:, 0:T], UBf[:, T:2 * T]]
        gate_m = [idf[:, 0:T], idf[:, T:2 * T]]
        gate_d = nc.dram_tensor("gates", (2, KT, P, T), F32).ap()
        Sld = [idf[:, 512 * i:512 * i + 512].rearrange("p (r n) -> p r n", r=4) for i in range(4)]
        vexp = [R2[0:64, 512 * i:512 * i + 512].rearrange("p (r n) -> p r n", r=4) for i in range(2)]
        kns = gv[0:64, 8:12, :].rearrange("p a b -> p (a b)")[:, 0:P]
        kqs = gv[:, 1:5, :].rearrange("p a b -> p (a b)")[:, 0:P].rearrange("p (e t) -> p e t", t=2)
        gtmp = idf[:, 0:T]
        m1 = idf[:, 2 * T:3 * T]
        m2b = qm[:, 0:T]
        oT = [idf[:, 0:T], idf[:, T:2 * T]]
        Yo = UAf[:, 0:5 * D].rearrange("p (t d) -> p t d", t=5)
        xf = UBf[:, 0:4 * D].rearrange("p (t d) -> p t d", t=4)
        xfs = hTf[:, 0:D]
        postb = hTf[:, D:2 * D]
        osq = hTf[:, 2 * D:3 * D]

        pj = [ctx.enter_context(nc.psum_tensor(f"pj{i}", [P, 2, 512], F32)) for i in range(2)]
        mb = [ctx.enter_context(nc.psum_tensor(f"mb{i}", [P, 512], F32)) for i in range(4)]

        consts = sem("consts")
        par_in, st_in, wa_in = sem("par_in"), sem("st_in"), sem("wa_in")
        x_in = [sem(f"x_in{t}") for t in range(5)]
        row_in = sem("row_in")
        w_in_s = [sem(f"w_slot{i}") for i in range(2)]
        w_hi, w_lo, x_tmp, x_hi = sem("w_hi"), sem("w_lo"), sem("x_tmp"), sem("x_hi")
        parT_ps, parT_sb, sq_done, mean_sq, rms, x_scaled = (sem(n) for n in (
            "parT_ps", "parT_sb", "sq_done", "mean_sq", "rms", "x_scaled"))
        xT_sb, ab_ps, ab_sb, ki_done, kiT_ps, kiT_sb = (sem(n) for n in (
            "xT_sb", "ab_ps", "ab_sb", "ki_done", "kiT_ps", "kiT_sb"))
        proj_done, proj_evac, y_evac = sem("proj_done"), sem("proj_evac"), sem("y_evac")
        kv_ps, kv_sb, kv_out = sem("kv_ps"), sem("kv_sb"), sem("kv_out")
        q_swap, w_x, qw_done = sem("q_swap"), sem("w_x"), sem("qw_done")
        idx_ps, idx_relu, idx_acc, idx_mask = sem("idx_ps"), sem("idx_relu"), sem("idx_acc"), sem("idx_mask")
        off_done, kraw_in = sem("off_done"), [sem("kraw_in0"), sem("kraw_in1")]
        kp_ps, kp_sb, ks_ps, ks_sum = sem("kp_ps"), sem("kp_sb"), sem("ks_ps"), sem("ks_sum")
        cnt_part, cnt_all, srch, topk = sem("cnt_part"), sem("cnt_all"), sem("srch"), sem("topk")
        rank_in, rank_ps, hot, hot_ps, row_sb, row_ps, sel_done = (sem(n) for n in (
            "rank_in", "rank_ps", "hot", "hot_ps", "row_sb", "row_ps", "sel_done"))
        kv_in = [sem(f"kv_in{i}") for i in range(3)]
        masks = sem("masks")
        lg_ps, lg_max, p_exp, p_rc, p_rdy, pt_ps, pt_sb, pv_ps, pv_sb = (sem(n) for n in (
            "lg_ps", "lg_max", "p_exp", "p_rc", "p_rdy", "pt_ps", "pt_sb", "pv_ps", "pv_sb"))
        sk_ps, sk_sb, sl_ps, s_max, s_exp, s_p, sp_ps, sp_sb, so_ps, so_sb = (sem(n) for n in (
            "sk_ps", "sk_sb", "sl_ps", "s_max", "s_exp", "s_p", "sp_ps", "sp_sb", "so_ps", "so_sb"))
        cv_ps, cv_sb, cv_out, cv_acc, cv_silu, cv_samp = (sem(n) for n in (
            "cv_ps", "cv_sb", "cv_out", "cv_acc", "cv_silu", "cv_samp"))
        nq_sq, nq_ps, nq_rt, nq_done = sem("nq_sq"), sem("nq_ps"), sem("nq_rt"), sem("nq_done")
        dec_a, dec_v, dec_ps, dec_e = sem("dec_a"), sem("dec_v"), sem("dec_ps"), sem("dec_e")
        g_pre_ps, g_row, g_exp, g_msk, g_n, g_at, g_tr, g_nt, g_y = (sem(n) for n in (
            "g_pre_ps", "g_row", "g_exp", "g_msk", "g_n", "g_at", "g_tr", "g_nt", "g_y"))
        g_sq, g_m, g_mt, g_yps = sem("g_sq"), sem("g_m"), sem("g_mt"), sem("g_yps")
        c_ks, c_r, c_vps, c_vn, c_st, c_s, c_o, g_oT, g_out, ssm_out = (sem(n) for n in (
            "c_ks", "c_r", "c_vps", "c_vn", "c_st", "c_s", "c_o", "g_oT", "g_out", "ssm_out"))
        S_in = [sem(f"S_in{i}") for i in range(4)]
        s_kq, s_bc, s_bcs, s_ks, s_vn, s_tps, s_tsb, s_vx, s_op, s_new = (sem(n) for n in (
            "s_kq", "s_bc", "s_bcs", "s_ks", "s_vn", "s_tps", "s_tsb", "s_vx", "s_op", "s_new"))
        S_out = [sem(f"S_out{i}") for i in range(4)]
        waited = sem("waited")
        gate_out = [sem("gate_out0"), sem("gate_out1")]
        gate_in = [sem("gate_in0"), sem("gate_in1")]
        gate_sig = sem("gate_sig")
        mrg, g_nt_in = sem("mrg"), sem("g_nt_in")
        z_silu, gated = sem("z_silu"), sem("gated")
        oT_ps, oT_sb, x_back, y_fin, y_out = (sem(n) for n in (
            "oT_ps", "oT_sb", "x_back", "y_fin", "y_out"))
        dve_c, act_c, pool_c = sem("dve_c"), sem("act_c"), sem("pool_c")

        def linker(eng, s):
            n = [0]

            def link(ins):
                n[0] += 1
                ins.then_inc(s, 1)
                eng.wait_ge(s, n[0])
            return link

        w_in_v = w_in[0].rearrange("(k p) n -> p k n", p=P)
        pa_v = w_pa[0].rearrange("(k p) n -> p k n", p=P)
        pb_v = w_pb[0].rearrange("(k p) n -> p k n", p=P)
        o_v = w_o[0].rearrange("(k p) n -> p k n", p=P)
        kidx_rows = cache_kidx[0].rearrange("g (q s) d -> (g q) (s d)", s=2)
        ck_rows = cache_k[0].rearrange("g t n d -> (g t) (n d)")
        cv_rows = cache_v[0].rearrange("g t n d -> (g t) (n d)")
        N_CONST = 15

        def gate_group(f):
            return G_H + f if f < 8 else G_A + f - 8 if f < 16 else G_G + f - 16

        def nq_ln(n):
            return 8 * (n // 4) + n % 4 + 1

        block = ctx.enter_context(nc.Block())

        @block.sync
        def _(sp):
            sp.dma_start(par[0:16, :], pre_norm[0].rearrange("(k p) -> k p", p=P)).then_inc(par_in, 16)
            sp.dma_start(par[16:112, :], conv_w[0].rearrange("j (c p) -> (j c) p", p=P)).then_inc(par_in, 16)
            sp.dma_start(par[112:113, :], gdn_norm[0:1, :]).then_inc(par_in, 16)
            for t in range(TT):
                sp.dma_start(x_nat[:, t, :], x_prompt[0, tok(t), :]).then_inc(x_in[t], 16)
            sp.dma_start(x_nat[0:NS, TT, :], x_sample.rearrange("b s d -> (b s) d")).then_inc(x_in[TT], 16)
            sp.dma_start(wa[:, :, 0:80], w_in_v[:, :, C_KI:C_KI + 80]).then_inc(wa_in, 16)
            sp.dma_start(wa[:, :, 80:96], w_in_v[:, :, C_AB:C_AB + 16], ).then_inc(wa_in, 16)
            sp.dma_start(st_nat, state_conv[0].rearrange("b j c -> (b j) c")).then_inc(st_in, 16)
            sp.dma_start(conv_s[0, :, 0:2, :], state_conv[0, :, 1:3, :]).then_inc(cv_out, 16)

            def load(slot, src, dst=None):
                sp.dma_start(raw[:, slot, :, :] if dst is None else dst, src).then_inc(w_in_s[slot], 16)

            def split_free(v):
                sp.wait_ge(w_lo, v)
                sp.sem_inc(waited, 1)

            def in_loads(i, base, col, first=0):
                for u in range(first, 4):
                    split_free(4 * i + (base + u - 1))
                    load(u % 2, w_in_v[:, :, bass.ds(col + P * u + 4 * P * i, P)])
            for u in range(2):
                load(u, w_in_v[:, :, C_Q + P * u:C_Q + P * u + P])
            in_loads(0, 0, C_Q, 2)
            with sp.Fori(1, 5) as i:
                in_loads(i, 0, C_Q)
            with sp.Fori(0, 2) as i:
                in_loads(i, G_H, C_GB)
            with sp.Fori(0, 8) as i:
                in_loads(i, G_C, C_ZA)
            with sp.Fori(0, 2) as i:
                in_loads(i, G_A, C_GB + 8 * P)
            with sp.Fori(0, 2) as i:
                in_loads(i, G_D, C_ZB)
            with sp.Fori(0, 4) as i:
                in_loads(i, G_G, C_GA)

            def merge_load(i, j):
                col = 4 * P * i + P * j
                split_free(4 * i + (G_E + j - 1))
                load(j % 2, pa_v[:, :, bass.ds(col, P)], raw[:, j % 2, 0:8, :])
                load(j % 2, pb_v[:, :, bass.ds(col, P)], raw[:, j % 2, 8:16, :])

            def gates_back(i, j, used):
                if used is not None:
                    sp.wait_ge(y_evac, used)
                    sp.sem_inc(waited, 1)
                n = 4 * i + j
                for br, dst in ((0, gate[j % 2]), (1, gate_m[j % 2])):
                    sp.dma_start(dst.unsqueeze(1), gate_d[br, bass.ds(n, 1)].rearrange("n p t -> p n t")).then_inc(gate_in[j % 2], 16)
            merge_load(0, 0)
            merge_load(0, 1)
            for r in range(2):
                sp.wait_ge(gate_out[r], 16 * 16)
            sp.wait_ge(gated, 16)
            gates_back(0, 0, None)
            gates_back(0, 1, None)
            for j in range(2, 4):
                merge_load(0, j)
                gates_back(0, j, 2 * j - 2)
            with sp.Fori(1, 4) as i:
                for j in range(4):
                    merge_load(i, j)
                    gates_back(i, j, 8 * i + (2 * j - 2))
            with sp.Fori(0, 4) as i:
                for u in range(4):
                    split_free(4 * i + (L_F + u - 1))
                    load(u % 2, o_v[:, :, bass.ds(P * u + 4 * P * i, P)])
            sp.wait_ge(y_evac, 32)
            sp.wait_ge(proj_done, G_F)
            for t in range(TT):
                sp.dma_start(xf[:, t, :], x_prompt[0, tok(t), :]).then_inc(x_back, 16)
            sp.dma_start(xfs[0:NS, :], x_sample.rearrange("b s d -> (b s) d")).then_inc(x_back, 16)
            sp.dma_start(postb, post_norm[0:1, :].broadcast_to([P, D])).then_inc(x_back, 16)
            for t in range(5):
                sp.wait_ge(y_fin, t + 1)
                sp.dma_start(y_p[0, tok(t), :] if t < TT else y_s.rearrange("b s d -> (b s) d"),
                             Yo[0:TOK[t], t, :]).then_inc(y_out, 16)
            sp.wait_ge(y_out, 16 * 5)

        @block.gpsimd
        def _(pool):
            link = linker(pool, pool_c)
            g = nc.gpsimd
            link(g.memset(ones[:, :], 1.0))
            g.affine_select(out=ident[:, :], in_=ones[:, :], compare_op=ALU.is_equal, fill=0.0, base=0,
                            pattern=[[-1, P]], channel_multiplier=1).then_inc(consts, 1)
            g.affine_select(out=tri_le[:, :], in_=ones[:, :], compare_op=ALU.is_ge, fill=0.0, base=0,
                            pattern=[[1, P]], channel_multiplier=-1).then_inc(consts, 1)
            g.affine_select(out=tri_lt[:, :], in_=ones[:, :], compare_op=ALU.is_gt, fill=0.0, base=0,
                            pattern=[[1, P]], channel_multiplier=-1).then_inc(consts, 1)
            link(g.affine_select(out=swap[:, :], in_=ones[:, :], compare_op=ALU.is_equal, fill=0.0, base=64,
                                 pattern=[[-1, P]], channel_multiplier=1))
            g.affine_select(out=swap[:, :], in_=swap[:, :], compare_op=ALU.not_equal, fill=1.0, base=-64,
                            pattern=[[-1, P]], channel_multiplier=1).then_inc(consts, 1)
            link(g.iota(pm64, [[0, 1]], base=0, channel_multiplier=1, allow_small_or_imprecise_dtypes=True))
            g.iota(small[64:128, 20:21], [[0, 1]], base=0, channel_multiplier=1,
                   allow_small_or_imprecise_dtypes=True).then_inc(consts, 1)
            pool.wait_ge(consts, 5)
            g.iota(iota_b[:, :], [[1, SEL_S]], base=0, channel_multiplier=0,
                   allow_small_or_imprecise_dtypes=True).then_inc(consts, 1)
            g.memset(eps_c, EPS).then_inc(consts, 1)
            link(g.memset(coef[:, :], 1.0))
            link(g.affine_select(out=coef[:, :], in_=coef[:, :], compare_op=ALU.not_equal, fill=2048.0, base=-1,
                                 pattern=[[0, 1]], channel_multiplier=1))
            g.affine_select(out=coef[:, :], in_=coef[:, :], compare_op=ALU.not_equal, fill=128.0, base=-2,
                            pattern=[[0, 1]], channel_multiplier=1).then_inc(consts, 1)
            for s in range(31):
                g.memset(bit_i[:, s:s + 1], 1 << (30 - s))
                g.memset(bit_f[:, s:s + 1], float(1 << (30 - s)))
            g.memset(bit_i[:, 31:32], 0)
            g.memset(bit_f[:, 31:32], 0.0).then_inc(consts, 1)
            g.memset(qblk[:, :, :], 0.0).then_inc(consts, 1)
            g.memset(qm[:, :], 0.0).then_inc(consts, 1)
            g.memset(ab[:, :, :], 0.0).then_inc(consts, 1)
            g.memset(small[:, 0:20], 1.0).then_inc(consts, 1)
            g.memset(Y[:, :, NPG:NPG + 1], TAKEN).then_inc(consts, 1)
            blk = cols[0:64, 0:8]
            link(g.affine_select(out=blk, in_=ones[0:64, 0:8], compare_op=ALU.is_ge, fill=0.0, base=0,
                                 pattern=[[-8, 8]], channel_multiplier=1))
            g.affine_select(out=blk, in_=blk, compare_op=ALU.is_ge, fill=0.0, base=7,
                            pattern=[[8, 8]], channel_multiplier=-1).then_inc(consts, 1)

            pool.wait_ge(off_done, 1)
            for b in range(NS):
                if b >= 2:
                    pool.wait_ge(kp_ps, 4 * (b - 1))
                for c in range(16):
                    g.indirect_dma_start(out=kraw[b % 2][:, c, :], out_offset=None, in_=kidx_rows,
                                         in_offset=bass.IndirectOffsetOnAxis(ap=off_i[:, 16 * b + c:16 * b + c + 1].bitcast(U32), axis=0),
                                         ).then_inc(kraw_in[b % 2], 16)
            for t in range(1, TT):
                pool.wait_ge(idx_acc, 16 * t)
                g.affine_select(out=idx[:, t, t * P:t * P + P], in_=idx[:, t, t * P:t * P + P], compare_op=ALU.is_ge,
                                fill=NEG, base=0, pattern=[[-1, P]], channel_multiplier=1).then_inc(idx_mask, 1)
            link(g.memset(idx[:, 0, 0:P], 0.0))
            g.affine_select(out=idx[:, 0, 0:P], in_=idx[:, 0, 0:P], compare_op=ALU.is_ge,
                            fill=NEG, base=0, pattern=[[-1, P]], channel_multiplier=1).then_inc(idx_mask, 1)

            pool.wait_ge(sel_done, 1)
            def gather(m):
                if m >= 3:
                    prev = m - 3
                    if prev < NS:
                        pool.wait_ge(sk_ps, prev + 1)
                    else:
                        pool.wait_ge(so_ps, prev - NS + 1)
                b = m % NS
                for half in range(2):
                    g.indirect_dma_start(out=kv_sel[:, m % 3, half, :], out_offset=None,
                                         in_=ck_rows if m < NS else cv_rows,
                                         in_offset=bass.IndirectOffsetOnAxis(
                                             ap=sel_i[:, 2 * b + half:2 * b + half + 1].bitcast(U32), axis=0),
                                         ).then_inc(kv_in[m % 3], 16)
            for m in range(3):
                gather(m)
            for n in range(AH * TT):
                L = P * (n % TT + 1)
                pool.wait_ge(p_rc, n + 1)
                g.tensor_scalar(Lb[:, n % 2, 0:L], Lb[:, n % 2, 0:L], rc[:, n % 2:n % 2 + 1], None,
                                ALU.mult).then_inc(p_rdy, 1)
            for m in range(3, 2 * NS):
                gather(m)

            for h in range(BH):
                pool.wait_ge(g_exp, h + 1)
                if h:
                    pool.wait_ge(g_oT, h)
                g.affine_select(out=Ds, in_=Di, compare_op=ALU.is_gt, fill=0.0, base=0,
                                pattern=[[0, TT], [-1, P]], channel_multiplier=1).then_inc(g_msk, 1)
                pool.wait_ge(g_msk, 2 * h + 1)
                g.affine_select(out=Di, in_=Di, compare_op=ALU.is_ge, fill=0.0, base=0,
                                pattern=[[0, TT], [-1, P]], channel_multiplier=1).then_inc(g_msk, 1)
            pool.wait_ge(s_tsb, 2)
            for q in range(16):
                if q >= 2:
                    pool.wait_ge(s_op, q - 1)
                g.tensor_tensor(vexp[q % 2], gsm[0:64, 0:2, :].rearrange("p a b -> p (a b)").unsqueeze(1).broadcast_to([64, 4, P]),
                                ident[0:64, 4 * q:4 * q + 4].unsqueeze(2).broadcast_to([64, 4, P]), ALU.mult).then_inc(s_vx, 1)

        @block.tensor
        def _(pe):
            te = nc.tensor
            pe.wait_ge(consts, N_CONST)
            pe.wait_ge(par_in, 48)
            te.transpose(mb[0][:, 0:113], par[0:113, :], ident[0:113, 0:113]).then_inc(parT_ps, 1)
            pe.wait_ge(st_in, 16)
            for c in range(24):
                m = te.transpose(mb[2 + c // 12][:, 24 * (c % 12):24 * (c % 12) + 24], st_nat[:, c * P:c * P + P],
                                 ident[0:24, 0:24])
            m.then_inc(parT_ps, 1)
            pe.wait_ge(parT_sb, 3)
            for t in range(5):
                n = TOK[t]
                pe.wait_ge(x_scaled, t + 1)
                for q in range(4):
                    e = 4 * t + q
                    if e >= 4:
                        pe.wait_ge(xT_sb, e - 3)
                    for u in range(4):
                        k = 4 * q + u
                        m = te.transpose(mb[q][:, u * P:u * P + n], x_nat[0:n, t, k * P:k * P + P], ident[0:n, 0:n])
                    m.then_inc(parT_ps, 1)
            pe.wait_ge(xT_sb, 21)
            for t in range(5):
                n = TOK[t]
                for k in range(KT):
                    for e, (xs, ws) in enumerate(((0, 0), (0, 1), (1, 0))):
                        m = te.matmul(mb[0][0:n, 96 * t:96 * t + 96], hT[:, k, xs, tok(t)], wa16[:, ws, k, :],
                                      start=(k == 0 and e == 0), stop=(k == KT - 1 and e == 2))
            m.then_inc(ab_ps, 1)
            pe.wait_ge(ki_done, 5)
            for t in range(5):
                n = TOK[t]
                m = te.transpose(mb[1 + t // 4][:, (t % 4) * P:(t % 4) * P + n], kin[0:n, t, :, :].rearrange("p a b -> p (a b)"),
                                 ident[0:n, 0:n])
            m.then_inc(kiT_ps, 1)

            def project_step(pair, slot, rhs, k, k0=0, kn=KT):
                for ws, xs in ((0, 0), (0, 1), (1, 0)):
                    for half in range(2):
                        m = te.matmul(pj[pair][:, half, 0:HALF], wsp[:, slot, ws, k0 + k, :],
                                      rhs[:, k, xs, half * HALF:half * HALF + HALF],
                                      start=(k == 0 and ws + xs == 0), stop=(k == kn - 1 and ws == 1))
                if k == kn - 1:
                    m.then_inc(proj_done, 1)

            def project(pair, slot, rhs, k0=0, kn=KT):
                for k in range(kn):
                    project_step(pair, slot, rhs, k, k0, kn)

            gate_step = [0]

            def gate_part(n):
                for x in range(n):
                    f, k = divmod(gate_step[0], KT)
                    gate_step[0] += 1
                    if k == 0:
                        pe.wait_ge(w_lo, gate_group(f) + 1)
                        pe.wait_ge(proj_evac, gate_group(f))
                    project_step(1, f % 2, hT, k)

            def tiles_b(i, first):
                for u in range(4):
                    pe.wait_ge(w_lo, 4 * i + (u + 1))
                    if not (first and u < 2):
                        pe.wait_ge(proj_evac, 4 * i + (u - 1))
                    project(u % 2, u % 2, hT)
            tiles_b(0, True)
            with pe.Fori(1, 5) as i:
                tiles_b(i, False)

            pe.wait_ge(proj_evac, 20)
            pe.wait_ge(kiT_sb, 2)
            for t in range(5):
                n = TOK[t]
                if t >= 2:
                    pe.wait_ge(kv_sb, t - 1)
                for c in range(4):
                    m = te.transpose(mb[t % 2][0:n, c * P:c * P + P], UA[:, U_K + c, tok(t)], ident[:, :])
                m.then_inc(kv_ps, 1)
            te.matmul(mb[2][:, 0:64], swap[:, :], UA[:, U_QI:U_QI + 8, NP:T], start=True, stop=True).then_inc(q_swap, 1)
            pe.wait_ge(w_x, 1)
            te.matmul(mb[3][:, 0:P], ones[0:NS, :], xw[:, :, :], start=True, stop=True).then_inc(q_swap, 1)
            pe.wait_ge(qw_done, 2)
            pe.wait_ge(kv_sb, 5)
            for n in range(48):
                t, hh = n // 16 + 1, n % 16
                if n >= 4:
                    pe.wait_ge(idx_relu, n - 3)
                lo = 64 * (hh % 2)
                te.matmul(mb[n % 4][:, 0:P * (t + 1)], UA[lo:lo + 64, U_QI + hh // 2, tok(t)],
                          kIT[lo:lo + 64, 0:P * (t + 1)], start=True, stop=True).then_inc(idx_ps, 1)
            pe.wait_ge(idx_relu, 48)

            def kidx_T(b):
                pe.wait_ge(kraw_in[b % 2], 256 * (b // 2 + 1))
                for q in range(4):
                    if b:
                        pe.wait_ge(kp_sb, 4 * (b - 1) + q + 1)
                    for u in range(4):
                        m = te.transpose(mb[q][:, u * P:u * P + P], kraw[b % 2][:, 4 * q + u, :], ident[:, :])
                    m.then_inc(kp_ps, 1)
                    if b:
                        gate_part(2)

            def kidx_score(b):
                pe.wait_ge(kp_sb, 4 * (b + 1))
                if b >= 2:
                    pe.wait_ge(ks_sum, b - 1)
                for c in range(16):
                    m = te.matmul(pj[0][:, b % 2, 32 * c:32 * c + 32], kTp[b % 2][:, c, :], qblk[:, b, :],
                                  start=True, stop=True)
                m.then_inc(ks_ps, 1)
            kidx_T(0)
            for b in range(NS):
                if b + 1 < NS:
                    kidx_T(b + 1)
                kidx_score(b)
                gate_part(8 if b + 1 < NS else 16)
            pe.wait_ge(proj_evac, G_C)
            for b in range(NS):
                m = te.matmul(pj[1][:, 0, 16 * b:16 * b + 16], kIT[0:64, NP + b:NP + b + 1].broadcast_to([64, P]),
                              qblk[0:64, b, 0:16], start=True, stop=True)
            m.then_inc(ks_ps, 1)
            pe.wait_ge(ks_sum, NS + 1)

            def count(v):
                pe.wait_ge(cnt_part, v)
                te.matmul(mb[0][:, 0:NS], ones[:, :], srt[:, 0, :], start=True, stop=True).then_inc(cnt_all, 1)
            count(1)
            with pe.Fori(0, 8) as i:
                for u in range(4):
                    pe.wait_ge(w_lo, 4 * i + (G_C + u + 1))
                    pe.wait_ge(proj_evac, 4 * i + (G_C + u - 1))
                    project(u % 2, u % 2, hT)
                    count(4 * i + (u + 2))

            srt_pair = t1[:, 0:NS * 17]
            pe.wait_ge(rank_in, 1)
            te.matmul(mb[0][:, 0:NS], ones[:, :], srt[:, 0, :], start=True, stop=True).then_inc(rank_ps, 1)
            pe.wait_ge(rank_in, 2)
            te.matmul(mb[2][:, 0:NS * 17], tri_lt[:, :], srt_pair, start=True, stop=True).then_inc(rank_ps, 1)
            te.matmul(mb[3][:, 0:NS * 17], ones[:, :], srt_pair, start=True, stop=True).then_inc(rank_ps, 1)
            pe.wait_ge(rank_in, 3)
            te.matmul(mb[2][:, 0:NS * 17], tri_lt[:, :], srt_pair, start=True, stop=True).then_inc(rank_ps, 1)
            te.matmul(mb[3][:, 0:NS * 17], ones[:, :], srt_pair, start=True, stop=True).then_inc(rank_ps, 1)
            pe.wait_ge(rank_in, 4)
            te.matmul(mb[0][:, 8:8 + NS], ones[:, :], srt[:, 0, :], start=True, stop=True).then_inc(rank_ps, 1)
            for b in range(NS):
                if b >= 2:
                    pe.wait_ge(row_sb, b - 1)
                for c in range(NPG):
                    e = NPG * b + c
                    pe.wait_ge(hot, e + 1)
                    m = te.matmul(mb[1][0:3, 256 * (b % 2):256 * (b % 2) + 256] if b % 2 == 0 else mb[2][0:3, 0:256],
                                  vals[:, e // 2, e % 2, :], onehot[:, e % 4, :],
                                  start=(c == 0), stop=(c == NPG - 1))
                    m.then_inc(hot_ps, 1)
                pe.wait_ge(row_sb, b + 1)
                for half in range(2):
                    m = te.matmul(mb[3][:, 2 * b + half:2 * b + half + 1], row3[0:3, b % 2, half * P:half * P + P],
                                  coef[:, :], start=True, stop=True)
                m.then_inc(row_ps, 1)
            pe.wait_ge(sel_done, 1)
            pe.wait_ge(masks, 1)
            pe.wait_ge(proj_evac, G_A)

            def logits(n):
                h, t = divmod(n, TT)
                if n >= 2:
                    pe.wait_ge(lg_max, n - 1)
                te.matmul(mb[n % 2][:, 0:P * (t + 1)], UA[:, h, tok(t)], UA[:, U_K + h // GRP, 0:P * (t + 1)],
                          start=True, stop=True).then_inc(lg_ps, 1)

            def probs_T(n):
                pe.wait_ge(p_rdy, n + 1)
                if n >= 2:
                    pe.wait_ge(pt_sb, n - 1)
                for l in range(n % TT + 1):
                    m = te.transpose(mb[2 + n % 2][:, l * P:l * P + P], Lb[:, n % 2, l * P:l * P + P], ident[:, :])
                m.then_inc(pt_ps, 1)

            def probs_v(n):
                h, t = divmod(n, TT)
                pe.wait_ge(pt_sb, n + 1)
                if n >= 2:
                    pe.wait_ge(pv_sb, n - 1)
                c0 = (h // GRP) * HD
                for l in range(t + 1):
                    m = te.matmul(pj[0][:, n % 2, 0:P], vn[:, l, c0:c0 + HD], PTs[:, n % 2, l * P:l * P + P],
                                  start=(l == 0), stop=(l == t))
                m.then_inc(pv_ps, 1)
            NI = AH * TT
            for n in range(NI + 2):
                if n < NI:
                    logits(n)
                    gate_part(1)
                if 1 <= n <= NI:
                    probs_T(n - 1)
                    if n < NI:
                        gate_part(1)
                if n >= 2:
                    probs_v(n - 2)
                if n < NI:
                    gate_part(3 if n == 0 else 2)
            pe.wait_ge(pv_sb, NI)
            pe.wait_ge(proj_evac, G_D)

            for b in range(NS):
                pe.wait_ge(kv_in[b % 3], 32 * (b // 3 + 1))
                if b >= 2:
                    pe.wait_ge(sk_sb, b - 1)
                for n in range(AKV):
                    for half in range(2):
                        m = te.transpose(mb[b % 2][:, n * 256 + half * P:n * 256 + half * P + P],
                                         kv_sel[:, b % 3, half, n * HD:n * HD + HD], ident[:, :])
                m.then_inc(sk_ps, 1)
                pe.wait_ge(sk_sb, b + 1)
                for n in range(AKV):
                    m = te.matmul(pj[1][0:64, 0, 0:257], qm[:, (2 * b + n) * 64:(2 * b + n) * 64 + 64], KTs[:, n, :],
                                  start=(b == 0 and n == 0), stop=(b == NS - 1 and n == AKV - 1))
                m.then_inc(sl_ps, 1)
            pe.wait_ge(s_p, 1)
            te.transpose(mb[2][:, 0:64], Ls[:, 0:P], ident[0:64, 0:64])
            te.transpose(mb[2][:, 64:128], Ls[:, P:2 * P], ident[0:64, 0:64])
            te.matmul(mb[2][:, 128:192], Ls[:, 256:257].broadcast_to([64, P]), ident[0:64, 0:64],
                      start=True, stop=True).then_inc(sp_ps, 1)
            pe.wait_ge(sp_sb, 1)
            for b in range(NS):
                m_ = NS + b
                pe.wait_ge(kv_in[m_ % 3], 32 * (m_ // 3 + 1))
                for n in range(AKV):
                    for half in range(2):
                        c = b * AH + n * GRP
                        m = te.matmul(mb[3][:, c:c + GRP], kv_sel[:, m_ % 3, half, n * HD:n * HD + HD],
                                      PTs_s[:, half, c:c + GRP], start=(half == 0), stop=(half == 1))
                m.then_inc(so_ps, 1)
            pe.wait_ge(so_sb, 1)

            for q in range(6):
                if q >= 2:
                    pe.wait_ge(cv_sb, q - 1)
                for u in range(4):
                    m = te.transpose(mb[q % 2][0:11, u * P:u * P + P], UB[:, U_BQ + 4 * q + u, NP - 3:T], ident[:, :])
                m.then_inc(cv_ps, 1)

            with pe.Fori(0, 2) as i:
                for u in range(4):
                    pe.wait_ge(w_lo, 4 * i + (G_D + u + 1))
                    pe.wait_ge(proj_evac, 4 * i + (G_D + u - 1))
                    project(u % 2, u % 2, hT)
            pe.wait_ge(proj_evac, G_G)

            def head_sums(n):
                pe.wait_ge(nq_sq, n + 1)
                if n >= 2:
                    pe.wait_ge(nq_rt, nq_ln(n - 2))
                for half in range(2):
                    m = te.matmul(pj[n % 2][:, half, 0:HALF], ones[:, :], nrm[n % 4][:, half * HALF:half * HALF + HALF],
                                  start=True, stop=True)
                m.then_inc(nq_ps, 1)
            for n in range(16):
                head_sums(n)
            pe.wait_ge(nq_done, 16)

            pe.wait_ge(dec_v, 1)
            te.matmul(mb[2][:, 0:32], tri_le[:, :], gv[:, 0, 0:32], start=True, stop=True)
            te.matmul(mb[2][:, 32:64], ones[:, :], gv[:, 0, 0:32], start=True, stop=True).then_inc(dec_ps, 1)
            pe.wait_ge(dec_v, 2)

            for h in range(BH):
                for c in range(TT):
                    m = te.matmul(mb[2][:, c * P:c * P + P], gv[:, 0, c * BH + h:c * BH + h + 1].broadcast_to([P, P]),
                                  tri_le[:, :], start=True, stop=True)
                m.then_inc(g_row, 1)
                for c in range(TT):
                    te.transpose(mb[0][:, c * P:c * P + P], UB[:, U_BK + h, tok(c)], ident[:, :])
                    te.transpose(mb[1][:, c * P:c * P + P], UB[:, U_BV + h, tok(c)], ident[:, :])
                    te.matmul(mb[3][:, c * P:c * P + P], UB[:, U_BK + h, tok(c)], UB[:, U_BK + h, tok(c)],
                              start=True, stop=True)
                    m = te.matmul(pj[0][:, 0, c * P:c * P + P], UB[:, U_BQ + h, tok(c)], UB[:, U_BK + h, tok(c)],
                                  start=True, stop=True)
                m.then_inc(g_pre_ps, 1)
                gate_part(5)
                pe.wait_ge(g_n, h + 1)
                for c in range(TT):
                    m = te.transpose(mb[2][:, c * P:c * P + P], Mb[0][:, c, :], ident[:, :])
                m.then_inc(g_tr, 1)
                gate_part(1)
                pe.wait_ge(g_at, h + 1)
                for c in range(TT):
                    m = te.transpose(pj[0][:, 1, c * P:c * P + P], outn[:, c, :], ident[:, :])
                m.then_inc(g_tr, 1)
                pe.wait_ge(g_nt, 2 * h + 1)
                pe.wait_ge(g_y, 7 * h + 1)
                for s in range(1, 7):
                    M, MT = Mb[2 * ((s - 1) % 2)], Mb[2 * ((s - 1) % 2) + 1]
                    M2 = Mb[2 * (s % 2)]
                    if s > 1:
                        pe.wait_ge(g_mt, 5 * h + s - 1)
                    for c in range(TT):
                        m = te.matmul(mb[0][:, c * P:c * P + P], MT[:, c, :], M[:, c, :], start=True, stop=True)
                    m.then_inc(g_sq, 1)
                    if s < 6:
                        for c in range(TT):
                            m = te.matmul(mb[1][:, c * P:c * P + P], M[:, c, :], MT[:, c, :], start=True, stop=True)
                        m.then_inc(g_sq, 1)
                    gate_part(1)
                    pe.wait_ge(g_m, 6 * h + s)
                    pe.wait_ge(g_y, 7 * h + s)
                    for c in range(TT):
                        m = te.matmul(mb[3][:, c * P:c * P + P], M2[:, c, :], Yt[:, c, :], start=True, stop=True)
                    m.then_inc(g_yps, 1)
                    gate_part(1)
                pe.wait_ge(g_nt, 2 * h + 2)
                pe.wait_ge(g_y, 7 * h + 7)
                for c in range(TT):
                    e = TT * h + c
                    if c:
                        pe.wait_ge(c_s, e)
                        te.matmul(mb[0][:, c * P:c * P + P], UB[:, U_BK + h, tok(c)], Sst, start=True, stop=True).then_inc(c_ks, 1)
                    gate_part(1)
                    pe.wait_ge(c_r, e + 1)
                    te.matmul(mb[1][:, c * P:c * P + P], Yt[:, c, :], rr, start=True, stop=True).then_inc(c_vps, 1)
                    gate_part(1)
                    pe.wait_ge(c_vn, e + 1)
                    if e:
                        pe.wait_ge(c_o, e)
                    te.matmul(mb[2][:, c * P:c * P + P], kd[:, c, :], vnew, start=True, stop=True)
                    m = te.matmul(mb[3][:, c * P:c * P + P], atT[:, c, :], vnew, start=True, stop=True)
                    if c:
                        m = te.matmul(pj[0][:, 0, c * P:c * P + P], UB[:, U_BQ + h, tok(c)], Sst, start=True, stop=True)
                    m.then_inc(c_st, 1)
                    gate_part(1)
                pe.wait_ge(c_o, TT * h + TT)
                for c in range(TT):
                    m = te.transpose(mb[2][:, c * P:c * P + P], outn[:, c, :], ident[:, :])
                m.then_inc(g_oT, 1)
                gate_part(2)
                pe.wait_ge(g_out, h + 1)

            pe.wait_ge(s_bc, 1)
            te.matmul(mb[0][:, 0:64], ones[0:NS, :], gsm[0:NS, 2, :], start=True, stop=True)
            te.matmul(mb[0][:, 64:128], ones[0:NS, :], gsm[0:NS, 3, :], start=True, stop=True)
            te.matmul(mb[0][:, 128:192], ones[:, :], gsm[:, 4, :], start=True, stop=True).then_inc(s_bcs, 1)
            for q in range(16):
                pe.wait_ge(S_in[q % 4], 16 * (q // 4 + 1))
                for r in range(4):
                    e = 4 * q + r
                    m = te.matmul(mb[1][:, 2 * e:2 * e + 2], Sld[q % 4][:, r, :], kqs[:, e, :], start=True, stop=True)
                m.then_inc(s_ks, 1)
            pe.wait_ge(s_vn, 1)
            te.transpose(mb[2][0:64, 0:P], gsm[:, 5, :], ident[:, :])
            te.transpose(mb[2][0:64, P:2 * P], gsm[:, 6, :], ident[:, :]).then_inc(s_tps, 1)
            pe.wait_ge(s_tsb, 2)
            for q in range(16):
                pe.wait_ge(s_vx, q + 1)
                if q >= 2:
                    pe.wait_ge(s_new, q - 1)
                te.matmul(mb[2 + q % 2][:, :], kns, vexp[q % 2].rearrange("p r n -> p (r n)"),
                          start=True, stop=True).then_inc(s_op, 1)
            pe.wait_ge(s_new, 16)
            for n in range(16, 24):
                head_sums(n)
            pe.wait_ge(gated, 16)

            def merge(i, first):
                for j in range(4):
                    before = not (first and j == 0)
                    pe.wait_ge(w_lo, 4 * i + (G_E + j + 1))
                    if before:
                        pe.wait_ge(y_evac, 8 * i + (2 * j - 1))
                    project(0, j % 2, UA16, 0, 8)
                    if before:
                        pe.wait_ge(y_evac, 8 * i + 2 * j)
                    project(1, j % 2, UBq16, 8, 8)
            merge(0, True)
            with pe.Fori(1, 4) as i:
                merge(i, False)

            pe.wait_ge(y_evac, 32)

            def out_T(i, j, first):
                pe.wait_ge(proj_evac, 4 * i + (93 + j))
                if not (first and j < 2):
                    pe.wait_ge(oT_sb, 4 * i + (j - 1))
                for t in range(TT):
                    te.transpose(mb[j % 2][:, t * P:t * P + P], oT[j % 2][:, tok(t)], ident[:, :])
                te.transpose(mb[2 + j % 2][0:NS, 0:P], oT[j % 2][:, NP:T], ident[:, :]).then_inc(oT_ps, 1)

            def out_tiles(i, first):
                for u in range(4):
                    pe.wait_ge(w_lo, 4 * i + (L_F + u + 1))
                    if not (first and u < 2):
                        pe.wait_ge(proj_evac, 4 * i + (92 + u - 1))
                    project(u % 2, u % 2, mT16)
                    if not (first and u == 0):
                        if u:
                            out_T(i, u - 1, first)
                        else:
                            out_T(i - 1, 3, False)
            out_tiles(0, True)
            with pe.Fori(1, 4) as i:
                out_tiles(i, False)
            out_T(3, 3, False)


        @block.scalar
        def _(act):
            sc = nc.scalar
            link = linker(act, act_c)
            act.dma_start(idxg, idx_k_norm[0:1, :].broadcast_to([P, ID])).then_inc(row_in, 16)
            act.dma_start(alog, a_log[0:1, :].broadcast_to([P, BH])).then_inc(row_in, 16)
            act.dma_start(dtb, dt_bias[0:1, :].broadcast_to([P, BH])).then_inc(row_in, 16)
            act.dma_start(pt_i[:, :], page_table.rearrange("(a b) n -> a (b n)", a=1).broadcast_to([P, NS * NPG])).then_inc(row_in, 16)
            act.wait_ge(consts, N_CONST)
            for t in range(5):
                n = TOK[t]
                act.wait_ge(x_in[t], 16)
                if t:
                    act.wait_ge(sq_done, t)
                sc.activation(junk[0:n, :], x_nat[0:n, t, :], ACT.Square, accum_out=ssq[0:n, t:t + 1]).then_inc(sq_done, 1)
            act.wait_ge(mean_sq, 1)
            sc.activation(rs_x, rs_x, ACT.Sqrt).then_inc(rms, 1)

            def hi(slot, arrived, freed, i=None):
                act.wait_ge(w_in_s[slot], arrived)
                if freed is not None:
                    act.wait_ge(proj_done, freed)
                sc.activation(wsp[:, slot, 0, :, :].rearrange("p k n -> p (k n)"), raw[:, slot, :, :].rearrange("p k n -> p (k n)"),
                              ACT.Copy, scale=W_SC).then_inc(w_hi, 1)
            hi(0, 16, None)
            hi(1, 16, None)
            act.wait_ge(wa_in, 32)
            sc.activation(wa16[:, 0, :, :].rearrange("p k n -> p (k n)"), wa.rearrange("p k n -> p (k n)"), ACT.Copy,
                          scale=W_SC).then_inc(x_hi, 1)
            for e in range(20):
                t, q = divmod(e, 4)
                n = TOK[t]
                act.wait_ge(x_tmp, e + 1)
                sc.activation(hT[:, 4 * q:4 * q + 4, 0, tok(t)], xtmp[:, e % 2, :, 0:n], ACT.Copy).then_inc(x_hi, 1)
            act.wait_ge(mean_sq, 2)
            sc.activation(ki_r, ki_s, ACT.Sqrt).then_inc(rms, 1)
            act.wait_ge(kiT_ps, 1)
            sc.activation(kIT[:, 0:NP], mb[1][:, :], ACT.Copy).then_inc(kiT_sb, 1)
            sc.activation(kIT[:, NP:T], mb[2][:, 0:NS], ACT.Copy).then_inc(kiT_sb, 1)

            def evac(dst, pair, done, func=ACT.Copy):
                act.wait_ge(proj_done, done)
                sc.activation(dst.rearrange("p (h n) -> p h n", h=2), pj[pair][:, :, 0:HALF], func, scale=UNSC).then_inc(proj_evac, 1)

            def gate_out_tile(f, place, before=2):
                x = f - before
                if x >= 0:
                    act.wait_ge(gate_out[x % 2], 16 * (x // 2 + 1))
                done = gate_group(f) + 1
                evac(place, 1, done)
                hi(f % 2, 16 * ((done + 1) // 2 + 1) + (16 if f >= 30 else 0), done)
                act.wait_ge(proj_evac, done)
                act.dma_start(gate_d[1 - f // 16, f % 16], place).then_inc(gate_out[f % 2], 16)

            def evac_in(U, i, g0, u0):
                for u in range(4):
                    evac(U[:, bass.ds(4 * i + (u0 + u), 1), :].rearrange("p a b -> p (a b)"), u % 2, 4 * i + (g0 + u + 1))
                    hi(u % 2, 32 * i + 16 * ((g0 + u + 2) // 2 + 1), 4 * i + (g0 + u + 1))
            with act.Fori(0, 5) as i:
                evac_in(UA, i, G_B, 0)
            for t in range(5):
                n = TOK[t]
                act.wait_ge(kv_ps, t + 1)
                if t:
                    act.wait_ge(kv_out, 32 * t)
                sc.activation(knat_t[0:n, :], mb[t % 2][0:n, :], ACT.Copy).then_inc(kv_sb, 1)
                act.wait_ge(kv_sb, t + 1)
                if t < TT:
                    link(sc.activation(vn[:, t, :], knat_t[:, 256:512], ACT.Copy))
                    act.dma_start(k_p[0, 0, tok(t)].rearrange("s n d -> s (n d)"), knat_t[:, 0:256]).then_inc(kv_out, 16)
                    act.dma_start(v_p[0, 0, tok(t)].rearrange("s n d -> s (n d)"), knat_t[:, 256:512]).then_inc(kv_out, 16)
                else:
                    act.dma_start(k_s[0].rearrange("b s n d -> (b s) (n d)"), knat_t[0:NS, 0:256]).then_inc(kv_out, 16)
                    act.dma_start(v_s[0].rearrange("b s n d -> (b s) (n d)"), knat_t[0:NS, 256:512]).then_inc(kv_out, 16)
            act.wait_ge(ki_done, 5)
            for t in range(TT):
                act.dma_start(kidx_p[0, 0, tok(t), :], kin[:, t, 0, :]).then_inc(kv_out, 16)
            act.dma_start(kidx_s[0].rearrange("b s d -> (b s) d"), kin[0:NS, TT, 0, :]).then_inc(kv_out, 16)
            for n in range(48):
                L = P * (n // 16 + 2)
                act.wait_ge(idx_ps, n + 1)
                if n >= 4:
                    act.wait_ge(idx_acc, n - 3)
                sc.activation(rel[:, n % 4, 0:L], mb[n % 4][:, 0:L], ACT.Relu).then_inc(idx_relu, 1)
            for b in range(NS):
                if b >= 2:
                    act.wait_ge(ks_ps, b - 1)
                for q in range(4):
                    act.wait_ge(kp_ps, 4 * b + q + 1)
                    sc.activation(kTp[b % 2][:, 4 * q:4 * q + 4, :].rearrange("p a b -> p (a b)"), mb[q][:, :],
                                  ACT.Copy).then_inc(kp_sb, 1)
                if b:
                    gate_out_tile(b - 1, gate_e[(b - 1) % 2])
            gate_out_tile(7, gate_e[1])
            for r in range(2):
                act.wait_ge(gate_out[r], 16 * 4)
            act.wait_ge(kv_out, 32 * 5 + 16 * 5)
            with act.Fori(0, 8) as i:
                evac_in(UB, i, G_C, 0)
            for b in range(NS):
                act.wait_ge(hot_ps, NPG * (b + 1))
                if b >= 2:
                    act.wait_ge(row_ps, b - 1)
                sc.activation(row3[:, b % 2, :], mb[1][0:3, 0:256] if b % 2 == 0 else mb[2][0:3, 0:256],
                              ACT.Copy).then_inc(row_sb, 1)
            NI = AH * TT
            for n in range(NI + 1):
                if n < NI:
                    L = P * (n % TT + 1)
                    act.wait_ge(lg_max, n + 1)
                    sc.activation(Lb[:, n % 2, 0:L], Lb[:, n % 2, 0:L], ACT.Exp, bias=nm[:, n % 2:n % 2 + 1], scale=A_SCALE,
                                  accum_out=sm[:, n % 2:n % 2 + 1]).then_inc(p_exp, 1)
                if n >= 1:
                    m = n - 1
                    L = P * (m % TT + 1)
                    act.wait_ge(pt_ps, m + 1)
                    if m >= 2:
                        act.wait_ge(pv_ps, m - 1)
                    sc.activation(PTs[:, m % 2, 0:L], mb[2 + m % 2][:, 0:L], ACT.Copy).then_inc(pt_sb, 1)
                if n < NI and n % TT == 3:
                    gate_out_tile(8 + n // TT, gate[0], 1)
            for b in range(NS):
                act.wait_ge(sk_ps, b + 1)
                if b:
                    act.wait_ge(sl_ps, b)
                link(sc.activation(KTs[:, :, 0:256], mb[b % 2][:, :].rearrange("p (n c) -> p n c", n=2), ACT.Copy))
                sc.activation(KTs[:, :, 256:257], UA[:, U_K:U_K + 2, NP + b:NP + b + 1], ACT.Copy).then_inc(sk_sb, 1)
            act.wait_ge(s_max, 1)
            sc.activation(Ls, Ls, ACT.Exp, bias=cols[0:64, 16:17], scale=A_SCALE, accum_out=cols[0:64, 17:18]).then_inc(s_exp, 1)
            act.wait_ge(sp_ps, 1)
            link(sc.activation(tmpS, mb[2][:, 128:192], ACT.Copy))
            sc.activation(PTs_s.rearrange("p h c -> p (h c)"), mb[2][:, 0:128], ACT.Copy).then_inc(sp_sb, 1)
            act.wait_ge(so_sb, 1)
            for q in range(6):
                act.wait_ge(cv_ps, q + 1)
                if q == 4:
                    act.wait_ge(cv_out, 16 + 32 * 4)
                win = R2[0:11, 512 * (q % 4):512 * (q % 4) + 512]
                sc.activation(win, mb[q % 2][0:11, :], ACT.Copy).then_inc(cv_sb, 1)
                act.wait_ge(cv_sb, q + 1)
                act.dma_start(conv_p[0, 0, :, 512 * q:512 * q + 512], win[0:3, :]).then_inc(cv_out, 16)
                act.dma_start(conv_s[0, :, 2, 512 * q:512 * q + 512], win[3:11, :]).then_inc(cv_out, 16)
            for g_ in range(8):
                evac(UA[:, U_QI + g_, :], g_ % 2, G_D + g_ + 1)
                hi(g_ % 2, 16 * ((G_D + g_ + 2) // 2 + 1), G_D + g_ + 1)
                for c in range(3 * g_, 3 * g_ + 3):
                    act.wait_ge(cv_acc, c + 1)
                    sc.activation(UB[:, U_BQ + c, :], cvt[c % 2], ACT.Silu).then_inc(cv_silu, 1)
            act.wait_ge(cv_silu, 24)
            act.wait_ge(cv_out, 16 + 32 * 6)

            def norms(n0, n1):
                for b in range(n0, n1, 4):
                    for n in range(b, b + 4):
                        if n >= 4:
                            act.wait_ge(nq_done, n - 3)
                        sc.activation(nrm[n % 4], UB[:, U_BQ + n % 16, :], ACT.Square).then_inc(nq_sq, 1)
                    for n in range(b, b + 4):
                        act.wait_ge(nq_ps, n + 1)
                        sc.activation(nrm[n % 4].rearrange("p (h n) -> p h n", h=2), pj[n % 2][:, :, 0:HALF], ACT.Ln, bias=eps_c,
                                      scale=1.0 if n < 16 else 1.0 / HD).then_inc(nq_rt, 1)
                    act.wait_ge(nq_rt, nq_ln(b + 3))
                    for n in range(b, b + 4):
                        sc.activation(nrm[n % 4], nrm[n % 4], ACT.Exp, scale=-0.5).then_inc(nq_rt, 1)
            norms(0, 16)
            act.wait_ge(dec_a, 1)
            link(sc.activation(gv[:, 1, :], gv[:, 1, :], ACT.Exp, scale=-1.0))
            link(sc.activation(gv[:, 1, :], gv[:, 1, :], ACT.Ln, bias=1.0))
            link(sc.activation(alog, alog, ACT.Exp))
            sc.activation(gv[:, 2, :].rearrange("p (t h) -> p t h", t=5), ab[:, :, 88:96], ACT.Sigmoid).then_inc(dec_e, 1)
            act.wait_ge(dec_a, 2)
            link(sc.activation(gv[:, 4, 0:32], gv[:, 3, 0:32], ACT.Exp))
            link(sc.activation(gv[:, 5, 0:32], gv[:, 5, 0:32], ACT.Exp))
            sc.activation(gv[:, 6, 0:32], gv[:, 6, 0:32], ACT.Exp).then_inc(dec_e, 1)
            for h in range(BH):
                act.wait_ge(g_nt_in, h + 1)
                sc.activation(Di, Di, ACT.Exp, scale=-1.0).then_inc(g_exp, 1)
                act.wait_ge(g_y, 7 * h + 1)
                sc.activation(Mb[1], mb[2][:, :].rearrange("p (c n) -> p c n", c=4), ACT.Copy).then_inc(g_nt, 1)
                act.wait_ge(g_tr, 2 * h + 2)
                sc.activation(atT, pj[0][:, 1, :].rearrange("p (c n) -> p c n", c=4), ACT.Copy).then_inc(g_nt, 1)
                for s in range(1, 6):
                    act.wait_ge(g_sq, 11 * h + 2 * s)
                    act.wait_ge(g_m, 6 * h + s)
                    sc.activation(Mb[2 * (s % 2) + 1], mb[1][:, :].rearrange("p (c n) -> p c n", c=4),
                                  ACT.Copy).then_inc(g_mt, 1)
                gate_out_tile(16 + 2 * h, gate[0], 2 if h else 1)
                for c in range(TT):
                    act.wait_ge(c_vps, TT * h + c + 1)
                    sc.activation(vnew, mb[1][:, c * P:c * P + P], ACT.Copy).then_inc(c_vn, 1)
                act.wait_ge(g_oT, h + 1)
                sc.activation(UB[:, U_BQ + h, 0:NP], mb[2][:, :], ACT.Copy).then_inc(g_out, 1)
                act.wait_ge(c_s, TT * h + TT)
                act.dma_start(ssm_p[0, 0, h], Sst).then_inc(ssm_out, 16)
                gate_out_tile(16 + 2 * h + 1, gate[1])
            act.wait_ge(ssm_out, 16 * BH)
            def load_S(q, n):
                h, b0 = q // 2, 4 * (q % 2)
                act.dma_start(Sld[n % 4], state_ssm[0, b0:b0 + 4, h].rearrange("b k v -> k b v")).then_inc(S_in[n % 4], 16)
            for q in range(16):
                if q >= 4:
                    act.wait_ge(s_ks, q - 3)
                load_S(q, q)
            act.wait_ge(s_bcs, 1)
            sc.activation(gsm[:, 7, :], mb[0][:, 0:64], ACT.Exp).then_inc(s_kq, 1)
            act.wait_ge(s_tps, 1)
            sc.activation(kns, mb[2][0:64, 0:P], ACT.Copy).then_inc(s_tsb, 1)
            sc.activation(gsm[0:64, 0:2, :].rearrange("p a b -> p (a b)"), mb[2][0:64, P:2 * P], ACT.Copy).then_inc(s_tsb, 1)
            for q in range(16 + 2):
                if q < 16:
                    if q >= 4:
                        act.wait_ge(S_out[q % 4], 16 * (q // 4))
                    else:
                        act.wait_ge(s_ks, 16)
                    load_S(q, q)
                if q >= 2:
                    m = q - 2
                    h, b0 = m // 2, 4 * (m % 2)
                    act.wait_ge(s_new, m + 1)
                    act.dma_start(ssm_s[0, b0:b0 + 4, h].rearrange("b k v -> k b v"), Sld[m % 4]).then_inc(S_out[m % 4], 16)
            for r in range(4):
                act.wait_ge(S_out[r], 16 * 4)
            norms(16, 24)
            for c in range(16):
                z = UB[:, c, :] if c < 8 else UA[:, U_QI + c - 8, :]
                sc.activation(z, z, ACT.Silu).then_inc(z_silu, 1)
            act.wait_ge(gated, 16)

            W0 = 16 * (G_E // 2)
            def merge(i, last):
                for j in range(4):
                    act.wait_ge(gate_in[j % 2], 64 * i + 32 * (j // 2 + 1))
                    for g_ in (gate, gate_m):
                        sc.activation(g_[j % 2], g_[j % 2], ACT.Sigmoid).then_inc(gate_sig, 1)
                    hi(j % 2, 64 * i + (W0 + 32 * ((j + 2) // 2 + 1) - (16 if last and j >= 2 else 0)), 8 * i + (G_E + 2 * j + 2))
            with act.Fori(0, 3) as i:
                merge(i, False)
            merge(3, True)
            W_F = W0 + 32 * 8

            def outs(i, first, last):
                for u in range(4):
                    if not (first and u < 2):
                        act.wait_ge(oT_ps, 4 * i + (u - 1))
                    evac(oT[u % 2], u % 2, 4 * i + (G_F + u + 1))
                    if not (last and u >= 2):
                        hi(u % 2, 32 * i + (W_F + 16 * ((u + 2) // 2 + 1)), 4 * i + (G_F + u + 1))
            outs(0, True, False)
            with act.Fori(1, 3) as i:
                outs(i, False, False)
            outs(3, False, True)
            act.wait_ge(oT_sb, 16)
            act.wait_ge(x_back, 96)
            for t in range(5):
                n = TOK[t]
                if t:
                    act.wait_ge(sq_done, 5 + t)
                sc.activation(osq[0:n, :], Yo[0:n, t, :], ACT.Square, accum_out=ssq[0:n, t:t + 1]).then_inc(sq_done, 1)
            act.wait_ge(mean_sq, 3)
            sc.activation(rs_x, rs_x, ACT.Sqrt).then_inc(rms, 1)

        @block.vector
        def _(dve):
            ve = nc.vector
            link = linker(dve, dve_c)
            dve.wait_ge(consts, N_CONST)
            dve.wait_ge(row_in, 64)
            ptv = pt_i[:, :].rearrange("p (c s) -> p c s", s=2)
            ve.tensor_copy(pg_i[0:64, :], ptv[0:64, :, 0])
            link(ve.tensor_copy(pg_i[64:128, :], ptv[64:128, :, 1]))
            ve.tensor_scalar(off_i[:, :], pg_i[:, :], 64.0, pm64, ALU.mult, ALU.add).then_inc(off_done, 1)
            dve.wait_ge(parT_ps, 1)
            link(ve.tensor_copy(parT[:, :], mb[0][:, 0:113]))
            ve.tensor_scalar(g_pre, g_pre, X_SC, None, ALU.mult).then_inc(parT_sb, 1)

            def lo(slot, n):
                dve.wait_ge(w_hi, n)
                ve.scalar_tensor_tensor(out=wsp[:, slot, 1, :, :].rearrange("p k n -> p (k n)"),
                                        in0=raw[:, slot, :, :].rearrange("p k n -> p (k n)"), scalar=W_SC,
                                        in1=wsp[:, slot, 0, :, :].rearrange("p k n -> p (k n)"),
                                        op0=ALU.mult, op1=ALU.subtract).then_inc(w_lo, 1)
            dve.wait_ge(parT_ps, 2)
            for c in range(2):
                ve.tensor_copy(stT[:, 12 * c:12 * c + 12, :].rearrange("p a b -> p (a b)"), mb[2 + c][:, 0:288]).then_inc(parT_sb, 1)
            dve.wait_ge(sq_done, 5)
            ve.tensor_scalar(rs_x, ssq, 1.0 / D, EPS, ALU.mult, ALU.add).then_inc(mean_sq, 1)
            dve.wait_ge(rms, 1)
            link(ve.reciprocal(rs_x, rs_x))
            for t in range(5):
                n = TOK[t]
                ve.tensor_scalar(x_nat[0:n, t, :], x_nat[0:n, t, :], rs_x[0:n, t:t + 1], None, ALU.mult).then_inc(x_scaled, 1)
            dve.wait_ge(parT_sb, 3)

            def x_lo(e):
                t, q = divmod(e, 4)
                n = TOK[t]
                dve.wait_ge(x_hi, e + 2)
                ve.tensor_tensor(hT[:, 4 * q:4 * q + 4, 1, tok(t)], xtmp[:, e % 2, :, 0:n], hT[:, 4 * q:4 * q + 4, 0, tok(t)],
                                 ALU.subtract).then_inc(xT_sb, 1)
            for t in range(5):
                n = TOK[t]
                for q in range(4):
                    dve.wait_ge(parT_ps, 4 * t + q + 3)
                    e = 4 * t + q
                    if e >= 2:
                        dve.wait_ge(xT_sb, e - 1)
                    ve.tensor_tensor(xtmp[:, e % 2, :, 0:n], mb[q][:, :].rearrange("p (a b) -> p a b", a=4)[:, :, 0:n],
                                     g_pre[:, 4 * q:4 * q + 4].unsqueeze(2).broadcast_to([P, 4, n]), ALU.mult).then_inc(x_tmp, 1)
                    if e:
                        x_lo(e - 1)
            x_lo(19)
            lo(0, 1)
            lo(1, 2)
            dve.wait_ge(x_hi, 1)
            ve.scalar_tensor_tensor(out=wa16[:, 1, :, :].rearrange("p k n -> p (k n)"), in0=wa.rearrange("p k n -> p (k n)"),
                                    scalar=W_SC, in1=wa16[:, 0, :, :].rearrange("p k n -> p (k n)"),
                                    op0=ALU.mult, op1=ALU.subtract).then_inc(xT_sb, 1)
            dve.wait_ge(ab_ps, 1)
            ve.tensor_scalar(ab[:, 0:4, :].rearrange("p a b -> p (a b)"), mb[0][:, 0:384], UNSC, None, ALU.mult)
            link(ve.tensor_scalar(ab[0:NS, 4, :], mb[0][0:NS, 384:480], UNSC, None, ALU.mult))
            jk = junk[:, 0:5 * ID].rearrange("p (t d) -> p t d", t=5)
            link(ve.tensor_tensor(jk, ab[:, :, 0:ID], ab[:, :, 0:ID], ALU.mult))
            link(ve.tensor_reduce(ki_s, jk, AX, ALU.add))
            ve.tensor_scalar(ki_s, ki_s, 1.0 / ID, EPS, ALU.mult, ALU.add).then_inc(mean_sq, 1)
            dve.wait_ge(rms, 2)
            dve.wait_ge(row_in, 64)
            link(ve.reciprocal(ki_r, ki_r))
            for t in range(5):
                ve.tensor_scalar(kin[:, t, 1, :], ab[:, t, 0:ID], ki_r[:, t:t + 1], None, ALU.mult)
            link(ve.tensor_scalar(ab[:, :, 64:80], ab[:, :, 64:80], I_SCALE, None, ALU.mult))
            for t in range(5):
                ve.tensor_tensor(kin[:, t, 0, :], kin[:, t, 1, :], idxg, ALU.mult)
            link(ve.memset(cols[:, 60:62], 0.0))
            for t in range(5):
                ve.tensor_copy(kin[:, t, 1, :], kin[:, t, 0, :]).then_inc(ki_done, 1)
            for b in range(NS):
                m = ve.tensor_scalar(xw[:, b, :].rearrange("p (e m) -> p e m", e=2), ab[0:NS, 4, 64:80].rearrange("p (m e) -> p e m", e=2),
                                     ident[0:NS, b:b + 1], None, ALU.mult)
            m.then_inc(w_x, 1)

            with dve.Fori(0, 5) as i:
                for u in range(4):
                    lo(u % 2, 4 * i + (u + 3))
            dve.wait_ge(q_swap, 1)
            qs = UA[:, U_QI:U_QI + 8, NP:T].rearrange("p m b -> p b m")
            qw = mb[2][:, 0:64].rearrange("p (m b) -> p b m", b=NS)
            ve.tensor_copy(qblk[0:64, :, 0:8], qs[0:64])
            ve.tensor_copy(qblk[0:64, :, 8:16], qw[0:64])
            ve.tensor_copy(qblk[64:128, :, 16:24], qw[64:128])
            ve.tensor_copy(qblk[64:128, :, 24:32], qs[64:128]).then_inc(qw_done, 1)
            dve.wait_ge(q_swap, 2)
            ve.tensor_copy(wbc[:, :, :].rearrange("p b h -> p (b h)"), mb[3][:, 0:P]).then_inc(qw_done, 1)
            qmd = qm[:, :].rearrange("p (c x) -> p c x", x=68)
            for b in range(NS):
                for n in range(AKV):
                    ve.tensor_copy(qmd[:, 2 * b + n, 0:GRP], UA[:, n * GRP:n * GRP + GRP, NP + b])

            for n in range(48):
                t, hh = n // 16 + 1, n % 16
                L = P * (t + 1)
                dve.wait_ge(idx_relu, n + 1)
                w = ab[:, t, 64 + hh:65 + hh]
                if hh == 0:
                    ve.tensor_scalar(idx[:, t, 0:L], rel[:, n % 4, 0:L], w, None, ALU.mult).then_inc(idx_acc, 1)
                else:
                    dve.wait_ge(idx_acc, n)
                    ve.scalar_tensor_tensor(out=idx[:, t, 0:L], in0=rel[:, n % 4, 0:L], scalar=w, in1=idx[:, t, 0:L],
                                            op0=ALU.mult, op1=ALU.add).then_inc(idx_acc, 1)
            for b in range(NS + 1):
                dve.wait_ge(ks_ps, b + 1)
                if b < NS:
                    link(ve.scalar_tensor_tensor(out=wsum.rearrange("p (c h) -> p c h", h=IH),
                                                 in0=pj[0][:, b % 2, :].rearrange("p (c h) -> p c h", h=IH), scalar=0.0,
                                                 in1=wbc[:, b, :].unsqueeze(1).broadcast_to([P, NPG, IH]),
                                                 op0=ALU.max, op1=ALU.mult))
                    ve.tensor_reduce(Y[:, b, 0:NPG], wsum.rearrange("p (c h) -> p c h", h=IH), AX, ALU.add).then_inc(ks_sum, 1)
                    dve.wait_ge(ks_sum, b + 1)
                    lo(b % 2, G_H + b + 3)
                else:
                    link(ve.scalar_tensor_tensor(out=wsum[:, 0:P].rearrange("p (b h) -> p b h", h=IH),
                                                 in0=pj[1][:, 0, 0:P].rearrange("p (b h) -> p b h", h=IH), scalar=0.0,
                                                 in1=wbc[:, :, :], op0=ALU.max, op1=ALU.mult))
                    ve.tensor_reduce(Y[0:1, :, NPG], wsum[0:1, 0:P].rearrange("p (b h) -> p b h", h=IH), AX, ALU.add).then_inc(ks_sum, 1)
                    dve.wait_ge(ks_sum, NS + 1)

            hi_i = ge[:, 0:P].bitcast(I32)
            lo_i = ge[:, P:2 * P].bitcast(I32)
            ve.tensor_scalar(hi_i, pg_i[:, :], 4, None, ALU.logical_shift_right)
            link(ve.tensor_scalar(lo_i, pg_i[:, :], 15, None, ALU.bitwise_and))
            for par_ in range(2):
                ve.tensor_copy(vals[:, :, par_, 1], hi_i)
                ve.tensor_copy(vals[:, :, par_, 2], lo_i)
                ve.tensor_scalar(t1[:, par_:par_ + 1], pm64, 2.0, float(par_), ALU.mult, ALU.add)
            link(ve.memset(t1[:, 2:2 + P], 0.0))
            for par_ in range(2):
                link(ve.tensor_scalar(vals[:, :, par_, 0], t1[:, 2:2 + P], t1[:, par_:par_ + 1], None, ALU.add))

            Yf = Y[:, :, :]
            ge3 = ge[:, :].rearrange("p (b c) -> p b c", b=NS)
            part, sgn, thr, dif, thm, fac, need, cgt = (srt[:, r, :] for r in range(8))
            link(ve.memset(thr_i[:, :], 0))
            link(ve.tensor_scalar(ge3, Yf, 0.0, None, ALU.is_ge))
            ve.tensor_reduce(part, ge3, AX, ALU.add).then_inc(cnt_part, 1)
            dve.wait_ge(cnt_all, 1)
            link(ve.tensor_scalar(sgn, mb[0][:, 0:NS], SEL_S - 0.5, None, ALU.is_gt))
            link(ve.tensor_scalar(sgn, sgn, 2.0, -1.0, ALU.mult, ALU.add))
            for t in range(1, TT):
                dve.wait_ge(idx_mask, t)
            with dve.Fori(0, 8) as i:
                for u in range(4):
                    s = 6 * (4 * i + u)
                    ve.tensor_tensor(cand_i[:, :], thr_i[:, :], bit_i[:, bass.ds(4 * i + u, 1)].broadcast_to([P, NS]),
                                     ALU.bitwise_or).then_inc(srch, 1)
                    dve.wait_ge(srch, s + 1)
                    ve.tensor_tensor(thr, cand_i[:, :].bitcast(F32), sgn, ALU.mult).then_inc(srch, 1)
                    dve.wait_ge(srch, s + 2)
                    ve.tensor_tensor(ge3, Yf, thr.unsqueeze(2).broadcast_to([P, NS, NPG + 1]), ALU.is_ge).then_inc(srch, 1)
                    dve.wait_ge(srch, s + 3)
                    ve.tensor_reduce(part, ge3, AX, ALU.add).then_inc(cnt_part, 1)
                    if u % 2 == 0:
                        for t in range(1, TT):
                            e = 6 * (2 * i + u // 2) + 2 * (t - 1)
                            L = P * (t + 1)
                            ve.max(top8[:, t, :], idx[:, t, 0:L]).then_inc(topk, 1)
                            dve.wait_ge(topk, e + 1)
                            dve.sem_inc(waited, 1)
                            ve.match_replace(out=idx[:, t, 0:L], in_to_replace=top8[:, t, :], in_values=idx[:, t, 0:L],
                                             imm_value=TAKEN).then_inc(topk, 1)
                            dve.wait_ge(topk, e + 2)
                            dve.sem_inc(waited, 1)
                    dve.wait_ge(cnt_all, 4 * i + (u + 2))
                    ve.scalar_tensor_tensor(out=dif, in0=mb[0][:, 0:NS], scalar=SEL_S - 0.5, in1=sgn,
                                            op0=ALU.subtract, op1=ALU.mult).then_inc(srch, 1)
                    dve.wait_ge(srch, s + 4)
                    ve.tensor_scalar(m_i[:, :], dif, 0.0, bit_f[:, bass.ds(4 * i + u, 1)], ALU.is_gt, ALU.mult).then_inc(srch, 1)
                    dve.wait_ge(srch, s + 5)
                    ve.tensor_tensor(thr_i[:, :], thr_i[:, :], m_i[:, :], ALU.bitwise_or).then_inc(srch, 1)
                    dve.wait_ge(srch, s + 6)
                    lo(u % 2, 4 * i + (G_C + u + 3))
            link(ve.tensor_scalar(fac, sgn, 0.0, None, ALU.is_lt))
            link(ve.tensor_scalar(dif, fac, 0.7 * 2.0 ** -23, None, ALU.mult))
            link(ve.tensor_tensor(thm, thr_i[:, :].bitcast(F32), dif, ALU.mult))
            link(ve.tensor_tensor(thm, thm, thr_i[:, :].bitcast(F32), ALU.add))
            link(ve.tensor_scalar(fac, fac, 1.2e-38, None, ALU.mult))
            link(ve.tensor_tensor(thm, thm, fac, ALU.max))
            link(ve.tensor_tensor(thr, thm, sgn, ALU.mult))
            thb = thr.unsqueeze(2).broadcast_to([P, NS, NPG + 1])
            gt3 = wsum_gt[:, :].rearrange("p (b c) -> p b c", b=NS)
            link(ve.tensor_tensor(gt3, Yf, thb, ALU.is_gt))
            ve.tensor_reduce(part, gt3, AX, ALU.add).then_inc(rank_in, 1)
            link(ve.tensor_tensor(ge3, Yf, thb, ALU.is_equal))
            pair = t1[:, 0:NS * 17].rearrange("p (b c) -> p b c", b=NS)

            def pair_sums(src):
                s4 = src[:, :, 0:NPG].rearrange("p b (c s) -> p b c s", s=2)
                link(ve.tensor_copy(pair[:, :, 16:17], src[:, :, NPG:NPG + 1]))
                ve.tensor_tensor(pair[:, :, 0:16], s4[:, :, :, 0], s4[:, :, :, 1], ALU.add).then_inc(rank_in, 1)
            incl = rk[:, 0:NS * 17]
            rank = rk[:, 136:136 + 264].rearrange("p (b c) -> p b c", b=NS)
            rs17 = rk2[:, 0:NS * 17]
            link(ve.memset(rs17, 1.0))
            link(ve.memset(rs17.rearrange("p (b c) -> p b c", b=NS)[:, :, 0:1], 0.0))

            def rank_of(src):
                link(ve.tensor_tensor_scan(incl, rs17, mb[3][:, 0:NS * 17], 0.0, ALU.mult, ALU.add))
                link(ve.tensor_tensor(incl, incl, mb[3][:, 0:NS * 17], ALU.subtract))
                link(ve.tensor_tensor(incl, incl, mb[2][:, 0:NS * 17], ALU.add))
                i3 = incl.rearrange("p (b c) -> p b c", b=NS)
                r4 = rank[:, :, 0:NPG].rearrange("p b (c s) -> p b c s", s=2)
                s4 = src[:, :, 0:NPG].rearrange("p b (c s) -> p b c s", s=2)
                link(ve.tensor_copy(r4[:, :, :, 0], i3[:, :, 0:16]))
                link(ve.tensor_tensor(r4[:, :, :, 1], i3[:, :, 0:16], s4[:, :, :, 0], ALU.add))
                link(ve.tensor_copy(rank[:, :, NPG:NPG + 1], i3[:, :, 16:17]))
            pair_sums(ge3)
            dve.wait_ge(rank_ps, 1)
            link(ve.tensor_scalar(need, mb[0][:, 0:NS], -1.0, float(SEL_S), ALU.mult, ALU.add))
            dve.wait_ge(rank_ps, 3)
            rank_of(ge3)
            link(ve.tensor_tensor(rank, rank, need.unsqueeze(2).broadcast_to([P, NS, NPG + 1]), ALU.is_lt))
            link(ve.tensor_tensor(ge3, ge3, rank, ALU.mult))
            link(ve.tensor_tensor(gt3, gt3, ge3, ALU.add))
            pair_sums(gt3)
            dve.wait_ge(rank_ps, 5)
            rank_of(gt3)
            link(ve.tensor_scalar(rank, rank, 1.0, None, ALU.add))
            link(ve.tensor_tensor(rank, rank, gt3, ALU.mult))
            link(ve.tensor_scalar(pos[:, :].rearrange("p (b c) -> p b c", b=NS), rank, -1.0, None, ALU.add))
            ve.tensor_copy(part, gt3[:, :, NPG]).then_inc(rank_in, 1)
            dve.wait_ge(rank_ps, 6)
            link(ve.tensor_copy(cgt, mb[0][:, 8:8 + NS]))
            for e in range(NS * NPG):
                b, c = divmod(e, NPG)
                if e >= 4:
                    dve.wait_ge(hot_ps, e - 3)
                ve.tensor_scalar(onehot[:, e % 4, :], iota_b[:, :], pos[:, b * (NPG + 1) + c:b * (NPG + 1) + c + 1], None,
                                 ALU.is_equal).then_inc(hot, 1)
            dve.wait_ge(row_ps, NS)
            ve.tensor_copy(sel_i[:, :], mb[3][:, 0:16]).then_inc(sel_done, 1)
            dve.wait_ge(idx_mask, TT)
            for t in range(1, TT):
                L = P * (t + 1)
                m = ve.tensor_scalar(idx[:, t, 0:L], idx[:, t, 0:L], TAKEN, NEG, ALU.not_equal, ALU.mult)
            m.then_inc(masks, 1)
            dve.wait_ge(masks, 1)

            NI = AH * TT
            for n in range(NI + 2):
                if n < NI:
                    t = n % TT
                    L = P * (t + 1)
                    dve.wait_ge(lg_ps, n + 1)
                    if n >= 2:
                        dve.wait_ge(pt_ps, n - 1)
                    link(ve.tensor_tensor_reduce(Lb[:, n % 2, 0:L], mb[n % 2][:, 0:L], idx[:, t, 0:L], 1.0, NEG, ALU.add,
                                                 ALU.max, mx[:, n % 2:n % 2 + 1]))
                    ve.tensor_scalar(nm[:, n % 2:n % 2 + 1], mx[:, n % 2:n % 2 + 1], -A_SCALE, None, ALU.mult).then_inc(lg_max, 1)
                if 1 <= n <= NI:
                    m = n - 1
                    dve.wait_ge(p_exp, m + 1)
                    ve.reciprocal(rc[:, m % 2:m % 2 + 1], sm[:, m % 2:m % 2 + 1]).then_inc(p_rc, 1)
                if n >= 2:
                    m = n - 2
                    dve.wait_ge(pv_ps, m + 1)
                    ve.tensor_copy(UA[:, m // TT, tok(m % TT)], pj[0][:, m % 2, 0:P]).then_inc(pv_sb, 1)
                if n >= 5 and n % TT == 1:
                    x = n // TT - 1
                    lo(x % 2, G_A + x + 3)
            dve.wait_ge(sl_ps, NS)
            link(ve.tensor_copy(Ls, pj[1][0:64, 0, 0:257]))
            fl, f2 = cols[0:64, 18:19], cols[0:64, 19:20]
            link(ve.tensor_tensor(cols[0:64, 8:16], cols[0:64, 0:8], cgt[0:64, :], ALU.mult))
            link(ve.tensor_reduce(fl, cols[0:64, 8:16], AX, ALU.add))
            link(ve.tensor_scalar(f2, fl, 1.0, -NEG, ALU.subtract, ALU.mult))
            link(ve.tensor_scalar(fl, fl, NEG, None, ALU.mult))
            link(ve.tensor_tensor(Ls[:, 255:256], Ls[:, 255:256], fl, ALU.add))
            link(ve.tensor_tensor(Ls[:, 256:257], Ls[:, 256:257], f2, ALU.add))
            link(ve.tensor_reduce(cols[0:64, 20:21], Ls, AX, ALU.max))
            ve.tensor_scalar(cols[0:64, 16:17], cols[0:64, 20:21], -A_SCALE, None, ALU.mult).then_inc(s_max, 1)
            dve.wait_ge(s_exp, 1)
            link(ve.reciprocal(cols[0:64, 17:18], cols[0:64, 17:18]))
            ve.tensor_scalar(Ls, Ls, cols[0:64, 17:18], None, ALU.mult).then_inc(s_p, 1)
            dve.wait_ge(sp_sb, 1)
            tS = tmpS.rearrange("p (b h) -> p b h", b=NS)
            for n in range(AKV):
                ve.tensor_tensor(tS[:, :, n * GRP:n * GRP + GRP], tS[:, :, n * GRP:n * GRP + GRP],
                                 UA[:, U_V + n, NP:T].unsqueeze(2).broadcast_to([P, NS, GRP]), ALU.mult)
            link(ve.memset(cols[:, 60:62], 0.0))
            dve.wait_ge(so_ps, NS)
            ve.tensor_tensor(UA[:, 0:8, NP:T].rearrange("p h b -> p b h"), mb[3][:, 0:64].rearrange("p (b h) -> p b h", b=NS),
                             tS, ALU.add).then_inc(so_sb, 1)

            dve.wait_ge(cv_ps, 6)
            for c in range(24):
                chan, cv = UB[:, U_BQ + c, :], cvt[c % 2]
                if c >= 2:
                    dve.wait_ge(cv_silu, c - 1)
                link(ve.tensor_scalar(cv, chan, conv_col(3, c), None, ALU.mult))
                for j in range(3):
                    d = 3 - j
                    ve.scalar_tensor_tensor(out=cv[:, d:NP], in0=chan[:, 0:NP - d], scalar=conv_col(j, c), in1=cv[:, d:NP],
                                            op0=ALU.mult, op1=ALU.add).then_inc(cv_samp, 1)
                    m = ve.scalar_tensor_tensor(out=cv[:, NP:T], in0=stT[:, c, j::3], scalar=conv_col(j, c), in1=cv[:, NP:T],
                                                op0=ALU.mult, op1=ALU.add)
                    if j < 2:
                        link(m)
                        dve.wait_ge(cv_samp, 3 * c + j + 1)
                m.then_inc(cv_acc, 1)
                if c % 3 == 2:
                    lo(c // 3 % 2, G_D + c // 3 + 3)

            def norm_mul(n):
                dve.wait_ge(nq_rt, nq_ln(n) + 4)
                dst = UB[:, U_BQ + n, :] if n < 16 else UB[:, U_BQ + n - 16, :]
                sc_ = A_SCALE if n < 8 else (1.0 if n < 16 else gdn_g)
                ve.scalar_tensor_tensor(out=dst, in0=dst, scalar=sc_, in1=nrm[n % 4], op0=ALU.mult, op1=ALU.mult).then_inc(nq_done, 1)
            for n in range(16):
                norm_mul(n)

            g3 = gv[:, 3, :].rearrange("p (t h) -> p t h", t=5)
            link(ve.tensor_tensor(g3, ab[:, :, 80:88], dtb.unsqueeze(1).broadcast_to([P, 5, BH]), ALU.add))
            link(ve.tensor_scalar(gv[:, 0, :], gv[:, 3, :], -1.0, None, ALU.mult))
            ve.tensor_tensor(gv[:, 1, :], gv[:, 3, :], gv[:, 0, :], ALU.max).then_inc(dec_a, 1)
            dve.wait_ge(dec_e, 1)
            link(ve.tensor_scalar(gv[:, 3, :], gv[:, 3, :], 0.0, None, ALU.max))
            link(ve.tensor_tensor(gv[:, 3, :], gv[:, 3, :], gv[:, 1, :], ALU.add))
            ve.scalar_tensor_tensor(out=gv[:, 0, :].rearrange("p (t h) -> p t h", t=5), in0=g3, scalar=-1.0,
                                    in1=alog.unsqueeze(1).broadcast_to([P, 5, BH]), op0=ALU.mult, op1=ALU.mult).then_inc(dec_v, 1)
            dve.wait_ge(dec_ps, 1)
            cum, beta, ecum, etot, kdec, nbe, nbeta = gv[:, 3, :], gv[:, 2, :], gv[:, 4, :], gv[:, 5, :], gv[:, 6, :], gv[:, 7, :], gv[:, 1, :]
            link(ve.tensor_copy(cum[:, 0:32], mb[2][:, 0:32]))
            link(ve.tensor_copy(etot[:, 0:32], mb[2][:, 32:64]))
            ve.tensor_tensor(kdec[:, 0:32], etot[:, 0:32], cum[:, 0:32], ALU.subtract).then_inc(dec_a, 1)
            dve.wait_ge(dec_e, 2)
            link(ve.tensor_scalar(nbeta, beta, -1.0, None, ALU.mult))
            ve.tensor_tensor(nbe[:, 0:32], nbeta[:, 0:32], ecum[:, 0:32], ALU.mult).then_inc(dec_v, 1)
            dve.wait_ge(dec_v, 2)

            def hc(v, h):
                return v[:, h:32:BH].unsqueeze(2).broadcast_to([P, TT, P])
            c4 = "p (c n) -> p c n"
            for h in range(BH):
                dve.wait_ge(g_row, h + 1)
                link(ve.tensor_tensor(Di, mb[2][:, :].rearrange(c4, c=4), hc(cum, h), ALU.subtract))
                ve.tensor_scalar(Di, Di, 0.0, None, ALU.max).then_inc(g_nt_in, 1)
                if h:
                    lo(1, G_G + 2 * h + 2)
                dve.wait_ge(g_pre_ps, h + 1)
                ve.tensor_tensor(kd, mb[0][:, :].rearrange(c4, c=4), hc(kdec, h), ALU.mult)
                ve.tensor_tensor(vb, mb[1][:, :].rearrange(c4, c=4), hc(beta, h), ALU.mult)
                dve.wait_ge(g_msk, 2 * h + 1)
                for c in range(TT):
                    e = c * BH + h
                    m = ve.scalar_tensor_tensor(out=Mb[0][:, c, :], in0=mb[3][:, c * P:c * P + P], scalar=nbeta[:, e:e + 1],
                                                in1=Ds[:, c, :], op0=ALU.mult, op1=ALU.mult)
                m.then_inc(g_n, 1)
                dve.wait_ge(g_msk, 2 * h + 2)
                ve.tensor_tensor(outn, pj[0][:, 0, :].rearrange(c4, c=4), Di, ALU.mult).then_inc(g_at, 1)
                dve.wait_ge(g_tr, 2 * h + 1)
                ve.tensor_tensor(Yt, mb[2][:, :].rearrange(c4, c=4), ident[:, :].unsqueeze(1).broadcast_to([P, TT, P]),
                                 ALU.add).then_inc(g_y, 1)
                for s in range(1, 7):
                    dve.wait_ge(g_sq, 11 * h + 2 * s - 1)
                    ve.tensor_copy(Mb[2 * (s % 2)], mb[0][:, :].rearrange(c4, c=4)).then_inc(g_m, 1)
                    dve.wait_ge(g_yps, 6 * h + s)
                    dve.wait_ge(g_y, 7 * h + s)
                    ve.tensor_tensor(Yt, Yt, mb[3][:, :].rearrange(c4, c=4), ALU.add).then_inc(g_y, 1)
                for c in range(TT):
                    e = c * BH + h
                    n = TT * h + c
                    if c == 0:
                        ve.tensor_copy(rr, vb[:, 0, :]).then_inc(c_r, 1)
                    else:
                        dve.wait_ge(c_ks, 3 * h + c)
                        ve.scalar_tensor_tensor(out=rr, in0=mb[0][:, c * P:c * P + P], scalar=nbe[:, e:e + 1], in1=vb[:, c, :],
                                                op0=ALU.mult, op1=ALU.add).then_inc(c_r, 1)
                    if c == 2:
                        lo(0, G_G + 2 * h + 3)
                    dve.wait_ge(c_st, n + 1)
                    if c == 0:
                        if h:
                            dve.wait_ge(ssm_out, 16 * h)
                        ve.tensor_copy(Sst, mb[2][:, 0:P]).then_inc(c_s, 1)
                        ve.tensor_copy(outn[:, 0, :], mb[3][:, 0:P]).then_inc(c_o, 1)
                    else:
                        ve.scalar_tensor_tensor(out=Sst, in0=Sst, scalar=etot[:, e:e + 1], in1=mb[2][:, c * P:c * P + P],
                                                op0=ALU.mult, op1=ALU.add).then_inc(c_s, 1)
                        link(ve.tensor_copy(outn[:, c, :], mb[3][:, c * P:c * P + P]))
                        ve.scalar_tensor_tensor(out=outn[:, c, :], in0=pj[0][:, 0, c * P:c * P + P], scalar=ecum[:, e:e + 1],
                                                in1=outn[:, c, :], op0=ALU.mult, op1=ALU.add).then_inc(c_o, 1)
                    dve.wait_ge(c_s, n + 1)

            dve.wait_ge(g_out, BH)
            lo(1, G_G + 2 * BH + 2)
            id8 = ident[0:NS, 0:NS].unsqueeze(1).broadcast_to([NS, BH, NS])
            for src, slot in ((0, 2), (2, 3)):
                ve.tensor_tensor(gsm[0:NS, slot, :].rearrange("p (h b) -> p h b", h=BH),
                                 gv[0:NS, src, 32:40].unsqueeze(2).broadcast_to([NS, BH, NS]), id8, ALU.mult)
            kS = UB[:, U_BK:U_BK + 8, NP:T]
            qS = UB[:, U_BQ:U_BQ + 8, NP:T]
            vS = UB[:, U_BV:U_BV + 8, NP:T]
            h8 = "p (h b) -> p h b"
            ve.tensor_tensor(gsm[:, 4, :].rearrange(h8, h=BH), kS, qS, ALU.mult)
            link(ve.tensor_copy(gsm[:, 5, :].rearrange(h8, h=BH), kS))
            ve.tensor_copy(kqs[:, :, 0].rearrange(h8, h=BH), kS)
            ve.tensor_copy(kqs[:, :, 1].rearrange(h8, h=BH), qS).then_inc(s_bc, 1)
            dve.wait_ge(s_kq, 1)
            eg, bt, qk, vv = gsm[:, 7, :], gsm[:, 2, :], gsm[:, 3, :], gsm[:, 6, :]
            ve.tensor_copy(bt, mb[0][:, 64:128])
            link(ve.tensor_copy(qk, mb[0][:, 128:192]))
            dve.wait_ge(s_ks, 16)
            kq_ps = mb[1][:, 0:P].rearrange("p (e t) -> p e t", t=2)
            link(ve.tensor_tensor(vv, kq_ps[:, :, 0], eg, ALU.mult))
            link(ve.tensor_tensor(vv.rearrange(h8, h=BH), vS, vv.rearrange(h8, h=BH), ALU.subtract))
            link(ve.tensor_tensor(vv, vv, bt, ALU.mult))
            link(ve.tensor_tensor(qk, qk, vv, ALU.mult))
            link(ve.tensor_tensor(bt, kq_ps[:, :, 1], eg, ALU.mult))
            ve.tensor_tensor(qS, bt.rearrange(h8, h=BH), qk.rearrange(h8, h=BH), ALU.add).then_inc(s_vn, 1)
            for q in range(16):
                dve.wait_ge(s_op, q + 1)
                dve.wait_ge(S_in[q % 4], 16 * (q // 4 + 5))
                for r in range(4):
                    e = 4 * q + r
                    m = ve.scalar_tensor_tensor(out=Sld[q % 4][:, r, :], in0=Sld[q % 4][:, r, :], scalar=eg[:, e:e + 1],
                                                in1=mb[2 + q % 2][:, r * P:r * P + P], op0=ALU.mult, op1=ALU.add)
                m.then_inc(s_new, 1)
            for n in range(16, 24):
                norm_mul(n)
            dve.wait_ge(nq_done, 24)
            for c in range(16):
                dve.wait_ge(z_silu, c + 1)
                dst = UA[:, c, :] if c < 8 else UB[:, U_BQ + c - 8, :]
                z = UB[:, c, :] if c < 8 else UA[:, U_QI + c - 8, :]
                d16 = UA16[:, c] if c < 8 else UBq16[:, c - 8]
                link(ve.tensor_tensor(gtmp, dst, z, ALU.mult))
                link(ve.tensor_scalar(d16[:, 0, :], gtmp, X_SC, None, ALU.mult))
                ve.scalar_tensor_tensor(out=d16[:, 1, :], in0=gtmp, scalar=X_SC, in1=d16[:, 0, :],
                                        op0=ALU.mult, op1=ALU.subtract).then_inc(gated, 1)
                dve.wait_ge(gated, c + 1)

            h2 = "p (h n) -> p h n"

            def merge(i):
                for j in range(4):
                    dve.wait_ge(proj_done, 8 * i + (G_E + 2 * j + 1))
                    dve.wait_ge(gate_sig, 8 * i + (2 * j + 1))
                    ve.tensor_tensor(m1.rearrange(h2, h=2), pj[0][:, :, 0:HALF], gate[j % 2].rearrange(h2, h=2), ALU.mult).then_inc(y_evac, 1)
                    dve.wait_ge(proj_done, 8 * i + (G_E + 2 * j + 2))
                    dve.wait_ge(gate_sig, 8 * i + (2 * j + 2))
                    ve.tensor_tensor(m2b.rearrange(h2, h=2), pj[1][:, :, 0:HALF], gate_m[j % 2].rearrange(h2, h=2), ALU.mult).then_inc(mrg, 1)
                    dve.wait_ge(y_evac, 8 * i + (2 * j + 1))
                    dve.wait_ge(mrg, 12 * i + (3 * j + 1))
                    ve.tensor_tensor(m1, m1, m2b, ALU.add).then_inc(mrg, 1)
                    dve.wait_ge(mrg, 12 * i + (3 * j + 2))
                    d16 = mT16[:, bass.ds(4 * i + j, 1), :, :]
                    ve.tensor_scalar(d16[:, :, 0, :].rearrange("p a b -> p (a b)"), m1, UNSC * X_SC, None, ALU.mult).then_inc(mrg, 1)
                    dve.wait_ge(mrg, 12 * i + (3 * j + 3))
                    ve.scalar_tensor_tensor(out=d16[:, :, 1, :].rearrange("p a b -> p (a b)"), in0=m1, scalar=UNSC * X_SC,
                                            in1=d16[:, :, 0, :].rearrange("p a b -> p (a b)"),
                                            op0=ALU.mult, op1=ALU.subtract).then_inc(y_evac, 1)
                    dve.wait_ge(y_evac, 8 * i + (2 * j + 2))
                    lo(j % 2, 4 * i + (G_E + j + 3))
            with dve.Fori(0, 4) as i:
                merge(i)

            def back(i, last):
                for u in range(4):
                    if not (last and u >= 2):
                        lo(u % 2, 4 * i + (L_F + u + 3))
                    dve.wait_ge(oT_ps, 4 * i + (u + 1))
                    col = P * u + 4 * P * i
                    ve.tensor_copy(Yo[:, 0:4, bass.ds(col, P)], mb[u % 2][:, :].rearrange("p (t n) -> p t n", t=4))
                    ve.tensor_copy(Yo[0:NS, 4, bass.ds(col, P)], mb[2 + u % 2][0:NS, 0:P]).then_inc(oT_sb, 1)
            with dve.Fori(0, 3) as i:
                back(i, False)
            back(3, True)
            dve.wait_ge(sq_done, 10)
            ve.tensor_scalar(rs_x, ssq, 1.0 / D, EPS, ALU.mult, ALU.add).then_inc(mean_sq, 1)
            dve.wait_ge(rms, 3)
            dve.wait_ge(x_back, 96)
            link(ve.reciprocal(rs_x, rs_x))
            for t in range(5):
                n = TOK[t]
                link(ve.scalar_tensor_tensor(out=Yo[0:n, t, :], in0=Yo[0:n, t, :], scalar=rs_x[0:n, t:t + 1], in1=postb[0:n, :],
                                             op0=ALU.mult, op1=ALU.mult))
                ve.tensor_tensor(Yo[0:n, t, :], Yo[0:n, t, :], xf[0:n, t, :] if t < TT else xfs[0:NS, :], ALU.add).then_inc(y_fin, 1)


_INS = ["x_prompt", "x_sample", "cache_k", "cache_v", "cache_kidx", "state_conv", "state_ssm", "page_table", "pre_norm",
        "post_norm", "w_in", "idx_k_norm", "conv_w", "a_log", "dt_bias", "gdn_norm", "w_pa", "w_pb", "w_o"]
_OUTS = [(1, NP, D), (NS, 1, D), (1, 1, NP, AKV, HD), (1, 1, NP, AKV, HD), (1, 1, NP, ID), (1, 1, CONV - 1, CD),
         (1, 1, BH, HD, HD), (1, NS, 1, AKV, HD), (1, NS, 1, AKV, HD), (1, NS, 1, ID), (1, NS, CONV - 1, CD),
         (1, NS, BH, HD, HD)]


def kernel(**inputs):
    import numpy as _np
    import concourse.bacc as _bacc
    from concourse import mybir as _mybir
    from concourse.bass_utils import run_bass_kernel_spmd as _run

    nc = _bacc.Bacc("TRN2", target_bir_lowering=False, num_devices=1)
    arrays, args = {}, []
    for name in _INS:
        a = _np.ascontiguousarray(inputs[name])
        arrays[f"in_{name}_dram"] = a
        args.append(nc.dram_tensor(f"in_{name}_dram", a.shape, _mybir.dt.from_np(a.dtype), kind="ExternalInput").ap())
    for i, shape in enumerate(_OUTS):
        args.append(nc.dram_tensor(f"out_{i}_dram", shape, _mybir.dt.float32, kind="ExternalOutput").ap())
    build(nc, *args)
    r = _run(nc, [arrays], core_ids=[0])
    return tuple(r.results[0][f"out_{i}_dram"] for i in range(len(_OUTS)))
```

```python
from contextlib import ExitStack

import concourse.bass as bass
from concourse import mybir

ALU = mybir.AluOpType
ACT = mybir.ActivationFunctionType
F32 = mybir.dt.float32
BF16 = mybir.dt.bfloat16
F16 = mybir.dt.float16
I32 = mybir.dt.int32
U32 = mybir.dt.uint32
AX = mybir.AxisListType.X

P = 128
D = 2048
KT = D // P
NP = 512
NS = 8
T = NP + NS
HALF = T // 2
TT = NP // P
TOK = [P] * TT + [NS]
HD = 128
AH, AKV = 8, 2
GRP = AH // AKV
IH, ID = 16, 64
BH = 8
CONV = 4
CD = 3 * BH * HD
NPG = 32
SEL_S = 256
EPS = 1e-6
NEG = -1.0e30
TAKEN = -3.0e38
A_SCALE = HD ** -0.5
I_SCALE = ID ** -0.5 * IH ** -0.5

C_Q = 0
C_KI = 2560
C_ZA = 2640
C_AB = 6736
C_ZB = 6752
C_GA = 7776
C_GB = 9824

U_K, U_V, U_QI = 8, 10, 12
U_BQ, U_BK, U_BV = 8, 16, 24

G_B, G_H, G_C, G_A, G_D, G_G, G_Z, G_E, G_F = 0, 20, 28, 60, 68, 72, 88, 92, 124
L_F = 108
W_SC = 256.0
X_SC = 16.0
UNSC = 1.0 / (W_SC * X_SC)


def tok(t):
    return slice(t * P, t * P + TOK[t])


def build(nc, x_prompt, x_sample, cache_k, cache_v, cache_kidx, state_conv, state_ssm, page_table, pre_norm,
          post_norm, w_in, idx_k_norm, conv_w, a_log, dt_bias, gdn_norm, w_pa, w_pb, w_o,
          y_p, y_s, k_p, v_p, kidx_p, conv_p, ssm_p, k_s, v_s, kidx_s, conv_s, ssm_s):
    with ExitStack() as ctx:
        def sb(name, shape, dt=F32):
            return ctx.enter_context(nc.sbuf_tensor(name, shape, dt))

        def sem(name):
            return ctx.enter_context(nc.semaphore(name))

        hT = sb("hT", [P, KT, 2, T], F16)
        raw = sb("raw", [P, 2, KT, P])
        wsp = sb("wsp", [P, 2, 2, KT, P], F16)
        UA = sb("UA", [P, 20, T])
        UB = sb("UB", [P, 32, T])
        idx = sb("idx", [P, TT, NP])
        UAf = UA[:, :, :].rearrange("p a b -> p (a b)")
        UBf = UB[:, :, :].rearrange("p a b -> p (a b)")
        idf = idx[:, :, :].rearrange("p a b -> p (a b)")
        hTf = hT[:, :, :, :].rearrange("p a s b -> p (a s b)").bitcast(F32)
        UA16 = UAf[:, 0:8 * T].bitcast(F16).rearrange("p (k s n) -> p k s n", k=8, s=2)
        UBq16 = UBf[:, U_BQ * T:(U_BQ + 8) * T].bitcast(F16).rearrange("p (k s n) -> p k s n", k=8, s=2)
        mT16 = UBf[:, 16 * T:32 * T].bitcast(F16).rearrange("p (k s n) -> p k s n", k=16, s=2)

        ident = sb("ident", [P, P])
        ones = sb("ones", [P, P])
        tri_le = sb("tri_le", [P, P])
        tri_lt = sb("tri_lt", [P, P])
        swap = sb("swap", [P, P])
        parT = sb("parT", [P, 113])
        stT = sb("stT", [P, 24, 24])
        small = sb("small", [P, 160])
        ab = sb("ab", [P, 5, 96])
        kin = sb("kin", [P, 5, 2, ID])
        kIT = sb("kIT", [P, T])
        qblk = sb("qblk", [P, NS, 32])
        wbc = sb("wbc", [P, NS, IH])
        Y = sb("Y", [P, NS, NPG + 1])
        bit_i = sb("bit_i", [P, 32], I32)
        bit_f = sb("bit_f", [P, 32])
        thr_i = sb("thr_i", [P, NS], I32)
        cand_i = sb("cand_i", [P, NS], I32)
        m_i = sb("m_i", [P, NS], I32)
        srt = sb("srt", [P, 12, NS])
        iota_b = sb("iota_b", [P, SEL_S], BF16)
        coef = sb("coef", [3, 1])
        pg_i = sb("pg_i", [P, P], I32)
        off_i = sb("off_i", [P, P], I32)
        sel_i = sb("sel_i", [P, 16], I32)
        gv = sb("gv", [P, 12, 5 * BH])
        qm = sb("qm", [P, 1088])
        vn = sb("vn", [P, TT, 256])
        gsm = sb("gsm", [P, 8, 64])
        cols = sb("cols", [P, 64])
        top8 = sb("top8", [P, TT, 8])

        rs_x = small[:, 0:5]
        ssq = small[:, 5:10]
        ki_s = small[:, 10:15]
        ki_r = small[:, 15:20]
        pm64 = small[:, 20:21]
        alog = small[:, 24:32]
        dtb = small[:, 32:40]
        eps_c = small[:, 40:41]
        idxg = small[:, 64:128]
        mx = small[:, 128:130]
        nm = small[:, 130:132]
        sm = small[:, 132:134]
        rc = small[:, 134:136]
        g_pre = parT[:, 0:16]
        gdn_g = parT[:, 112:113]

        x_nat = UAf[:, 0:5 * D].rearrange("p (t d) -> p t d", t=5)
        st_nat = UBf[0:24, 0:CD]
        wa = UBf[:, 3072:3072 + KT * 96].rearrange("p (k n) -> p k n", k=KT)
        wa16 = UBf[:, 15872 - 1536:15872].bitcast(F16).rearrange("p (s k n) -> p s k n", s=2, k=KT)
        kraw = [UBf[:, x:x + 2048].rearrange("p (c d) -> p c d", c=16) for x in (4608, 6656, 2 * T)]
        kTp = [UBf[:, 8704 + 2048 * i:10752 + 2048 * i].rearrange("p (c d) -> p c d", c=16) for i in range(2)]
        rel = UBf[:, 12800:14848].rearrange("p (r n) -> p r n", r=4)
        wsum = UBf[:, 4096:4608]
        junk = UBf[:, 12800:14848]
        knat = [UBf[:, x:x + 512] for x in (0, 512, 2 * T + 2048, 14848, 15360)]

        pt_i = UBf[:, 15872:16128].bitcast(I32)
        xw = UBf[0:NS, 16128:16256].rearrange("p (b h) -> p b h", b=NS)
        par = UBf[:, 16256:16384]

        QS = UAf[:, U_QI * T:U_QI * T + 8 * T]
        NY = NS * (NPG + 1)
        ge, t1, pos, wsum_gt = (QS[:, NY * x:NY * x + NY] for x in range(4))
        rk = QS[:, 4 * NY:4 * NY + 400]
        rk2 = QS[:, 4 * NY + 400:4 * NY + 400 + NS * 17]
        qs0 = 4 * NY + 400 + NS * 17
        vals = QS[:, qs0:qs0 + 384].bitcast(BF16).rearrange("p (c s v) -> p c s v", s=2, v=3)
        onehot = QS[:, qs0 + 384:qs0 + 896].bitcast(BF16).rearrange("p (r n) -> p r n", r=4)
        row3 = QS[0:3, qs0 + 896:qs0 + 1408].rearrange("p (r n) -> p r n", r=2)
        QS = UAf[:, U_QI * T:U_QI * T + 8 * T]
        Lb = QS[:, 0:1024].rearrange("p (r n) -> p r n", r=2)
        PTs = QS[:, 1024:2048].rearrange("p (r n) -> p r n", r=2)
        KTs = QS[:, 2048:2562].rearrange("p (n c) -> p n c", n=2)
        kv_sel = QS[:, 2562:2562 + 1536].rearrange("p (s h c) -> p s h c", s=3, h=2)
        Ls = idf[0:64, 0:257]
        PTs_s = idf[:, 512:640].rearrange("p (h c) -> p h c", h=2)
        tmpS = idf[:, 640:704]

        kd = idf[:, 0:512].rearrange("p (c n) -> p c n", c=4)
        vb = idf[:, 512:1024].rearrange("p (c n) -> p c n", c=4)
        Ds = idf[:, 1024:1536].rearrange("p (c n) -> p c n", c=4)
        atT = idf[:, 1536:2048].rearrange("p (c n) -> p c n", c=4)
        R2 = UAf[:, U_K * T:U_K * T + 4 * T]
        Mb = [R2[:, 512 * i:512 * i + 512].rearrange("p (c n) -> p c n", c=4) for i in range(4)]
        Yt = qm[:, 0:512].rearrange("p (c n) -> p c n", c=4)
        outn = qm[:, 512:1024].rearrange("p (c n) -> p c n", c=4)
        vnf = vn[:, :, :].rearrange("p a b -> p (a b)")
        Di = vnf[:, 0:512].rearrange("p (c n) -> p c n", c=4)
        Sst = vnf[:, 512:640]
        rr = vnf[:, 640:768]
        vnew = vnf[:, 768:896]
        nrm = [idf[:, 0:T], idf[:, T:2 * T], idf[:, 2 * T:3 * T], qm[:, 0:T]]
        cvt = kIT[:, :]
        gate = [kIT[:, :], stT[:, :, :].rearrange("p a b -> p (a b)")[:, 0:T]]
        win = gsm[:, :, :].rearrange("p a b -> p (a b)")[:, 0:264].rearrange("p (c t) -> p c t", c=24)
        gate_e = [UBf[:, 0:T], UBf[:, T:2 * T]]
        gate_m = [idf[:, 0:T], idf[:, T:2 * T]]
        gate_d = nc.dram_tensor("gates", (2, KT, P, T), F32).ap()
        Sld = [idf[:, 512 * i:512 * i + 512].rearrange("p (r n) -> p r n", r=4) for i in range(4)]
        vexp = [R2[0:64, 512 * i:512 * i + 512].rearrange("p (r n) -> p r n", r=4) for i in range(2)]
        kns = gv[0:64, 8:12, :].rearrange("p a b -> p (a b)")[:, 0:P]
        kqs = gv[:, 1:5, :].rearrange("p a b -> p (a b)")[:, 0:P].rearrange("p (e t) -> p e t", t=2)
        gtmp = qm[:, T:2 * T]
        m1 = idf[:, 2 * T:3 * T]
        m2b = qm[:, 0:T]
        oT = [idf[:, 0:T], idf[:, T:2 * T]]
        Yo = UAf[:, 0:5 * D].rearrange("p (t d) -> p t d", t=5)
        xf = UBf[:, 0:4 * D].rearrange("p (t d) -> p t d", t=4)
        xfs = hTf[:, 0:D]
        postb = hTf[:, D:2 * D]
        osq = hTf[:, 2 * D:2 * D + 10 * P].rearrange("p (r n) -> p r n", r=10)
        ssq16 = gsm[:, :, :].rearrange("p a b -> p (a b)")[:, 0:80].rearrange("p (t n) -> p t n", t=5)

        pj = [ctx.enter_context(nc.psum_tensor(f"pj{i}", [P, 2, 512], F32)) for i in range(2)]
        mb = [ctx.enter_context(nc.psum_tensor(f"mb{i}", [P, 512], F32)) for i in range(4)]

        consts = sem("consts")
        par_in, st_in, wa_in = sem("par_in"), sem("st_in"), sem("wa_in")
        x_in = [sem(f"x_in{t}") for t in range(5)]
        row_in = sem("row_in")
        w_in_s = [sem(f"w_slot{i}") for i in range(2)]
        w_hi, w_lo, x_hi = sem("w_hi"), sem("w_lo"), sem("x_hi")
        parT_ps, parT_sb, sq_done, mean_sq, rms, x_scaled = (sem(n) for n in (
            "parT_ps", "parT_sb", "sq_done", "mean_sq", "rms", "x_scaled"))
        xT_sb, ab_ps, ki_done, kiT_ps, kiT_sb = (sem(n) for n in (
            "xT_sb", "ab_ps", "ki_done", "kiT_ps", "kiT_sb"))
        proj_done, proj_evac, y_evac = sem("proj_done"), sem("proj_evac"), sem("y_evac")
        kv_ps, kv_sb, kv_out = sem("kv_ps"), sem("kv_sb"), sem("kv_out")
        q_swap, w_x, qw_done = sem("q_swap"), sem("w_x"), sem("qw_done")
        idx_ps, idx_relu, idx_acc, idx_mask = sem("idx_ps"), sem("idx_relu"), sem("idx_acc"), sem("idx_mask")
        off_done, kraw_in = sem("off_done"), [sem(f"kraw_in{i}") for i in range(3)]
        kp_ps, kp_sb, ks_ps, ks_sum = sem("kp_ps"), sem("kp_sb"), sem("ks_ps"), sem("ks_sum")
        cnt_part, cnt_all, srch, topk = sem("cnt_part"), sem("cnt_all"), sem("srch"), sem("topk")
        rank_in, rank_ps, hot, hot_ps, row_sb, row_ps, sel_done = (sem(n) for n in (
            "rank_in", "rank_ps", "hot", "hot_ps", "row_sb", "row_ps", "sel_done"))
        kv_in = [sem(f"kv_in{i}") for i in range(3)]
        masks = sem("masks")
        lg_ps, lg_max, p_exp, p_rdy, pt_ps, pt_sb, pv_ps, pv_sb = (sem(n) for n in (
            "lg_ps", "lg_max", "p_exp", "p_rdy", "pt_ps", "pt_sb", "pv_ps", "pv_sb"))
        sk_ps, sk_sb, sl_ps, s_max, s_exp, s_p, sp_ps, sp_sb, so_ps, so_sb = (sem(n) for n in (
            "sk_ps", "sk_sb", "sl_ps", "s_max", "s_exp", "s_p", "sp_ps", "sp_sb", "so_ps", "so_sb"))
        cv_ps, cv_sb, cv_out, cv_acc, cv_silu, cv_step = (sem(n) for n in (
            "cv_ps", "cv_sb", "cv_out", "cv_acc", "cv_silu", "cv_step"))
        nq_sq, nq_ps, nq_rt, nq_done = sem("nq_sq"), sem("nq_ps"), sem("nq_rt"), sem("nq_done")
        dec_a, dec_v, dec_ps, dec_e = sem("dec_a"), sem("dec_v"), sem("dec_ps"), sem("dec_e")
        g_pre_ps, g_row, g_exp, g_msk, g_n, g_at, g_tr, g_nt, g_y = (sem(n) for n in (
            "g_pre_ps", "g_row", "g_exp", "g_msk", "g_n", "g_at", "g_tr", "g_nt", "g_y"))
        g_sq, g_m, g_mt, g_yps = sem("g_sq"), sem("g_m"), sem("g_mt"), sem("g_yps")
        c_ks, c_r, c_vps, c_vn, c_st, c_s, c_o, g_oT, g_out, ssm_out = (sem(n) for n in (
            "c_ks", "c_r", "c_vps", "c_vn", "c_st", "c_s", "c_o", "g_oT", "g_out", "ssm_out"))
        S_in = [sem(f"S_in{i}") for i in range(4)]
        s_kq, s_bc, s_bcs, s_ks, s_vn, s_tps, s_tsb, s_vx, s_op, s_new = (sem(n) for n in (
            "s_kq", "s_bc", "s_bcs", "s_ks", "s_vn", "s_tps", "s_tsb", "s_vx", "s_op", "s_new"))
        S_out = [sem(f"S_out{i}") for i in range(4)]
        waited = sem("waited")
        gate_out = [sem("gate_out0"), sem("gate_out1")]
        gate_in = [sem("gate_in0"), sem("gate_in1")]
        gate_sig = sem("gate_sig")
        mrg, g_nt_in = sem("mrg"), sem("g_nt_in")
        z_silu, gated = sem("z_silu"), sem("gated")
        oT_ps, oT_sb, x_back, post_in, y_fin, y_out = (sem(n) for n in (
            "oT_ps", "oT_sb", "x_back", "post_in", "y_fin", "y_out"))
        dve_c, act_c, pool_c = sem("dve_c"), sem("act_c"), sem("pool_c")

        def linker(eng, s):
            n = [0]

            def link(ins):
                n[0] += 1
                ins.then_inc(s, 1)
                eng.wait_ge(s, n[0])
            return link

        w_in_v = w_in[0].rearrange("(k p) n -> p k n", p=P)
        pa_v = w_pa[0].rearrange("(k p) n -> p k n", p=P)
        pb_v = w_pb[0].rearrange("(k p) n -> p k n", p=P)
        o_v = w_o[0].rearrange("(k p) n -> p k n", p=P)
        kidx_rows = cache_kidx[0].rearrange("g (q s) d -> (g q) (s d)", s=2)
        ck_rows = cache_k[0].rearrange("g t n d -> (g t) (n d)")
        cv_rows = cache_v[0].rearrange("g t n d -> (g t) (n d)")
        N_CONST = 15

        def gate_group(f):
            return G_H + f if f < 8 else G_A + f - 8 if f < 16 else G_G + f - 16

        def zb_group(z):
            return G_D + z if z < 4 else G_Z + z - 4

        def nq_ln(n):
            return 8 * (n // 4) + n % 4 + 1

        block = ctx.enter_context(nc.Block())

        @block.sync
        def _(sp):
            sp.dma_start(par[0:16, :], pre_norm[0].rearrange("(k p) -> k p", p=P)).then_inc(par_in, 16)
            sp.dma_start(par[16:112, :], conv_w[0].rearrange("j (c p) -> (j c) p", p=P)).then_inc(par_in, 16)
            sp.dma_start(par[112:113, :], gdn_norm[0:1, :]).then_inc(par_in, 16)
            for t in range(TT):
                sp.dma_start(x_nat[:, t, :], x_prompt[0, tok(t), :]).then_inc(x_in[t], 16)
            sp.dma_start(x_nat[0:NS, TT, :], x_sample.rearrange("b s d -> (b s) d")).then_inc(x_in[TT], 16)
            sp.dma_start(wa[:, :, 0:80], w_in_v[:, :, C_KI:C_KI + 80]).then_inc(wa_in, 16)
            sp.dma_start(wa[:, :, 80:96], w_in_v[:, :, C_AB:C_AB + 16], ).then_inc(wa_in, 16)
            sp.dma_start(st_nat, state_conv[0].rearrange("b j c -> (b j) c")).then_inc(st_in, 16)
            sp.dma_start(conv_s[0, :, 0:2, :], state_conv[0, :, 1:3, :]).then_inc(cv_out, 16)

            def load(slot, src, dst=None):
                sp.dma_start(raw[:, slot, :, :] if dst is None else dst, src).then_inc(w_in_s[slot], 16)

            def split_free(v):
                sp.wait_ge(w_lo, v)
                sp.sem_inc(waited, 1)

            def in_loads(i, base, col, first=0):
                for u in range(first, 4):
                    split_free(4 * i + (base + u - 1))
                    load(u % 2, w_in_v[:, :, bass.ds(col + P * u + 4 * P * i, P)])
            for u in range(2):
                load(u, w_in_v[:, :, C_Q + P * u:C_Q + P * u + P])
            in_loads(0, 0, C_Q, 2)
            with sp.Fori(1, 5) as i:
                in_loads(i, 0, C_Q)
            with sp.Fori(0, 2) as i:
                in_loads(i, G_H, C_GB)
            with sp.Fori(0, 8) as i:
                in_loads(i, G_C, C_ZA)
            with sp.Fori(0, 2) as i:
                in_loads(i, G_A, C_GB + 8 * P)
            in_loads(0, G_D, C_ZB)
            with sp.Fori(0, 4) as i:
                in_loads(i, G_G, C_GA)
            in_loads(0, G_Z, C_ZB + 4 * P)

            def merge_load(i, j):
                col = 4 * P * i + P * j
                split_free(4 * i + (G_E + j - 1))
                load(j % 2, pa_v[:, :, bass.ds(col, P)], raw[:, j % 2, 0:8, :])
                load(j % 2, pb_v[:, :, bass.ds(col, P)], raw[:, j % 2, 8:16, :])

            def gates_back(i, j, used):
                if used is not None:
                    sp.wait_ge(y_evac, used)
                    sp.sem_inc(waited, 1)
                n = 4 * i + j
                for br, dst in ((0, gate[j % 2]), (1, gate_m[j % 2])):
                    sp.dma_start(dst.unsqueeze(1), gate_d[br, bass.ds(n, 1)].rearrange("n p t -> p n t")).then_inc(gate_in[j % 2], 16)
            merge_load(0, 0)
            merge_load(0, 1)
            for r in range(2):
                sp.wait_ge(gate_out[r], 16 * 16)
            sp.wait_ge(gated, 16)
            gates_back(0, 0, None)
            gates_back(0, 1, None)
            for j in range(2, 4):
                merge_load(0, j)
                gates_back(0, j, 2 * j - 2)
            with sp.Fori(1, 4) as i:
                for j in range(4):
                    merge_load(i, j)
                    gates_back(i, j, 8 * i + (2 * j - 2))
            def out_loads(i):
                for u in range(4):
                    split_free(4 * i + (L_F + u - 1))
                    load(u % 2, o_v[:, :, bass.ds(P * u + 4 * P * i, P)])
            out_loads(0)
            sp.wait_ge(y_evac, 32)
            sp.wait_ge(proj_done, G_F)
            sp.dma_start(postb, post_norm[0:1, :].broadcast_to([P, D])).then_inc(post_in, 16)
            sp.dma_start(xfs[0:NS, :], x_sample.rearrange("b s d -> (b s) d")).then_inc(x_back, 16)
            with sp.Fori(1, 4) as i:
                out_loads(i)
            for t in range(TT):
                sp.dma_start(xf[:, t, :], x_prompt[0, tok(t), :]).then_inc(x_back, 16)
            for t in range(5):
                sp.wait_ge(y_fin, t + 1)
                sp.dma_start(y_p[0, tok(t), :] if t < TT else y_s.rearrange("b s d -> (b s) d"),
                             Yo[0:TOK[t], t, :]).then_inc(y_out, 16)
            sp.wait_ge(y_out, 16 * 5)

        @block.gpsimd
        def _(pool):
            link = linker(pool, pool_c)
            g = nc.gpsimd
            link(g.memset(ones[:, :], 1.0))
            g.affine_select(out=ident[:, :], in_=ones[:, :], compare_op=ALU.is_equal, fill=0.0, base=0,
                            pattern=[[-1, P]], channel_multiplier=1).then_inc(consts, 1)
            g.affine_select(out=tri_le[:, :], in_=ones[:, :], compare_op=ALU.is_ge, fill=0.0, base=0,
                            pattern=[[1, P]], channel_multiplier=-1).then_inc(consts, 1)
            g.affine_select(out=tri_lt[:, :], in_=ones[:, :], compare_op=ALU.is_gt, fill=0.0, base=0,
                            pattern=[[1, P]], channel_multiplier=-1).then_inc(consts, 1)
            link(g.affine_select(out=swap[:, :], in_=ones[:, :], compare_op=ALU.is_equal, fill=0.0, base=64,
                                 pattern=[[-1, P]], channel_multiplier=1))
            g.affine_select(out=swap[:, :], in_=swap[:, :], compare_op=ALU.not_equal, fill=1.0, base=-64,
                            pattern=[[-1, P]], channel_multiplier=1).then_inc(consts, 1)
            link(g.iota(pm64, [[0, 1]], base=0, channel_multiplier=1, allow_small_or_imprecise_dtypes=True))
            g.iota(small[64:128, 20:21], [[0, 1]], base=0, channel_multiplier=1,
                   allow_small_or_imprecise_dtypes=True).then_inc(consts, 1)
            pool.wait_ge(consts, 5)
            g.iota(iota_b[:, :], [[1, SEL_S]], base=0, channel_multiplier=0,
                   allow_small_or_imprecise_dtypes=True).then_inc(consts, 1)
            g.memset(eps_c, EPS).then_inc(consts, 1)
            link(g.memset(coef[:, :], 1.0))
            link(g.affine_select(out=coef[:, :], in_=coef[:, :], compare_op=ALU.not_equal, fill=2048.0, base=-1,
                                 pattern=[[0, 1]], channel_multiplier=1))
            g.affine_select(out=coef[:, :], in_=coef[:, :], compare_op=ALU.not_equal, fill=128.0, base=-2,
                            pattern=[[0, 1]], channel_multiplier=1).then_inc(consts, 1)
            for s in range(31):
                g.memset(bit_i[:, s:s + 1], 1 << (30 - s))
                g.memset(bit_f[:, s:s + 1], float(1 << (30 - s)))
            g.memset(bit_i[:, 31:32], 0)
            g.memset(bit_f[:, 31:32], 0.0).then_inc(consts, 1)
            g.memset(qblk[:, :, :], 0.0).then_inc(consts, 1)
            g.memset(qm[:, :], 0.0).then_inc(consts, 1)
            g.memset(ab[:, :, :], 0.0).then_inc(consts, 1)
            g.memset(small[:, 0:20], 1.0).then_inc(consts, 1)
            g.memset(Y[:, :, NPG:NPG + 1], TAKEN).then_inc(consts, 1)
            blk = cols[0:64, 0:8]
            link(g.affine_select(out=blk, in_=ones[0:64, 0:8], compare_op=ALU.is_ge, fill=0.0, base=0,
                                 pattern=[[-8, 8]], channel_multiplier=1))
            g.affine_select(out=blk, in_=blk, compare_op=ALU.is_ge, fill=0.0, base=7,
                            pattern=[[8, 8]], channel_multiplier=-1).then_inc(consts, 1)

            pool.wait_ge(off_done, 1)
            for b in range(NS):
                if b == 2:
                    pool.wait_ge(parT_ps, 22)
                if b >= 3:
                    pool.wait_ge(kp_ps, 4 * (b - 2))
                for c in range(16):
                    g.indirect_dma_start(out=kraw[b % 3][:, c, :], out_offset=None, in_=kidx_rows,
                                         in_offset=bass.IndirectOffsetOnAxis(ap=off_i[:, 16 * b + c:16 * b + c + 1].bitcast(U32), axis=0),
                                         ).then_inc(kraw_in[b % 3], 16)
            for t in range(1, TT):
                pool.wait_ge(idx_acc, 16 * t)
                g.affine_select(out=idx[:, t, t * P:t * P + P], in_=idx[:, t, t * P:t * P + P], compare_op=ALU.is_ge,
                                fill=NEG, base=0, pattern=[[-1, P]], channel_multiplier=1).then_inc(idx_mask, 1)
            link(g.memset(idx[:, 0, 0:P], 0.0))
            g.affine_select(out=idx[:, 0, 0:P], in_=idx[:, 0, 0:P], compare_op=ALU.is_ge,
                            fill=NEG, base=0, pattern=[[-1, P]], channel_multiplier=1).then_inc(idx_mask, 1)

            pool.wait_ge(sel_done, 1)
            def gather(m):
                if m >= 3:
                    prev = m - 3
                    if prev < NS:
                        pool.wait_ge(sk_ps, prev + 1)
                    else:
                        pool.wait_ge(so_ps, prev - NS + 1)
                b = m % NS
                for half in range(2):
                    g.indirect_dma_start(out=kv_sel[:, m % 3, half, :], out_offset=None,
                                         in_=ck_rows if m < NS else cv_rows,
                                         in_offset=bass.IndirectOffsetOnAxis(
                                             ap=sel_i[:, 2 * b + half:2 * b + half + 1].bitcast(U32), axis=0),
                                         ).then_inc(kv_in[m % 3], 16)
            for m in range(3):
                gather(m)
            for m in range(3, 2 * NS):
                gather(m)

            for h in range(BH):
                pool.wait_ge(g_exp, h + 1)
                if h:
                    pool.wait_ge(g_oT, h)
                g.affine_select(out=Ds, in_=Di, compare_op=ALU.is_gt, fill=0.0, base=0,
                                pattern=[[0, TT], [-1, P]], channel_multiplier=1).then_inc(g_msk, 1)
                pool.wait_ge(g_msk, 2 * h + 1)
                g.affine_select(out=Di, in_=Di, compare_op=ALU.is_ge, fill=0.0, base=0,
                                pattern=[[0, TT], [-1, P]], channel_multiplier=1).then_inc(g_msk, 1)
            pool.wait_ge(s_tsb, 2)
            for q in range(16):
                if q >= 2:
                    pool.wait_ge(s_op, q - 1)
                g.tensor_tensor(vexp[q % 2], gsm[0:64, 0:2, :].rearrange("p a b -> p (a b)").unsqueeze(1).broadcast_to([64, 4, P]),
                                ident[0:64, 4 * q:4 * q + 4].unsqueeze(2).broadcast_to([64, 4, P]), ALU.mult).then_inc(s_vx, 1)

        @block.tensor
        def _(pe):
            te = nc.tensor
            pe.wait_ge(consts, N_CONST)
            pe.wait_ge(par_in, 48)
            te.transpose(mb[0][:, 0:113], par[0:113, :], ident[0:113, 0:113]).then_inc(parT_ps, 1)
            pe.wait_ge(parT_sb, 1)
            def ab_tile(t):
                n = TOK[t]
                for k in range(KT):
                    for e, (xs, ws) in enumerate(((0, 0), (0, 1), (1, 0))):
                        m = te.matmul(pj[1][0:n, 0, 96 * t:96 * t + 96], hT[:, k, xs, tok(t)], wa16[:, ws, k, :],
                                      start=(k == 0 and e == 0), stop=(k == KT - 1 and e == 2))
                if t == TT:
                    m.then_inc(ab_ps, 1)

            for t in range(6):
                if t < 5:
                    n = TOK[t]
                    pe.wait_ge(x_scaled, t + 1)
                    for q in range(4):
                        e = 4 * t + q
                        if e >= 4:
                            pe.wait_ge(xT_sb, e - 2)
                        for u in range(4):
                            k = 4 * q + u
                            m = te.transpose(mb[q][:, u * P:u * P + n], x_nat[0:n, t, k * P:k * P + P], ident[0:n, 0:n])
                        m.then_inc(parT_ps, 1)
                if t:
                    pe.wait_ge(xT_sb, 4 * t + 1)
                    ab_tile(t - 1)

            def project_step(pair, slot, rhs, k, k0=0, kn=KT):
                for ws, xs in ((0, 0), (0, 1), (1, 0)):
                    for half in range(2):
                        m = te.matmul(pj[pair][:, half, 0:HALF], wsp[:, slot, ws, k0 + k, :],
                                      rhs[:, k, xs, half * HALF:half * HALF + HALF],
                                      start=(k == 0 and ws + xs == 0), stop=(k == kn - 1 and ws == 1))
                if k == kn - 1:
                    m.then_inc(proj_done, 1)

            def project(pair, slot, rhs, k0=0, kn=KT):
                for k in range(kn):
                    project_step(pair, slot, rhs, k, k0, kn)

            def parts(group_of):
                step = [0]

                def part(n):
                    for x in range(n):
                        f, k = divmod(step[0], KT)
                        step[0] += 1
                        if k == 0:
                            pe.wait_ge(w_lo, group_of(f) + 1)
                            pe.wait_ge(proj_evac, group_of(f))
                        project_step(1, f % 2, hT, k)
                return part
            gate_part = parts(gate_group)
            zb_part = parts(zb_group)

            def tiles_b(i, first):
                for u in range(1 if first else 0, 4):
                    pe.wait_ge(w_lo, 4 * i + (u + 1))
                    if not (first and u < 2):
                        pe.wait_ge(proj_evac, 4 * i + (u - 1))
                    project(u % 2, u % 2, hT)
            pe.wait_ge(w_lo, 1)
            project(0, 0, hT)
            pe.wait_ge(st_in, 16)
            for c in range(24):
                m = te.transpose(mb[2 + c // 12][:, 24 * (c % 12):24 * (c % 12) + 24], st_nat[:, c * P:c * P + P],
                                 ident[0:24, 0:24])
            m.then_inc(parT_ps, 1)
            pe.wait_ge(ki_done, 5)
            for t in range(5):
                n = TOK[t]
                m = te.transpose(mb[t // 4][:, (t % 4) * P:(t % 4) * P + n], kin[0:n, t, :, :].rearrange("p a b -> p (a b)"),
                                 ident[0:n, 0:n])
            m.then_inc(kiT_ps, 1)
            tiles_b(0, True)
            with pe.Fori(1, 5) as i:
                tiles_b(i, False)

            pe.wait_ge(proj_evac, 20)
            pe.wait_ge(kiT_sb, 2)
            for t in range(5):
                n = TOK[t]
                if t >= 2:
                    pe.wait_ge(kv_sb, t - 1)
                for c in range(4):
                    m = te.transpose(mb[t % 2][0:n, c * P:c * P + P], UA[:, U_K + c, tok(t)], ident[:, :])
                m.then_inc(kv_ps, 1)
            te.matmul(mb[2][:, 0:64], swap[:, :], UA[:, U_QI:U_QI + 8, NP:T], start=True, stop=True).then_inc(q_swap, 1)
            pe.wait_ge(w_x, 1)
            te.matmul(mb[3][:, 0:P], ones[0:NS, :], xw[:, :, :], start=True, stop=True).then_inc(q_swap, 1)
            pe.wait_ge(qw_done, 2)
            pe.wait_ge(kv_sb, 5)
            for n in range(48):
                t, hh = n // 16 + 1, n % 16
                if n >= 4:
                    pe.wait_ge(idx_relu, n - 3)
                lo = 64 * (hh % 2)
                te.matmul(mb[n % 4][:, 0:P * (t + 1)], UA[lo:lo + 64, U_QI + hh // 2, tok(t)],
                          kIT[lo:lo + 64, 0:P * (t + 1)], start=True, stop=True).then_inc(idx_ps, 1)
            pe.wait_ge(idx_relu, 48)

            def kidx_T(b):
                pe.wait_ge(kraw_in[b % 3], 256 * (b // 3 + 1))
                for q in range(4):
                    if b:
                        pe.wait_ge(kp_sb, 4 * (b - 1) + q + 1)
                    for u in range(4):
                        m = te.transpose(mb[q][:, u * P:u * P + P], kraw[b % 3][:, 4 * q + u, :], ident[:, :])
                    m.then_inc(kp_ps, 1)
                    if b:
                        gate_part(2)

            def kidx_score(b):
                pe.wait_ge(kp_sb, 4 * (b + 1))
                if b >= 2:
                    pe.wait_ge(ks_sum, b - 1)
                for c in range(16):
                    m = te.matmul(pj[0][:, b % 2, 32 * c:32 * c + 32], kTp[b % 2][:, c, :], qblk[:, b, :],
                                  start=True, stop=True)
                m.then_inc(ks_ps, 1)
            kidx_T(0)
            for b in range(NS):
                if b + 1 < NS:
                    kidx_T(b + 1)
                kidx_score(b)
                gate_part(8 if b + 1 < NS else 16)
            pe.wait_ge(proj_evac, G_C)
            for b in range(NS):
                m = te.matmul(pj[1][:, 0, 16 * b:16 * b + 16], kIT[0:64, NP + b:NP + b + 1].broadcast_to([64, P]),
                              qblk[0:64, b, 0:16], start=True, stop=True)
            m.then_inc(ks_ps, 1)
            pe.wait_ge(ks_sum, NS + 1)

            def count(v):
                pe.wait_ge(cnt_part, v)
                te.matmul(mb[0][:, 0:NS], ones[:, :], srt[:, 0, :], start=True, stop=True).then_inc(cnt_all, 1)
            count(1)
            with pe.Fori(0, 8) as i:
                for u in range(4):
                    pe.wait_ge(w_lo, 4 * i + (G_C + u + 1))
                    pe.wait_ge(proj_evac, 4 * i + (G_C + u - 1))
                    project(u % 2, u % 2, hT)
                    count(4 * i + (u + 2))

            srt_pair = t1[:, 0:NS * 17]
            pe.wait_ge(rank_in, 1)
            te.matmul(mb[0][:, 0:NS], ones[:, :], srt[:, 0, :], start=True, stop=True).then_inc(rank_ps, 1)
            pe.wait_ge(rank_in, 2)
            te.matmul(mb[2][:, 0:NS * 17], tri_lt[:, :], srt_pair, start=True, stop=True).then_inc(rank_ps, 1)
            te.matmul(mb[3][:, 0:NS * 17], ones[:, :], srt_pair, start=True, stop=True).then_inc(rank_ps, 1)
            pe.wait_ge(rank_in, 3)
            te.matmul(mb[2][:, 0:NS * 17], tri_lt[:, :], srt_pair, start=True, stop=True).then_inc(rank_ps, 1)
            te.matmul(mb[3][:, 0:NS * 17], ones[:, :], srt_pair, start=True, stop=True).then_inc(rank_ps, 1)
            pe.wait_ge(rank_in, 4)
            te.matmul(mb[0][:, 8:8 + NS], ones[:, :], srt[:, 0, :], start=True, stop=True).then_inc(rank_ps, 1)
            for b in range(NS):
                if b >= 2:
                    pe.wait_ge(row_sb, b - 1)
                for c in range(NPG):
                    e = NPG * b + c
                    pe.wait_ge(hot, e + 1)
                    m = te.matmul(mb[1][0:3, 256 * (b % 2):256 * (b % 2) + 256] if b % 2 == 0 else mb[2][0:3, 0:256],
                                  vals[:, e // 2, e % 2, :], onehot[:, e % 4, :],
                                  start=(c == 0), stop=(c == NPG - 1))
                    m.then_inc(hot_ps, 1)
                    if e % 8 == 7:
                        gate_part(1)
                pe.wait_ge(row_sb, b + 1)
                for half in range(2):
                    m = te.matmul(mb[3][:, 2 * b + half:2 * b + half + 1], row3[0:3, b % 2, half * P:half * P + P],
                                  coef[:, :], start=True, stop=True)
                m.then_inc(row_ps, 1)
            pe.wait_ge(sel_done, 1)
            pe.wait_ge(masks, 1)
            pe.wait_ge(proj_evac, G_A)

            def logits(n):
                h, t = divmod(n, TT)
                if n >= 2:
                    pe.wait_ge(lg_max, n - 1)
                te.matmul(mb[n % 2][:, 0:P * (t + 1)], UA[:, h, tok(t)], UA[:, U_K + h // GRP, 0:P * (t + 1)],
                          start=True, stop=True).then_inc(lg_ps, 1)

            def probs_T(n):
                pe.wait_ge(p_rdy, n + 1)
                if n >= 2:
                    pe.wait_ge(pt_sb, n - 1)
                for l in range(n % TT + 1):
                    m = te.transpose(mb[2 + n % 2][:, l * P:l * P + P], Lb[:, n % 2, l * P:l * P + P], ident[:, :])
                m.then_inc(pt_ps, 1)

            def probs_v(n):
                h, t = divmod(n, TT)
                pe.wait_ge(pt_sb, n + 1)
                if n >= 2:
                    pe.wait_ge(pv_sb, n - 1)
                c0 = (h // GRP) * HD
                for l in range(t + 1):
                    m = te.matmul(pj[0][:, n % 2, 0:P], vn[:, l, c0:c0 + HD], PTs[:, n % 2, l * P:l * P + P],
                                  start=(l == 0), stop=(l == t))
                m.then_inc(pv_ps, 1)
            NI = AH * TT
            for n in range(NI + 2):
                if n < NI:
                    logits(n)
                    gate_part(1)
                if 1 <= n <= NI:
                    probs_T(n - 1)
                    if n < NI:
                        gate_part(1)
                if n >= 2:
                    probs_v(n - 2)
                if n == 0:
                    gate_part(1)
            pe.wait_ge(pv_sb, NI)

            for b in range(NS):
                pe.wait_ge(kv_in[b % 3], 32 * (b // 3 + 1))
                if b >= 2:
                    pe.wait_ge(sk_sb, b - 1)
                for n in range(AKV):
                    for half in range(2):
                        m = te.transpose(mb[b % 2][:, n * 256 + half * P:n * 256 + half * P + P],
                                         kv_sel[:, b % 3, half, n * HD:n * HD + HD], ident[:, :])
                m.then_inc(sk_ps, 1)
                gate_part(2)
                pe.wait_ge(sk_sb, b + 1)
                for n in range(AKV):
                    m = te.matmul(pj[0][0:64, 0, 0:257], qm[:, (2 * b + n) * 64:(2 * b + n) * 64 + 64], KTs[:, n, :],
                                  start=(b == 0 and n == 0), stop=(b == NS - 1 and n == AKV - 1))
                m.then_inc(sl_ps, 1)
            pe.wait_ge(s_p, 1)
            te.transpose(mb[2][:, 0:64], Ls[:, 0:P], ident[0:64, 0:64])
            te.transpose(mb[2][:, 64:128], Ls[:, P:2 * P], ident[0:64, 0:64])
            te.matmul(mb[2][:, 128:192], Ls[:, 256:257].broadcast_to([64, P]), ident[0:64, 0:64],
                      start=True, stop=True).then_inc(sp_ps, 1)
            pe.wait_ge(sp_sb, 1)
            for b in range(NS):
                m_ = NS + b
                pe.wait_ge(kv_in[m_ % 3], 32 * (m_ // 3 + 1))
                for n in range(AKV):
                    for half in range(2):
                        c = b * AH + n * GRP
                        m = te.matmul(mb[3][:, c:c + GRP], kv_sel[:, m_ % 3, half, n * HD:n * HD + HD],
                                      PTs_s[:, half, c:c + GRP], start=(half == 0), stop=(half == 1))
                m.then_inc(so_ps, 1)
                if b < 6:
                    if b >= 2:
                        pe.wait_ge(cv_sb, b - 1)
                    for u in range(4):
                        m = te.transpose(mb[b % 2][0:11, u * P:u * P + P], win[:, 4 * b + u, :], ident[:, :])
                    m.then_inc(cv_ps, 1)
                gate_part(2)
            pe.wait_ge(so_sb, 1)

            def head_sums(n):
                pe.wait_ge(nq_sq, n + 1)
                if n >= 1:
                    pe.wait_ge(nq_rt, nq_ln(n - 1))
                for half in range(2):
                    m = te.matmul(pj[0][:, half, 0:HALF], ones[:, :], nrm[n % 4][:, half * HALF:half * HALF + HALF],
                                  start=True, stop=True)
                m.then_inc(nq_ps, 1)
            zb_part(8)
            pe.wait_ge(dec_v, 1)
            te.matmul(mb[2][:, 0:32], tri_le[:, :], gv[:, 0, 0:32], start=True, stop=True)
            te.matmul(mb[2][:, 32:64], ones[:, :], gv[:, 0, 0:32], start=True, stop=True).then_inc(dec_ps, 1)
            for n in range(16):
                head_sums(n)
                zb_part(4 if n >= 4 else 2)
            pe.wait_ge(nq_done, 16)
            pe.wait_ge(dec_v, 2)

            for h in range(BH):
                for c in range(TT):
                    m = te.matmul(mb[2][:, c * P:c * P + P], gv[:, 0, c * BH + h:c * BH + h + 1].broadcast_to([P, P]),
                                  tri_le[:, :], start=True, stop=True)
                m.then_inc(g_row, 1)
                for c in range(TT):
                    te.transpose(mb[0][:, c * P:c * P + P], UB[:, U_BK + h, tok(c)], ident[:, :])
                    te.transpose(mb[1][:, c * P:c * P + P], UB[:, U_BV + h, tok(c)], ident[:, :])
                    te.matmul(mb[3][:, c * P:c * P + P], UB[:, U_BK + h, tok(c)], UB[:, U_BK + h, tok(c)],
                              start=True, stop=True)
                    m = te.matmul(pj[0][:, 0, c * P:c * P + P], UB[:, U_BQ + h, tok(c)], UB[:, U_BK + h, tok(c)],
                                  start=True, stop=True)
                m.then_inc(g_pre_ps, 1)
                gate_part(5)
                pe.wait_ge(g_n, h + 1)
                for c in range(TT):
                    m = te.transpose(mb[2][:, c * P:c * P + P], Mb[0][:, c, :], ident[:, :])
                m.then_inc(g_tr, 1)
                gate_part(1)
                pe.wait_ge(g_at, h + 1)
                for c in range(TT):
                    m = te.transpose(pj[0][:, 1, c * P:c * P + P], outn[:, c, :], ident[:, :])
                m.then_inc(g_tr, 1)
                pe.wait_ge(g_nt, 2 * h + 1)
                pe.wait_ge(g_y, 7 * h + 1)
                for s in range(1, 7):
                    M, MT = Mb[2 * ((s - 1) % 2)], Mb[2 * ((s - 1) % 2) + 1]
                    M2 = Mb[2 * (s % 2)]
                    if s > 1:
                        pe.wait_ge(g_mt, 5 * h + s - 1)
                    for c in range(TT):
                        m = te.matmul(mb[0][:, c * P:c * P + P], MT[:, c, :], M[:, c, :], start=True, stop=True)
                    m.then_inc(g_sq, 1)
                    if s < 6:
                        for c in range(TT):
                            m = te.matmul(mb[1][:, c * P:c * P + P], M[:, c, :], MT[:, c, :], start=True, stop=True)
                        m.then_inc(g_sq, 1)
                    gate_part(1)
                    pe.wait_ge(g_m, 6 * h + s)
                    pe.wait_ge(g_y, 7 * h + s)
                    for c in range(TT):
                        m = te.matmul(mb[3][:, c * P:c * P + P], M2[:, c, :], Yt[:, c, :], start=True, stop=True)
                    m.then_inc(g_yps, 1)
                    gate_part(1)
                pe.wait_ge(g_nt, 2 * h + 2)
                pe.wait_ge(g_y, 7 * h + 7)
                for c in range(TT):
                    e = TT * h + c
                    if c:
                        pe.wait_ge(c_s, e)
                        te.matmul(mb[0][:, c * P:c * P + P], UB[:, U_BK + h, tok(c)], Sst, start=True, stop=True).then_inc(c_ks, 1)
                    gate_part(1)
                    pe.wait_ge(c_r, e + 1)
                    te.matmul(mb[1][:, c * P:c * P + P], Yt[:, c, :], rr, start=True, stop=True).then_inc(c_vps, 1)
                    gate_part(1)
                    pe.wait_ge(c_vn, e + 1)
                    if e:
                        pe.wait_ge(c_o, e)
                    te.matmul(mb[2][:, c * P:c * P + P], kd[:, c, :], vnew, start=True, stop=True)
                    m = te.matmul(mb[3][:, c * P:c * P + P], atT[:, c, :], vnew, start=True, stop=True)
                    if c:
                        m = te.matmul(pj[0][:, 0, c * P:c * P + P], UB[:, U_BQ + h, tok(c)], Sst, start=True, stop=True)
                    m.then_inc(c_st, 1)
                    gate_part(1)
                pe.wait_ge(c_o, TT * h + TT)
                for c in range(TT):
                    m = te.transpose(mb[2][:, c * P:c * P + P], outn[:, c, :], ident[:, :])
                m.then_inc(g_oT, 1)
                gate_part(2)
                pe.wait_ge(g_out, h + 1)

            pe.wait_ge(s_bc, 1)
            te.matmul(mb[0][:, 0:64], ones[0:NS, :], gsm[0:NS, 2, :], start=True, stop=True)
            te.matmul(mb[0][:, 64:128], ones[0:NS, :], gsm[0:NS, 3, :], start=True, stop=True)
            te.matmul(mb[0][:, 128:192], ones[:, :], gsm[:, 4, :], start=True, stop=True).then_inc(s_bcs, 1)
            zb_part(8)
            for q in range(16):
                pe.wait_ge(S_in[q % 4], 16 * (q // 4 + 1))
                for r in range(4):
                    e = 4 * q + r
                    m = te.matmul(mb[1][:, 2 * e:2 * e + 2], Sld[q % 4][:, r, :], kqs[:, e, :], start=True, stop=True)
                m.then_inc(s_ks, 1)
                zb_part(1)
            pe.wait_ge(s_vn, 1)
            te.transpose(mb[2][0:64, 0:P], gsm[:, 5, :], ident[:, :])
            te.transpose(mb[2][0:64, P:2 * P], gsm[:, 6, :], ident[:, :]).then_inc(s_tps, 1)
            zb_part(8)
            pe.wait_ge(s_tsb, 2)
            for q in range(16):
                pe.wait_ge(s_vx, q + 1)
                if q >= 2:
                    pe.wait_ge(s_new, q - 1)
                te.matmul(mb[2 + q % 2][:, :], kns, vexp[q % 2].rearrange("p r n -> p (r n)"),
                          start=True, stop=True).then_inc(s_op, 1)
                if 4 <= q < 12:
                    zb_part(4)
            pe.wait_ge(s_new, 16)
            pe.wait_ge(w_lo, G_E + 1)
            pe.wait_ge(proj_evac, G_E)
            pe.wait_ge(gated, 8)
            for n in range(16, 24):
                head_sums(n)
                project_step(1, 0, UA16, n - 16, 0, 8)
            pe.wait_ge(nq_rt, nq_ln(23))
            for k in range(8):
                pe.wait_ge(gated, 9 + k)
                project_step(0, 0, UBq16, k, 8, 8)

            def merge(i, first):
                for j in range(4):
                    before = not (first and j == 0)
                    if before:
                        pe.wait_ge(w_lo, 4 * i + (G_E + j + 1))
                        pe.wait_ge(y_evac, 8 * i + (2 * j - 1))
                        project(1, j % 2, UA16, 0, 8)
                        pe.wait_ge(y_evac, 8 * i + 2 * j)
                        project(0, j % 2, UBq16, 8, 8)
            merge(0, True)
            with pe.Fori(1, 4) as i:
                merge(i, False)

            pe.wait_ge(y_evac, 32)

            def out_T(i, j, first):
                pe.wait_ge(proj_evac, 4 * i + (93 + j))
                if not (first and j < 2):
                    pe.wait_ge(oT_sb, 4 * i + (j - 1))
                for t in range(TT):
                    te.transpose(mb[j % 2][:, t * P:t * P + P], oT[j % 2][:, tok(t)], ident[:, :])
                te.transpose(mb[2 + j % 2][0:NS, 0:P], oT[j % 2][:, NP:T], ident[:, :]).then_inc(oT_ps, 1)

            def out_tiles(i, first):
                for u in range(4):
                    pe.wait_ge(w_lo, 4 * i + (L_F + u + 1))
                    if not (first and u < 2):
                        pe.wait_ge(proj_evac, 4 * i + (92 + u - 1))
                    project(u % 2, u % 2, mT16)
                    if not (first and u == 0):
                        if u:
                            out_T(i, u - 1, first)
                        else:
                            out_T(i - 1, 3, False)
            out_tiles(0, True)
            with pe.Fori(1, 4) as i:
                out_tiles(i, False)
            out_T(3, 3, False)


        @block.scalar
        def _(act):
            sc = nc.scalar
            link = linker(act, act_c)
            act.dma_start(idxg, idx_k_norm[0:1, :].broadcast_to([P, ID])).then_inc(row_in, 16)
            act.dma_start(alog, a_log[0:1, :].broadcast_to([P, BH])).then_inc(row_in, 16)
            act.dma_start(dtb, dt_bias[0:1, :].broadcast_to([P, BH])).then_inc(row_in, 16)
            act.dma_start(pt_i[:, :], page_table.rearrange("(a b) n -> a (b n)", a=1).broadcast_to([P, NS * NPG])).then_inc(row_in, 16)
            act.wait_ge(consts, N_CONST)
            for t in range(5):
                n = TOK[t]
                act.wait_ge(x_in[t], 16)
                if t:
                    act.wait_ge(sq_done, t)
                sc.activation(junk[0:n, :], x_nat[0:n, t, :], ACT.Square, accum_out=ssq[0:n, t:t + 1]).then_inc(sq_done, 1)
            act.wait_ge(mean_sq, 1)
            sc.activation(rs_x, rs_x, ACT.Sqrt).then_inc(rms, 1)

            def hi(slot, arrived, freed, i=None):
                act.wait_ge(w_in_s[slot], arrived)
                if freed is not None:
                    act.wait_ge(proj_done, freed)
                sc.activation(wsp[:, slot, 0, :, :].rearrange("p k n -> p (k n)"), raw[:, slot, :, :].rearrange("p k n -> p (k n)"),
                              ACT.Copy, scale=W_SC).then_inc(w_hi, 1)
            act.wait_ge(wa_in, 32)
            sc.activation(wa16[:, 0, :, :].rearrange("p k n -> p (k n)"), wa.rearrange("p k n -> p (k n)"), ACT.Copy,
                          scale=W_SC).then_inc(x_hi, 1)
            hi(0, 16, None)
            hi(1, 16, None)
            for e in range(20):
                t, q = divmod(e, 4)
                n = TOK[t]
                act.wait_ge(parT_ps, e + 2)
                for u in range(4):
                    m = sc.activation(hT[:, 4 * q + u, 0, tok(t)], mb[q][:, u * P:u * P + n], ACT.Copy,
                                      scale=g_pre[:, 4 * q + u:4 * q + u + 1])
                m.then_inc(x_hi, 1)
            act.wait_ge(mean_sq, 2)
            sc.activation(ki_r, ki_s, ACT.Sqrt).then_inc(rms, 1)
            act.wait_ge(kiT_ps, 1)
            sc.activation(kIT[:, 0:NP], mb[0][:, :], ACT.Copy).then_inc(kiT_sb, 1)
            sc.activation(kIT[:, NP:T], mb[1][:, 0:NS], ACT.Copy).then_inc(kiT_sb, 1)

            def evac(dst, pair, done, func=ACT.Copy):
                act.wait_ge(proj_done, done)
                sc.activation(dst.rearrange("p (h n) -> p h n", h=2), pj[pair][:, :, 0:HALF], func, scale=UNSC).then_inc(proj_evac, 1)

            def gate_out_tile(f, place, before=2):
                x = f - before
                if x >= 0:
                    act.wait_ge(gate_out[x % 2], 16 * (x // 2 + 1))
                done = gate_group(f) + 1
                evac(place, 1, done)
                hi(f % 2, 16 * ((done + 1) // 2 + 1), done)
                act.wait_ge(proj_evac, done)
                act.dma_start(gate_d[1 - f // 16, f % 16], place).then_inc(gate_out[f % 2], 16)

            def zb_out(z):
                done = zb_group(z) + 1
                evac(UA[:, U_QI + z, :], 1, done)
                hi(z % 2, 16 * ((done + 1) // 2 + 1) + (16 if z >= 6 else 0), done)

            def evac_in(U, i, g0, u0):
                for u in range(4):
                    evac(U[:, bass.ds(4 * i + (u0 + u), 1), :].rearrange("p a b -> p (a b)"), u % 2, 4 * i + (g0 + u + 1))
                    hi(u % 2, 32 * i + 16 * ((g0 + u + 2) // 2 + 1), 4 * i + (g0 + u + 1))
            with act.Fori(0, 5) as i:
                evac_in(UA, i, G_B, 0)
            for t in range(5):
                n = TOK[t]
                act.wait_ge(kv_ps, t + 1)
                knat_t = knat[t]
                sc.activation(knat_t[0:n, :], mb[t % 2][0:n, :], ACT.Copy).then_inc(kv_sb, 1)
                act.wait_ge(kv_sb, t + 1)
                if t < TT:
                    link(sc.activation(vn[:, t, :], knat_t[:, 256:512], ACT.Copy))
                    act.dma_start(k_p[0, 0, tok(t)].rearrange("s n d -> s (n d)"), knat_t[:, 0:256]).then_inc(kv_out, 16)
                    act.dma_start(v_p[0, 0, tok(t)].rearrange("s n d -> s (n d)"), knat_t[:, 256:512]).then_inc(kv_out, 16)
                else:
                    act.dma_start(k_s[0].rearrange("b s n d -> (b s) (n d)"), knat_t[0:NS, 0:256]).then_inc(kv_out, 16)
                    act.dma_start(v_s[0].rearrange("b s n d -> (b s) (n d)"), knat_t[0:NS, 256:512]).then_inc(kv_out, 16)
            act.wait_ge(ki_done, 5)
            for t in range(TT):
                act.dma_start(kidx_p[0, 0, tok(t), :], kin[:, t, 0, :]).then_inc(kv_out, 16)
            act.dma_start(kidx_s[0].rearrange("b s d -> (b s) d"), kin[0:NS, TT, 0, :]).then_inc(kv_out, 16)
            for n in range(48):
                L = P * (n // 16 + 2)
                act.wait_ge(idx_ps, n + 1)
                if n >= 4:
                    act.wait_ge(idx_acc, n - 3)
                sc.activation(rel[:, n % 4, 0:L], mb[n % 4][:, 0:L], ACT.Relu).then_inc(idx_relu, 1)
            act.wait_ge(kv_out, 32 * 5 + 16 * 5)
            for b in range(NS):
                if b >= 2:
                    act.wait_ge(ks_ps, b - 1)
                for q in range(4):
                    act.wait_ge(kp_ps, 4 * b + q + 1)
                    sc.activation(kTp[b % 2][:, 4 * q:4 * q + 4, :].rearrange("p a b -> p (a b)"), mb[q][:, :],
                                  ACT.Copy).then_inc(kp_sb, 1)
                if b:
                    gate_out_tile(b - 1, gate_e[(b - 1) % 2])
            gate_out_tile(7, gate_e[1])
            for r in range(2):
                act.wait_ge(gate_out[r], 16 * 4)
            with act.Fori(0, 2) as i:
                evac_in(UB, i, G_C, 0)
            def silu_conv(i, u):
                act.wait_ge(cv_acc, 4 * i + (u - 7))
                act.sem_inc(waited, 1)
                sc.activation(UB[:, bass.ds(4 * i + u, 1), :].rearrange("p a b -> p (a b)"), cvt, ACT.Silu).then_inc(cv_silu, 1)

            def evac_conv(i, first):
                for u in range(4):
                    done = 4 * i + (G_C + u + 1)
                    act.wait_ge(proj_done, done)
                    act.sem_inc(waited, 1)
                    sc.activation(win[:, bass.ds(4 * i + (u - 8), 1), :].rearrange("p a b -> p (a b)"),
                                  pj[u % 2][:, 1, HALF - 11:HALF], ACT.Copy, scale=UNSC)
                    sc.activation(UB[:, bass.ds(4 * i + u, 1), :].rearrange("p a (h n) -> p (a h) n", h=2),
                                  pj[u % 2][:, :, 0:HALF], ACT.Copy, scale=UNSC).then_inc(proj_evac, 1)
                    hi(u % 2, 32 * i + 16 * ((G_C + u + 2) // 2 + 1), done)
                    if not (first and u == 0):
                        if u:
                            silu_conv(i, u - 1)
                        else:
                            silu_conv(i - 1, 3)
            evac_conv(2, True)
            with act.Fori(3, 8) as i:
                evac_conv(i, False)
            silu_conv(7, 3)
            act.wait_ge(cv_silu, 24)
            for b in range(NS):
                act.wait_ge(hot_ps, NPG * (b + 1))
                if b >= 2:
                    act.wait_ge(row_ps, b - 1)
                sc.activation(row3[:, b % 2, :], mb[1][0:3, 0:256] if b % 2 == 0 else mb[2][0:3, 0:256],
                              ACT.Copy).then_inc(row_sb, 1)
                if b % 4 == 3:
                    gate_out_tile(8 + b // 4, gate[0], 1)
            NI = AH * TT
            for n in range(NI + 1):
                if n < NI:
                    L = P * (n % TT + 1)
                    act.wait_ge(lg_max, n + 1)
                    sc.activation(Lb[:, n % 2, 0:L], Lb[:, n % 2, 0:L], ACT.Exp, bias=nm[:, n % 2:n % 2 + 1], scale=A_SCALE,
                                  accum_out=sm[:, n % 2:n % 2 + 1]).then_inc(p_exp, 1)
                if n >= 1:
                    m = n - 1
                    L = P * (m % TT + 1)
                    act.wait_ge(pt_ps, m + 1)
                    if m >= 2:
                        act.wait_ge(pv_ps, m - 1)
                    sc.activation(PTs[:, m % 2, 0:L], mb[2 + m % 2][:, 0:L], ACT.Copy).then_inc(pt_sb, 1)
                if n < NI and n % 8 == 7:
                    gate_out_tile(10 + n // 8, gate[0], 1)
            for b in range(NS):
                act.wait_ge(sk_ps, b + 1)
                if b:
                    act.wait_ge(sl_ps, b)
                link(sc.activation(KTs[:, :, 0:256], mb[b % 2][:, :].rearrange("p (n c) -> p n c", n=2), ACT.Copy))
                sc.activation(KTs[:, :, 256:257], UA[:, U_K:U_K + 2, NP + b:NP + b + 1], ACT.Copy).then_inc(sk_sb, 1)
            act.wait_ge(s_max, 1)
            sc.activation(Ls, Ls, ACT.Exp, bias=cols[0:64, 16:17], scale=A_SCALE, accum_out=cols[0:64, 17:18]).then_inc(s_exp, 1)
            gate_out_tile(14, gate[0], 1)
            act.wait_ge(sp_ps, 1)
            link(sc.activation(tmpS, mb[2][:, 128:192], ACT.Copy))
            sc.activation(PTs_s.rearrange("p h c -> p (h c)"), mb[2][:, 0:128], ACT.Copy).then_inc(sp_sb, 1)
            for q in range(6):
                act.wait_ge(cv_ps, q + 1)
                rows = QS[0:11, 512 * q:512 * q + 512] if q < 4 else idf[0:11, 704 + 512 * (q - 4):704 + 512 * (q - 3)]
                sc.activation(rows, mb[q % 2][0:11, :], ACT.Copy).then_inc(cv_sb, 1)
                act.wait_ge(cv_sb, q + 1)
                act.dma_start(conv_p[0, 0, :, 512 * q:512 * q + 512], rows[0:3, :]).then_inc(cv_out, 16)
                act.dma_start(conv_s[0, :, 2, 512 * q:512 * q + 512], rows[3:11, :]).then_inc(cv_out, 16)
            gate_out_tile(15, gate[0], 1)
            act.wait_ge(so_sb, 1)
            act.wait_ge(cv_out, 16 + 32 * 6)

            def norms(n0, n1):
                for b in range(n0, n1, 4):
                    for n in range(b, b + 4):
                        if n >= 4:
                            act.wait_ge(nq_done, n - 3)
                        sc.activation(nrm[n % 4], UB[:, U_BQ + n % 16, :], ACT.Square).then_inc(nq_sq, 1)
                    if 0 < b < 16:
                        zb_out(b // 4 - 1)
                    for n in range(b, b + 4):
                        act.wait_ge(nq_ps, n + 1)
                        sc.activation(nrm[n % 4].rearrange("p (h n) -> p h n", h=2), pj[0][:, :, 0:HALF], ACT.Ln, bias=eps_c,
                                      scale=1.0 if n < 16 else 1.0 / HD).then_inc(nq_rt, 1)
                    act.wait_ge(nq_rt, nq_ln(b + 3))
                    for n in range(b, b + 4):
                        sc.activation(nrm[n % 4], nrm[n % 4], ACT.Exp, scale=-0.5).then_inc(nq_rt, 1)
            act.wait_ge(dec_a, 1)
            link(sc.activation(gv[:, 1, :], gv[:, 1, :], ACT.Exp, scale=-1.0))
            link(sc.activation(gv[:, 1, :], gv[:, 1, :], ACT.Ln, bias=1.0))
            link(sc.activation(alog, alog, ACT.Exp))
            sc.activation(gv[:, 2, :].rearrange("p (t h) -> p t h", t=5), ab[:, :, 88:96], ACT.Sigmoid).then_inc(dec_e, 1)
            act.wait_ge(dec_a, 2)
            link(sc.activation(gv[:, 4, 0:32], gv[:, 3, 0:32], ACT.Exp))
            link(sc.activation(gv[:, 5, 0:32], gv[:, 5, 0:32], ACT.Exp))
            sc.activation(gv[:, 6, 0:32], gv[:, 6, 0:32], ACT.Exp).then_inc(dec_e, 1)
            norms(0, 16)
            zb_out(3)
            for h in range(BH):
                act.wait_ge(g_nt_in, h + 1)
                sc.activation(Di, Di, ACT.Exp, scale=-1.0).then_inc(g_exp, 1)
                act.wait_ge(g_y, 7 * h + 1)
                sc.activation(Mb[1], mb[2][:, :].rearrange("p (c n) -> p c n", c=4), ACT.Copy).then_inc(g_nt, 1)
                act.wait_ge(g_tr, 2 * h + 2)
                sc.activation(atT, pj[0][:, 1, :].rearrange("p (c n) -> p c n", c=4), ACT.Copy).then_inc(g_nt, 1)
                for s in range(1, 6):
                    act.wait_ge(g_sq, 11 * h + 2 * s)
                    act.wait_ge(g_m, 6 * h + s)
                    sc.activation(Mb[2 * (s % 2) + 1], mb[1][:, :].rearrange("p (c n) -> p c n", c=4),
                                  ACT.Copy).then_inc(g_mt, 1)
                gate_out_tile(16 + 2 * h, gate[0], 2 if h else 1)
                for c in range(TT):
                    act.wait_ge(c_vps, TT * h + c + 1)
                    sc.activation(vnew, mb[1][:, c * P:c * P + P], ACT.Copy).then_inc(c_vn, 1)
                act.wait_ge(g_oT, h + 1)
                sc.activation(UB[:, U_BQ + h, 0:NP], mb[2][:, :], ACT.Copy).then_inc(g_out, 1)
                act.wait_ge(c_s, TT * h + TT)
                act.dma_start(ssm_p[0, 0, h], Sst).then_inc(ssm_out, 16)
                gate_out_tile(16 + 2 * h + 1, gate[1])
            act.wait_ge(ssm_out, 16 * BH)
            def load_S(q, n):
                h, b0 = q // 2, 4 * (q % 2)
                act.dma_start(Sld[n % 4], state_ssm[0, b0:b0 + 4, h].rearrange("b k v -> k b v")).then_inc(S_in[n % 4], 16)
            for q in range(16):
                if q >= 4:
                    act.wait_ge(s_ks, q - 3)
                load_S(q, q)
                if q == 11:
                    zb_out(4)
            act.wait_ge(s_bcs, 1)
            sc.activation(gsm[:, 7, :], mb[0][:, 0:64], ACT.Exp).then_inc(s_kq, 1)
            act.wait_ge(s_tps, 1)
            sc.activation(kns, mb[2][0:64, 0:P], ACT.Copy).then_inc(s_tsb, 1)
            sc.activation(gsm[0:64, 0:2, :].rearrange("p a b -> p (a b)"), mb[2][0:64, P:2 * P], ACT.Copy).then_inc(s_tsb, 1)

            def silu_z(c0):
                for c in range(c0, c0 + 8):
                    z = UB[:, c, :] if c < 8 else UA[:, U_QI + c - 8, :]
                    sc.activation(z, z, ACT.Silu).then_inc(z_silu, 1)
            silu_z(0)
            for q in range(16 + 2):
                if q in (4, 10, 15):
                    zb_out({4: 5, 10: 6, 15: 7}[q])
                if q < 16:
                    if q >= 4:
                        act.wait_ge(S_out[q % 4], 16 * (q // 4))
                    else:
                        act.wait_ge(s_ks, 16)
                    load_S(q, q)
                if q >= 2:
                    m = q - 2
                    h, b0 = m // 2, 4 * (m % 2)
                    act.wait_ge(s_new, m + 1)
                    act.dma_start(ssm_s[0, b0:b0 + 4, h].rearrange("b k v -> k b v"), Sld[m % 4]).then_inc(S_out[m % 4], 16)
            act.wait_ge(proj_evac, G_E)
            silu_z(8)
            for r in range(4):
                act.wait_ge(S_out[r], 16 * 4)
            norms(16, 24)
            act.wait_ge(gated, 16)

            W0 = 16 * (G_E // 2)
            def merge(i, last):
                for j in range(4):
                    act.wait_ge(gate_in[j % 2], 64 * i + 32 * (j // 2 + 1))
                    for g_ in (gate, gate_m):
                        sc.activation(g_[j % 2], g_[j % 2], ACT.Sigmoid).then_inc(gate_sig, 1)
                    hi(j % 2, 64 * i + (W0 + 32 * ((j + 2) // 2 + 1) - (16 if last and j >= 2 else 0)), 8 * i + (G_E + 2 * j + 2))
            with act.Fori(0, 3) as i:
                merge(i, False)
            merge(3, True)
            W_F = W0 + 32 * 8

            def squares(n):
                act.wait_ge(oT_ps, n + 1)
                if n >= 2:
                    act.wait_ge(sq_done, 5 + n - 1)
                for t in range(5):
                    src = mb[n % 2][:, t * P:t * P + P] if t < TT else mb[2 + n % 2][0:NS, 0:P]
                    m = sc.activation(osq[0:TOK[t], 5 * (n % 2) + t, :], src, ACT.Square, accum_out=ssq16[0:TOK[t], t, n:n + 1])
                m.then_inc(sq_done, 1)
            for n in range(16):
                evac(oT[n % 2], n % 2, G_F + n + 1)
                if n < 14:
                    hi(n % 2, W_F + 16 * ((n + 2) // 2 + 1), G_F + n + 1)
                if n:
                    squares(n - 1)
            squares(15)
            act.wait_ge(mean_sq, 3)
            sc.activation(rs_x, rs_x, ACT.Sqrt).then_inc(rms, 1)

        @block.vector
        def _(dve):
            ve = nc.vector
            link = linker(dve, dve_c)
            dve.wait_ge(consts, N_CONST)
            dve.wait_ge(row_in, 64)
            ptv = pt_i[:, :].rearrange("p (c s) -> p c s", s=2)
            ve.tensor_copy(pg_i[0:64, :], ptv[0:64, :, 0])
            link(ve.tensor_copy(pg_i[64:128, :], ptv[64:128, :, 1]))
            ve.tensor_scalar(off_i[:, :], pg_i[:, :], 64.0, pm64, ALU.mult, ALU.add).then_inc(off_done, 1)
            dve.wait_ge(parT_ps, 1)
            link(ve.tensor_copy(parT[:, :], mb[0][:, 0:113]))
            ve.tensor_scalar(g_pre, g_pre, X_SC, None, ALU.mult).then_inc(parT_sb, 1)

            def lo(slot, n):
                dve.wait_ge(w_hi, n)
                ve.scalar_tensor_tensor(out=wsp[:, slot, 1, :, :].rearrange("p k n -> p (k n)"),
                                        in0=raw[:, slot, :, :].rearrange("p k n -> p (k n)"), scalar=W_SC,
                                        in1=wsp[:, slot, 0, :, :].rearrange("p k n -> p (k n)"),
                                        op0=ALU.mult, op1=ALU.subtract).then_inc(w_lo, 1)
            dve.wait_ge(sq_done, 5)
            ve.tensor_scalar(rs_x, ssq, 1.0 / D, EPS, ALU.mult, ALU.add).then_inc(mean_sq, 1)
            dve.wait_ge(rms, 1)
            link(ve.reciprocal(rs_x, rs_x))
            for t in range(5):
                n = TOK[t]
                ve.tensor_scalar(x_nat[0:n, t, :], x_nat[0:n, t, :], rs_x[0:n, t:t + 1], None, ALU.mult).then_inc(x_scaled, 1)
            dve.wait_ge(x_hi, 1)
            ve.scalar_tensor_tensor(out=wa16[:, 1, :, :].rearrange("p k n -> p (k n)"), in0=wa.rearrange("p k n -> p (k n)"),
                                    scalar=W_SC, in1=wa16[:, 0, :, :].rearrange("p k n -> p (k n)"),
                                    op0=ALU.mult, op1=ALU.subtract).then_inc(xT_sb, 1)
            dve.wait_ge(parT_sb, 1)
            for e in range(20):
                t, q = divmod(e, 4)
                n = TOK[t]
                dve.wait_ge(x_hi, e + 2)
                for u in range(4):
                    k = 4 * q + u
                    m = ve.scalar_tensor_tensor(out=hT[:, k, 1, tok(t)], in0=mb[q][:, u * P:u * P + n], scalar=g_pre[:, k:k + 1],
                                                in1=hT[:, k, 0, tok(t)], op0=ALU.mult, op1=ALU.subtract)
                m.then_inc(xT_sb, 1)
                if e in (3, 7):
                    lo(e // 4, e // 4 + 1)
            dve.wait_ge(ab_ps, 1)
            ve.tensor_scalar(ab[:, 0:4, :].rearrange("p a b -> p (a b)"), pj[1][:, 0, 0:384], UNSC, None, ALU.mult)
            link(ve.tensor_scalar(ab[0:NS, 4, :], pj[1][0:NS, 0, 384:480], UNSC, None, ALU.mult))
            jk = junk[:, 0:5 * ID].rearrange("p (t d) -> p t d", t=5)
            link(ve.tensor_tensor(jk, ab[:, :, 0:ID], ab[:, :, 0:ID], ALU.mult))
            link(ve.tensor_reduce(ki_s, jk, AX, ALU.add))
            ve.tensor_scalar(ki_s, ki_s, 1.0 / ID, EPS, ALU.mult, ALU.add).then_inc(mean_sq, 1)
            dve.wait_ge(rms, 2)
            dve.wait_ge(row_in, 64)
            link(ve.reciprocal(ki_r, ki_r))
            for t in range(5):
                ve.tensor_scalar(kin[:, t, 1, :], ab[:, t, 0:ID], ki_r[:, t:t + 1], None, ALU.mult)
            link(ve.tensor_scalar(ab[:, :, 64:80], ab[:, :, 64:80], I_SCALE, None, ALU.mult))
            for t in range(5):
                ve.tensor_tensor(kin[:, t, 0, :], kin[:, t, 1, :], idxg, ALU.mult)
            link(ve.memset(cols[:, 60:62], 0.0))
            for t in range(5):
                ve.tensor_copy(kin[:, t, 1, :], kin[:, t, 0, :]).then_inc(ki_done, 1)
            for b in range(NS):
                m = ve.tensor_scalar(xw[:, b, :].rearrange("p (e m) -> p e m", e=2), ab[0:NS, 4, 64:80].rearrange("p (m e) -> p e m", e=2),
                                     ident[0:NS, b:b + 1], None, ALU.mult)
            m.then_inc(w_x, 1)

            dve.wait_ge(parT_ps, 22)
            for c in range(2):
                ve.tensor_copy(stT[:, 12 * c:12 * c + 12, :].rearrange("p a b -> p (a b)"), mb[2 + c][:, 0:288]).then_inc(parT_sb, 1)
            with dve.Fori(0, 5) as i:
                for u in range(4):
                    lo(u % 2, 4 * i + (u + 3))
            dve.wait_ge(q_swap, 1)
            qs = UA[:, U_QI:U_QI + 8, NP:T].rearrange("p m b -> p b m")
            qw = mb[2][:, 0:64].rearrange("p (m b) -> p b m", b=NS)
            ve.tensor_copy(qblk[0:64, :, 0:8], qs[0:64])
            ve.tensor_copy(qblk[0:64, :, 8:16], qw[0:64])
            ve.tensor_copy(qblk[64:128, :, 16:24], qw[64:128])
            ve.tensor_copy(qblk[64:128, :, 24:32], qs[64:128]).then_inc(qw_done, 1)
            dve.wait_ge(q_swap, 2)
            ve.tensor_copy(wbc[:, :, :].rearrange("p b h -> p (b h)"), mb[3][:, 0:P]).then_inc(qw_done, 1)
            qmd = qm[:, :].rearrange("p (c x) -> p c x", x=68)
            for b in range(NS):
                for n in range(AKV):
                    ve.tensor_copy(qmd[:, 2 * b + n, 0:GRP], UA[:, n * GRP:n * GRP + GRP, NP + b])

            for n in range(48):
                t, hh = n // 16 + 1, n % 16
                L = P * (t + 1)
                dve.wait_ge(idx_relu, n + 1)
                w = ab[:, t, 64 + hh:65 + hh]
                if hh == 0:
                    ve.tensor_scalar(idx[:, t, 0:L], rel[:, n % 4, 0:L], w, None, ALU.mult).then_inc(idx_acc, 1)
                else:
                    dve.wait_ge(idx_acc, n)
                    ve.scalar_tensor_tensor(out=idx[:, t, 0:L], in0=rel[:, n % 4, 0:L], scalar=w, in1=idx[:, t, 0:L],
                                            op0=ALU.mult, op1=ALU.add).then_inc(idx_acc, 1)
            for b in range(NS + 1):
                dve.wait_ge(ks_ps, b + 1)
                if b < NS:
                    link(ve.scalar_tensor_tensor(out=wsum.rearrange("p (c h) -> p c h", h=IH),
                                                 in0=pj[0][:, b % 2, :].rearrange("p (c h) -> p c h", h=IH), scalar=0.0,
                                                 in1=wbc[:, b, :].unsqueeze(1).broadcast_to([P, NPG, IH]),
                                                 op0=ALU.max, op1=ALU.mult))
                    ve.tensor_reduce(Y[:, b, 0:NPG], wsum.rearrange("p (c h) -> p c h", h=IH), AX, ALU.add).then_inc(ks_sum, 1)
                    dve.wait_ge(ks_sum, b + 1)
                    lo(b % 2, G_H + b + 3)
                else:
                    link(ve.scalar_tensor_tensor(out=wsum[:, 0:P].rearrange("p (b h) -> p b h", h=IH),
                                                 in0=pj[1][:, 0, 0:P].rearrange("p (b h) -> p b h", h=IH), scalar=0.0,
                                                 in1=wbc[:, :, :], op0=ALU.max, op1=ALU.mult))
                    ve.tensor_reduce(Y[0:1, :, NPG], wsum[0:1, 0:P].rearrange("p (b h) -> p b h", h=IH), AX, ALU.add).then_inc(ks_sum, 1)
                    dve.wait_ge(ks_sum, NS + 1)

            hi_i = ge[:, 0:P].bitcast(I32)
            lo_i = ge[:, P:2 * P].bitcast(I32)
            ve.tensor_scalar(hi_i, pg_i[:, :], 4, None, ALU.logical_shift_right)
            link(ve.tensor_scalar(lo_i, pg_i[:, :], 15, None, ALU.bitwise_and))
            for par_ in range(2):
                ve.tensor_copy(vals[:, :, par_, 1], hi_i)
                ve.tensor_copy(vals[:, :, par_, 2], lo_i)
                ve.tensor_scalar(t1[:, par_:par_ + 1], pm64, 2.0, float(par_), ALU.mult, ALU.add)
            link(ve.memset(t1[:, 2:2 + P], 0.0))
            for par_ in range(2):
                link(ve.tensor_scalar(vals[:, :, par_, 0], t1[:, 2:2 + P], t1[:, par_:par_ + 1], None, ALU.add))

            Yf = Y[:, :, :]
            ge3 = ge[:, :].rearrange("p (b c) -> p b c", b=NS)
            part, sgn, thr, dif, thm, fac, need, cgt = (srt[:, r, :] for r in range(8))
            link(ve.memset(thr_i[:, :], 0))
            link(ve.tensor_scalar(ge3, Yf, 0.0, None, ALU.is_ge))
            ve.tensor_reduce(part, ge3, AX, ALU.add).then_inc(cnt_part, 1)
            dve.wait_ge(cnt_all, 1)
            link(ve.tensor_scalar(sgn, mb[0][:, 0:NS], SEL_S - 0.5, None, ALU.is_gt))
            link(ve.tensor_scalar(sgn, sgn, 2.0, -1.0, ALU.mult, ALU.add))
            for t in range(1, TT):
                dve.wait_ge(idx_mask, t)
            def convolve(i, u):
                c = 4 * i + (u - 8)
                chan = UB[:, bass.ds(4 * i + u, 1), :].rearrange("p a b -> p (a b)")

                def w_conv(j):
                    return parT[:, bass.ds(4 * i + (16 + 24 * j + u - 8), 1)]
                dve.wait_ge(proj_evac, 4 * i + (G_C + u + 1))
                dve.sem_inc(waited, 1)
                if not (type(c) is int and c == 0):
                    dve.wait_ge(cv_silu, c)
                    dve.sem_inc(waited, 1)
                ve.tensor_scalar(cvt, chan, w_conv(3), None, ALU.mult).then_inc(cv_step, 1)
                for j in range(3):
                    d = 3 - j
                    dve.wait_ge(cv_step, 6 * c + (2 * j + 1))
                    ve.scalar_tensor_tensor(out=cvt[:, d:NP], in0=chan[:, 0:NP - d], scalar=w_conv(j), in1=cvt[:, d:NP],
                                            op0=ALU.mult, op1=ALU.add).then_inc(cv_step, 1)
                    ve.scalar_tensor_tensor(out=cvt[:, NP:T], in0=stT[:, bass.ds(c, 1), j::3].rearrange("p a b -> p (a b)"),
                                            scalar=w_conv(j), in1=cvt[:, NP:T], op0=ALU.mult,
                                            op1=ALU.add).then_inc(cv_step if j < 2 else cv_acc, 1)

            def search(i, conv, first):
                for u in range(4):
                    s = 6 * (4 * i + u)
                    ve.tensor_tensor(cand_i[:, :], thr_i[:, :], bit_i[:, bass.ds(4 * i + u, 1)].broadcast_to([P, NS]),
                                     ALU.bitwise_or).then_inc(srch, 1)
                    dve.wait_ge(srch, s + 1)
                    ve.tensor_tensor(thr, cand_i[:, :].bitcast(F32), sgn, ALU.mult).then_inc(srch, 1)
                    dve.wait_ge(srch, s + 2)
                    ve.tensor_tensor(ge3, Yf, thr.unsqueeze(2).broadcast_to([P, NS, NPG + 1]), ALU.is_ge).then_inc(srch, 1)
                    dve.wait_ge(srch, s + 3)
                    ve.tensor_reduce(part, ge3, AX, ALU.add).then_inc(cnt_part, 1)
                    for x, t in ((0, 3),) if u % 2 == 0 else ((1, 1), (2, 2)):
                        e = 6 * (2 * i + u // 2) + 2 * x
                        L = P * (t + 1)
                        ve.max(top8[:, t, :], idx[:, t, 0:L]).then_inc(topk, 1)
                        dve.wait_ge(topk, e + 1)
                        dve.sem_inc(waited, 1)
                        ve.match_replace(out=idx[:, t, 0:L], in_to_replace=top8[:, t, :], in_values=idx[:, t, 0:L],
                                         imm_value=TAKEN).then_inc(topk, 1)
                        dve.wait_ge(topk, e + 2)
                        dve.sem_inc(waited, 1)
                    if conv and not (first and u == 0):
                        if u:
                            convolve(i, u - 1)
                        else:
                            convolve(i - 1, 3)
                    dve.wait_ge(cnt_all, 4 * i + (u + 2))
                    ve.scalar_tensor_tensor(out=dif, in0=mb[0][:, 0:NS], scalar=SEL_S - 0.5, in1=sgn,
                                            op0=ALU.subtract, op1=ALU.mult).then_inc(srch, 1)
                    dve.wait_ge(srch, s + 4)
                    ve.tensor_scalar(m_i[:, :], dif, 0.0, bit_f[:, bass.ds(4 * i + u, 1)], ALU.is_gt, ALU.mult).then_inc(srch, 1)
                    dve.wait_ge(srch, s + 5)
                    ve.tensor_tensor(thr_i[:, :], thr_i[:, :], m_i[:, :], ALU.bitwise_or).then_inc(srch, 1)
                    dve.wait_ge(srch, s + 6)
                    lo(u % 2, 4 * i + (G_C + u + 3))
            with dve.Fori(0, 2) as i:
                search(i, False, False)
            search(2, True, True)
            with dve.Fori(3, 8) as i:
                search(i, True, False)
            convolve(7, 3)
            link(ve.tensor_scalar(fac, sgn, 0.0, None, ALU.is_lt))
            link(ve.tensor_scalar(dif, fac, 0.7 * 2.0 ** -23, None, ALU.mult))
            link(ve.tensor_tensor(thm, thr_i[:, :].bitcast(F32), dif, ALU.mult))
            link(ve.tensor_tensor(thm, thm, thr_i[:, :].bitcast(F32), ALU.add))
            link(ve.tensor_scalar(fac, fac, 1.2e-38, None, ALU.mult))
            link(ve.tensor_tensor(thm, thm, fac, ALU.max))
            link(ve.tensor_tensor(thr, thm, sgn, ALU.mult))
            thb = thr.unsqueeze(2).broadcast_to([P, NS, NPG + 1])
            gt3 = wsum_gt[:, :].rearrange("p (b c) -> p b c", b=NS)
            link(ve.tensor_tensor(gt3, Yf, thb, ALU.is_gt))
            ve.tensor_reduce(part, gt3, AX, ALU.add).then_inc(rank_in, 1)
            link(ve.tensor_tensor(ge3, Yf, thb, ALU.is_equal))
            pair = t1[:, 0:NS * 17].rearrange("p (b c) -> p b c", b=NS)

            def pair_sums(src):
                s4 = src[:, :, 0:NPG].rearrange("p b (c s) -> p b c s", s=2)
                link(ve.tensor_copy(pair[:, :, 16:17], src[:, :, NPG:NPG + 1]))
                ve.tensor_tensor(pair[:, :, 0:16], s4[:, :, :, 0], s4[:, :, :, 1], ALU.add).then_inc(rank_in, 1)
            incl = rk[:, 0:NS * 17]
            rank = rk[:, 136:136 + 264].rearrange("p (b c) -> p b c", b=NS)
            rs17 = rk2[:, 0:NS * 17]
            link(ve.memset(rs17, 1.0))
            link(ve.memset(rs17.rearrange("p (b c) -> p b c", b=NS)[:, :, 0:1], 0.0))

            def rank_of(src):
                link(ve.tensor_tensor_scan(incl, rs17, mb[3][:, 0:NS * 17], 0.0, ALU.mult, ALU.add))
                link(ve.tensor_tensor(incl, incl, mb[3][:, 0:NS * 17], ALU.subtract))
                link(ve.tensor_tensor(incl, incl, mb[2][:, 0:NS * 17], ALU.add))
                i3 = incl.rearrange("p (b c) -> p b c", b=NS)
                r4 = rank[:, :, 0:NPG].rearrange("p b (c s) -> p b c s", s=2)
                s4 = src[:, :, 0:NPG].rearrange("p b (c s) -> p b c s", s=2)
                link(ve.tensor_copy(r4[:, :, :, 0], i3[:, :, 0:16]))
                link(ve.tensor_tensor(r4[:, :, :, 1], i3[:, :, 0:16], s4[:, :, :, 0], ALU.add))
                link(ve.tensor_copy(rank[:, :, NPG:NPG + 1], i3[:, :, 16:17]))
            pair_sums(ge3)
            dve.wait_ge(rank_ps, 1)
            link(ve.tensor_scalar(need, mb[0][:, 0:NS], -1.0, float(SEL_S), ALU.mult, ALU.add))
            dve.wait_ge(rank_ps, 3)
            rank_of(ge3)
            link(ve.tensor_tensor(rank, rank, need.unsqueeze(2).broadcast_to([P, NS, NPG + 1]), ALU.is_lt))
            link(ve.tensor_tensor(ge3, ge3, rank, ALU.mult))
            link(ve.tensor_tensor(gt3, gt3, ge3, ALU.add))
            pair_sums(gt3)
            dve.wait_ge(rank_ps, 5)
            rank_of(gt3)
            link(ve.tensor_scalar(rank, rank, 1.0, None, ALU.add))
            link(ve.tensor_tensor(rank, rank, gt3, ALU.mult))
            link(ve.tensor_scalar(pos[:, :].rearrange("p (b c) -> p b c", b=NS), rank, -1.0, None, ALU.add))
            ve.tensor_copy(part, gt3[:, :, NPG]).then_inc(rank_in, 1)
            dve.wait_ge(rank_ps, 6)
            link(ve.tensor_copy(cgt, mb[0][:, 8:8 + NS]))
            for e in range(NS * NPG):
                b, c = divmod(e, NPG)
                if e == 160:
                    lo(0, G_A + 3)
                if e >= 4:
                    dve.wait_ge(hot_ps, e - 3)
                ve.tensor_scalar(onehot[:, e % 4, :], iota_b[:, :], pos[:, b * (NPG + 1) + c:b * (NPG + 1) + c + 1], None,
                                 ALU.is_equal).then_inc(hot, 1)
            dve.wait_ge(row_ps, NS)
            ve.tensor_copy(sel_i[:, :], mb[3][:, 0:16]).then_inc(sel_done, 1)
            lo(1, G_A + 4)
            dve.wait_ge(idx_mask, TT)
            for t in range(1, TT):
                L = P * (t + 1)
                m = ve.tensor_scalar(idx[:, t, 0:L], idx[:, t, 0:L], TAKEN, NEG, ALU.not_equal, ALU.mult)
            m.then_inc(masks, 1)
            dve.wait_ge(masks, 1)

            NI = AH * TT
            for n in range(NI + 2):
                if 1 <= n <= NI:
                    m = n - 1
                    L = P * (m % TT + 1)
                    dve.wait_ge(p_exp, m + 1)
                    link(ve.reciprocal(rc[:, m % 2:m % 2 + 1], sm[:, m % 2:m % 2 + 1]))
                    ve.tensor_scalar(Lb[:, m % 2, 0:L], Lb[:, m % 2, 0:L], rc[:, m % 2:m % 2 + 1], None, ALU.mult).then_inc(p_rdy, 1)
                if n < NI:
                    t = n % TT
                    L = P * (t + 1)
                    dve.wait_ge(lg_ps, n + 1)
                    if n >= 2:
                        dve.wait_ge(pt_ps, n - 1)
                    link(ve.tensor_tensor_reduce(Lb[:, n % 2, 0:L], mb[n % 2][:, 0:L], idx[:, t, 0:L], 1.0, NEG, ALU.add,
                                                 ALU.max, mx[:, n % 2:n % 2 + 1]))
                    ve.tensor_scalar(nm[:, n % 2:n % 2 + 1], mx[:, n % 2:n % 2 + 1], -A_SCALE, None, ALU.mult).then_inc(lg_max, 1)
                if n >= 2:
                    m = n - 2
                    dve.wait_ge(pv_ps, m + 1)
                    ve.tensor_copy(UA[:, m // TT, tok(m % TT)], pj[0][:, m % 2, 0:P]).then_inc(pv_sb, 1)
                if n >= 9 and n % 8 == 1:
                    x = n // 8 - 1
                    lo(x % 2, G_A + x + 5)
            dve.wait_ge(sl_ps, NS)
            link(ve.tensor_copy(Ls, pj[0][0:64, 0, 0:257]))
            fl, f2 = cols[0:64, 18:19], cols[0:64, 19:20]
            link(ve.tensor_tensor(cols[0:64, 8:16], cols[0:64, 0:8], cgt[0:64, :], ALU.mult))
            link(ve.tensor_reduce(fl, cols[0:64, 8:16], AX, ALU.add))
            link(ve.tensor_scalar(f2, fl, 1.0, -NEG, ALU.subtract, ALU.mult))
            link(ve.tensor_scalar(fl, fl, NEG, None, ALU.mult))
            link(ve.tensor_tensor(Ls[:, 255:256], Ls[:, 255:256], fl, ALU.add))
            link(ve.tensor_tensor(Ls[:, 256:257], Ls[:, 256:257], f2, ALU.add))
            link(ve.tensor_reduce(cols[0:64, 20:21], Ls, AX, ALU.max))
            ve.tensor_scalar(cols[0:64, 16:17], cols[0:64, 20:21], -A_SCALE, None, ALU.mult).then_inc(s_max, 1)
            dve.wait_ge(s_exp, 1)
            link(ve.reciprocal(cols[0:64, 17:18], cols[0:64, 17:18]))
            ve.tensor_scalar(Ls, Ls, cols[0:64, 17:18], None, ALU.mult).then_inc(s_p, 1)
            lo(0, G_A + 9)
            dve.wait_ge(sp_sb, 1)
            tS = tmpS.rearrange("p (b h) -> p b h", b=NS)
            for n in range(AKV):
                ve.tensor_tensor(tS[:, :, n * GRP:n * GRP + GRP], tS[:, :, n * GRP:n * GRP + GRP],
                                 UA[:, U_V + n, NP:T].unsqueeze(2).broadcast_to([P, NS, GRP]), ALU.mult)
            link(ve.memset(cols[:, 60:62], 0.0))
            dve.wait_ge(so_ps, NS)
            ve.tensor_tensor(UA[:, 0:8, NP:T].rearrange("p h b -> p b h"), mb[3][:, 0:64].rearrange("p (b h) -> p b h", b=NS),
                             tS, ALU.add).then_inc(so_sb, 1)
            lo(1, G_A + 10)

            def norm_mul(n):
                dve.wait_ge(nq_rt, nq_ln(n) + 4)
                dst = UB[:, U_BQ + n, :] if n < 16 else UB[:, U_BQ + n - 16, :]
                sc_ = A_SCALE if n < 8 else (1.0 if n < 16 else gdn_g)
                ve.scalar_tensor_tensor(out=dst, in0=dst, scalar=sc_, in1=nrm[n % 4], op0=ALU.mult, op1=ALU.mult).then_inc(nq_done, 1)
            g3 = gv[:, 3, :].rearrange("p (t h) -> p t h", t=5)
            link(ve.tensor_tensor(g3, ab[:, :, 80:88], dtb.unsqueeze(1).broadcast_to([P, 5, BH]), ALU.add))
            link(ve.tensor_scalar(gv[:, 0, :], gv[:, 3, :], -1.0, None, ALU.mult))
            ve.tensor_tensor(gv[:, 1, :], gv[:, 3, :], gv[:, 0, :], ALU.max).then_inc(dec_a, 1)
            dve.wait_ge(dec_e, 1)
            link(ve.tensor_scalar(gv[:, 3, :], gv[:, 3, :], 0.0, None, ALU.max))
            link(ve.tensor_tensor(gv[:, 3, :], gv[:, 3, :], gv[:, 1, :], ALU.add))
            ve.scalar_tensor_tensor(out=gv[:, 0, :].rearrange("p (t h) -> p t h", t=5), in0=g3, scalar=-1.0,
                                    in1=alog.unsqueeze(1).broadcast_to([P, 5, BH]), op0=ALU.mult, op1=ALU.mult).then_inc(dec_v, 1)
            dve.wait_ge(dec_ps, 1)
            cum, beta, ecum, etot, kdec, nbe, nbeta = gv[:, 3, :], gv[:, 2, :], gv[:, 4, :], gv[:, 5, :], gv[:, 6, :], gv[:, 7, :], gv[:, 1, :]
            link(ve.tensor_copy(cum[:, 0:32], mb[2][:, 0:32]))
            link(ve.tensor_copy(etot[:, 0:32], mb[2][:, 32:64]))
            ve.tensor_tensor(kdec[:, 0:32], etot[:, 0:32], cum[:, 0:32], ALU.subtract).then_inc(dec_a, 1)
            dve.wait_ge(dec_e, 2)
            link(ve.tensor_scalar(nbeta, beta, -1.0, None, ALU.mult))
            ve.tensor_tensor(nbe[:, 0:32], nbeta[:, 0:32], ecum[:, 0:32], ALU.mult).then_inc(dec_v, 1)
            dve.wait_ge(dec_v, 2)

            for n in range(16):
                if n in (4, 8, 12):
                    lo((n // 4 - 1) % 2, G_D + n // 4 + 2)
                norm_mul(n)
            lo(1, G_D + 6)

            def hc(v, h):
                return v[:, h:32:BH].unsqueeze(2).broadcast_to([P, TT, P])
            c4 = "p (c n) -> p c n"
            for h in range(BH):
                dve.wait_ge(g_row, h + 1)
                link(ve.tensor_tensor(Di, mb[2][:, :].rearrange(c4, c=4), hc(cum, h), ALU.subtract))
                ve.tensor_scalar(Di, Di, 0.0, None, ALU.max).then_inc(g_nt_in, 1)
                if h:
                    lo(1, G_G + 2 * h + 2)
                dve.wait_ge(g_pre_ps, h + 1)
                ve.tensor_tensor(kd, mb[0][:, :].rearrange(c4, c=4), hc(kdec, h), ALU.mult)
                ve.tensor_tensor(vb, mb[1][:, :].rearrange(c4, c=4), hc(beta, h), ALU.mult)
                dve.wait_ge(g_msk, 2 * h + 1)
                for c in range(TT):
                    e = c * BH + h
                    m = ve.scalar_tensor_tensor(out=Mb[0][:, c, :], in0=mb[3][:, c * P:c * P + P], scalar=nbeta[:, e:e + 1],
                                                in1=Ds[:, c, :], op0=ALU.mult, op1=ALU.mult)
                m.then_inc(g_n, 1)
                dve.wait_ge(g_msk, 2 * h + 2)
                ve.tensor_tensor(outn, pj[0][:, 0, :].rearrange(c4, c=4), Di, ALU.mult).then_inc(g_at, 1)
                dve.wait_ge(g_tr, 2 * h + 1)
                ve.tensor_tensor(Yt, mb[2][:, :].rearrange(c4, c=4), ident[:, :].unsqueeze(1).broadcast_to([P, TT, P]),
                                 ALU.add).then_inc(g_y, 1)
                for s in range(1, 7):
                    dve.wait_ge(g_sq, 11 * h + 2 * s - 1)
                    ve.tensor_copy(Mb[2 * (s % 2)], mb[0][:, :].rearrange(c4, c=4)).then_inc(g_m, 1)
                    dve.wait_ge(g_yps, 6 * h + s)
                    dve.wait_ge(g_y, 7 * h + s)
                    ve.tensor_tensor(Yt, Yt, mb[3][:, :].rearrange(c4, c=4), ALU.add).then_inc(g_y, 1)
                for c in range(TT):
                    e = c * BH + h
                    n = TT * h + c
                    if c == 0:
                        ve.tensor_copy(rr, vb[:, 0, :]).then_inc(c_r, 1)
                    else:
                        dve.wait_ge(c_ks, 3 * h + c)
                        ve.scalar_tensor_tensor(out=rr, in0=mb[0][:, c * P:c * P + P], scalar=nbe[:, e:e + 1], in1=vb[:, c, :],
                                                op0=ALU.mult, op1=ALU.add).then_inc(c_r, 1)
                    if c == 2:
                        lo(0, G_G + 2 * h + 3)
                    dve.wait_ge(c_st, n + 1)
                    if c == 0:
                        if h:
                            dve.wait_ge(ssm_out, 16 * h)
                        ve.tensor_copy(Sst, mb[2][:, 0:P]).then_inc(c_s, 1)
                        ve.tensor_copy(outn[:, 0, :], mb[3][:, 0:P]).then_inc(c_o, 1)
                    else:
                        ve.scalar_tensor_tensor(out=Sst, in0=Sst, scalar=etot[:, e:e + 1], in1=mb[2][:, c * P:c * P + P],
                                                op0=ALU.mult, op1=ALU.add).then_inc(c_s, 1)
                        link(ve.tensor_copy(outn[:, c, :], mb[3][:, c * P:c * P + P]))
                        ve.scalar_tensor_tensor(out=outn[:, c, :], in0=pj[0][:, 0, c * P:c * P + P], scalar=ecum[:, e:e + 1],
                                                in1=outn[:, c, :], op0=ALU.mult, op1=ALU.add).then_inc(c_o, 1)
                    dve.wait_ge(c_s, n + 1)

            dve.wait_ge(g_out, BH)
            lo(1, G_G + 2 * BH + 2)
            id8 = ident[0:NS, 0:NS].unsqueeze(1).broadcast_to([NS, BH, NS])
            for src, slot in ((0, 2), (2, 3)):
                ve.tensor_tensor(gsm[0:NS, slot, :].rearrange("p (h b) -> p h b", h=BH),
                                 gv[0:NS, src, 32:40].unsqueeze(2).broadcast_to([NS, BH, NS]), id8, ALU.mult)
            kS = UB[:, U_BK:U_BK + 8, NP:T]
            qS = UB[:, U_BQ:U_BQ + 8, NP:T]
            vS = UB[:, U_BV:U_BV + 8, NP:T]
            h8 = "p (h b) -> p h b"
            ve.tensor_tensor(gsm[:, 4, :].rearrange(h8, h=BH), kS, qS, ALU.mult)
            link(ve.tensor_copy(gsm[:, 5, :].rearrange(h8, h=BH), kS))
            ve.tensor_copy(kqs[:, :, 0].rearrange(h8, h=BH), kS)
            ve.tensor_copy(kqs[:, :, 1].rearrange(h8, h=BH), qS).then_inc(s_bc, 1)
            dve.wait_ge(s_kq, 1)
            eg, bt, qk, vv = gsm[:, 7, :], gsm[:, 2, :], gsm[:, 3, :], gsm[:, 6, :]
            ve.tensor_copy(bt, mb[0][:, 64:128])
            link(ve.tensor_copy(qk, mb[0][:, 128:192]))
            lo(0, G_Z + 3)
            dve.wait_ge(s_ks, 16)
            kq_ps = mb[1][:, 0:P].rearrange("p (e t) -> p e t", t=2)
            link(ve.tensor_tensor(vv, kq_ps[:, :, 0], eg, ALU.mult))
            link(ve.tensor_tensor(vv.rearrange(h8, h=BH), vS, vv.rearrange(h8, h=BH), ALU.subtract))
            link(ve.tensor_tensor(vv, vv, bt, ALU.mult))
            link(ve.tensor_tensor(qk, qk, vv, ALU.mult))
            link(ve.tensor_tensor(bt, kq_ps[:, :, 1], eg, ALU.mult))
            ve.tensor_tensor(qS, bt.rearrange(h8, h=BH), qk.rearrange(h8, h=BH), ALU.add).then_inc(s_vn, 1)

            def gate_z(c):
                dve.wait_ge(z_silu, c + 1)
                dst = UA[:, c, :] if c < 8 else UB[:, U_BQ + c - 8, :]
                z = UB[:, c, :] if c < 8 else UA[:, U_QI + c - 8, :]
                d16 = UA16[:, c] if c < 8 else UBq16[:, c - 8]
                link(ve.tensor_tensor(gtmp, dst, z, ALU.mult))
                link(ve.tensor_scalar(d16[:, 0, :], gtmp, X_SC, None, ALU.mult))
                ve.scalar_tensor_tensor(out=d16[:, 1, :], in0=gtmp, scalar=X_SC, in1=d16[:, 0, :],
                                        op0=ALU.mult, op1=ALU.subtract).then_inc(gated, 1)
                dve.wait_ge(gated, c + 1)
            for q in range(16):
                if q % 2:
                    gate_z(q // 2)
                if q == 3:
                    lo(1, G_Z + 4)
                if q == 12:
                    lo(0, G_Z + 5)
                dve.wait_ge(s_op, q + 1)
                dve.wait_ge(S_in[q % 4], 16 * (q // 4 + 5))
                for r in range(4):
                    e = 4 * q + r
                    m = ve.scalar_tensor_tensor(out=Sld[q % 4][:, r, :], in0=Sld[q % 4][:, r, :], scalar=eg[:, e:e + 1],
                                                in1=mb[2 + q % 2][:, r * P:r * P + P], op0=ALU.mult, op1=ALU.add)
                m.then_inc(s_new, 1)
            lo(1, G_Z + 6)
            for b in (16, 20):
                for n in range(b, b + 4):
                    norm_mul(n)
                for n in range(b, b + 4):
                    dve.wait_ge(nq_done, n + 1)
                    gate_z(n - 8)
            h2 = "p (h n) -> p h n"

            def merge(i):
                for j in range(4):
                    dve.wait_ge(proj_done, 8 * i + (G_E + 2 * j + 1))
                    dve.wait_ge(gate_sig, 8 * i + (2 * j + 1))
                    ve.tensor_tensor(m1.rearrange(h2, h=2), pj[1][:, :, 0:HALF], gate[j % 2].rearrange(h2, h=2), ALU.mult).then_inc(y_evac, 1)
                    dve.wait_ge(proj_done, 8 * i + (G_E + 2 * j + 2))
                    dve.wait_ge(gate_sig, 8 * i + (2 * j + 2))
                    ve.tensor_tensor(m2b.rearrange(h2, h=2), pj[0][:, :, 0:HALF], gate_m[j % 2].rearrange(h2, h=2), ALU.mult).then_inc(mrg, 1)
                    dve.wait_ge(y_evac, 8 * i + (2 * j + 1))
                    dve.wait_ge(mrg, 12 * i + (3 * j + 1))
                    ve.tensor_tensor(m1, m1, m2b, ALU.add).then_inc(mrg, 1)
                    dve.wait_ge(mrg, 12 * i + (3 * j + 2))
                    d16 = mT16[:, bass.ds(4 * i + j, 1), :, :]
                    ve.tensor_scalar(d16[:, :, 0, :].rearrange("p a b -> p (a b)"), m1, UNSC * X_SC, None, ALU.mult).then_inc(mrg, 1)
                    dve.wait_ge(mrg, 12 * i + (3 * j + 3))
                    ve.scalar_tensor_tensor(out=d16[:, :, 1, :].rearrange("p a b -> p (a b)"), in0=m1, scalar=UNSC * X_SC,
                                            in1=d16[:, :, 0, :].rearrange("p a b -> p (a b)"),
                                            op0=ALU.mult, op1=ALU.subtract).then_inc(y_evac, 1)
                    dve.wait_ge(y_evac, 8 * i + (2 * j + 2))
                    lo(j % 2, 4 * i + (G_E + j + 3))
            with dve.Fori(0, 4) as i:
                merge(i)

            dve.wait_ge(post_in, 16)
            for n in range(16):
                if n < 14:
                    lo(n % 2, L_F + n + 3)
                dve.wait_ge(sq_done, 5 + n + 1)
                col = P * n
                pn = postb[:, col:col + P]
                ve.tensor_tensor(Yo[:, 0:4, col:col + P], mb[n % 2][:, :].rearrange("p (t n) -> p t n", t=4),
                                 pn.unsqueeze(1).broadcast_to([P, 4, P]), ALU.mult)
                ve.tensor_tensor(Yo[0:NS, 4, col:col + P], mb[2 + n % 2][0:NS, 0:P], pn[0:NS, :], ALU.mult).then_inc(oT_sb, 1)
            ve.tensor_reduce(ssq[:, 0:TT], ssq16[:, 0:TT, :], AX, ALU.add)
            link(ve.tensor_reduce(ssq[0:NS, TT:TT + 1], ssq16[0:NS, TT, :], AX, ALU.add))
            ve.tensor_scalar(rs_x, ssq, 1.0 / D, EPS, ALU.mult, ALU.add).then_inc(mean_sq, 1)
            dve.wait_ge(rms, 3)
            dve.wait_ge(x_back, 80)
            link(ve.reciprocal(rs_x, rs_x))
            for t in range(5):
                n = TOK[t]
                ve.scalar_tensor_tensor(out=Yo[0:n, t, :], in0=Yo[0:n, t, :], scalar=rs_x[0:n, t:t + 1],
                                        in1=xf[0:n, t, :] if t < TT else xfs[0:NS, :], op0=ALU.mult, op1=ALU.add).then_inc(y_fin, 1)


_INS = ["x_prompt", "x_sample", "cache_k", "cache_v", "cache_kidx", "state_conv", "state_ssm", "page_table", "pre_norm",
        "post_norm", "w_in", "idx_k_norm", "conv_w", "a_log", "dt_bias", "gdn_norm", "w_pa", "w_pb", "w_o"]
_OUTS = [(1, NP, D), (NS, 1, D), (1, 1, NP, AKV, HD), (1, 1, NP, AKV, HD), (1, 1, NP, ID), (1, 1, CONV - 1, CD),
         (1, 1, BH, HD, HD), (1, NS, 1, AKV, HD), (1, NS, 1, AKV, HD), (1, NS, 1, ID), (1, NS, CONV - 1, CD),
         (1, NS, BH, HD, HD)]


def kernel(**inputs):
    import numpy as _np
    import concourse.bacc as _bacc
    from concourse import mybir as _mybir
    from concourse.bass_utils import run_bass_kernel_spmd as _run

    nc = _bacc.Bacc("TRN2", target_bir_lowering=False, num_devices=1)
    arrays, args = {}, []
    for name in _INS:
        a = _np.ascontiguousarray(inputs[name])
        arrays[f"in_{name}_dram"] = a
        args.append(nc.dram_tensor(f"in_{name}_dram", a.shape, _mybir.dt.from_np(a.dtype), kind="ExternalInput").ap())
    for i, shape in enumerate(_OUTS):
        args.append(nc.dram_tensor(f"out_{i}_dram", shape, _mybir.dt.float32, kind="ExternalOutput").ap())
    build(nc, *args)
    r = _run(nc, [arrays], core_ids=[0])
    return tuple(r.results[0][f"out_{i}_dram"] for i in range(len(_OUTS)))
```
